# Optimizing a Trainium2 kernel written in Bass

```python
import math
import jax
import jax.numpy as jnp
from jax import lax
import numpy as np

D_MODEL = 1024
BATCH = 1
SEQ = 1024
DEPTH = 2

GRID_W = 64
CTX_LEN = 256
EPS = 1e-6

GDN_HEADS = 6
GDN_DK = 64
GDN_DV = 64
GDN_CHUNK = 64

MLA_HEADS = 6
MLA_Q_RANK = 256
MLA_KV_RANK = 128
MLA_NOPE = 64
MLA_ROPE = 32
MLA_V = 64
MLA_QK = MLA_NOPE + MLA_ROPE
ATTN_BLOCK = 128
ROPE_BASE = 10000.0
ROPE_AXIS = MLA_ROPE // 2

HY_CH = 256
HY_BANDS = 16
HY_EMB = 1 + 2 * HY_BANDS
HY_HIDDEN = 64
HY_TARGET = 1e-2
HY_FAST_DECAY_PCT = 0.3
HY_SLOW_DECAY_PCT = 1.5
HY_MAX_DECAY = math.log(HY_TARGET) / HY_FAST_DECAY_PCT
HY_MIN_DECAY = math.log(HY_TARGET) / HY_SLOW_DECAY_PCT

D_FF = 2816

GDN_WIDTH = GDN_HEADS * GDN_DV
MLA_WIDTH = MLA_HEADS * MLA_V
HY_WIDTH = HY_CH
MIX_WIDTH = GDN_WIDTH + MLA_WIDTH + HY_WIDTH

GDN_QKV = GDN_HEADS * (2 * GDN_DK + GDN_DV)
GDN_IN = GDN_QKV + GDN_WIDTH + 4 * GDN_HEADS
MLA_IN = MLA_Q_RANK + MLA_KV_RANK + MLA_ROPE
HY_IN = 3 * HY_CH
P_IN = GDN_IN + MLA_IN + HY_IN

kernel_name = 'hybrid_gdn_mla_hyena_prefix_dit'

def rms_norm(x, g):
    xf = x.astype(jnp.float32)
    y = xf * lax.rsqrt(jnp.mean(xf * xf, axis=-1, keepdims=True) + EPS)
    return (y * g.astype(jnp.float32)).astype(x.dtype)

def modulate(h, shift, scale):
    return h * (1.0 + scale) + shift

def dwconv3(x, w, b=None):
    xp = jnp.pad(x, ((0, 0), (1, 1), (0, 0)))
    y = xp[:, :-2] * w[0] + xp[:, 1:-1] * w[1] + xp[:, 2:] * w[2]
    return y if b is None else y + b

def axial_rope(l):
    rows = l // GRID_W
    row = jnp.repeat(jnp.arange(rows, dtype=jnp.float32), GRID_W)
    col = jnp.tile(jnp.arange(GRID_W, dtype=jnp.float32), rows)
    inv = ROPE_BASE ** (-jnp.arange(0, ROPE_AXIS, 2, dtype=jnp.float32) / ROPE_AXIS)
    ang = jnp.concatenate([row[:, None] * inv, col[:, None] * inv], axis=-1)
    return jnp.cos(ang), jnp.sin(ang)

def apply_rope(x, cos, sin):
    half = x.shape[-1] // 2
    x1, x2 = x[..., :half], x[..., half:]
    cos, sin = cos[None, :, None, :], sin[None, :, None, :]
    return jnp.concatenate([x1 * cos - x2 * sin, x1 * sin + x2 * cos], axis=-1)

def gdn_chunked(q, k, v, g, beta, s0):
    b, l, h, dk = q.shape
    dv = v.shape[-1]
    n = l // GDN_CHUNK

    def blocks(t):
        t = t.reshape((b, n, GDN_CHUNK, h) + t.shape[3:])
        return jnp.moveaxis(t, 3, 1)

    q, k, v, g, beta = (blocks(t) for t in (q, k, v, g, beta))
    gc = jnp.cumsum(g, axis=-1)
    idx = jnp.arange(GDN_CHUNK)
    incl = idx[:, None] >= idx[None, :]
    strict = idx[:, None] > idx[None, :]
    diff = gc[..., :, None] - gc[..., None, :]
    dec_incl = jnp.where(incl, jnp.exp(jnp.where(incl, diff, 0.0)), 0.0)
    dec_strict = jnp.where(strict, dec_incl, 0.0)
    a_mat = beta[..., :, None] * jnp.einsum('bhnik,bhnjk->bhnij', k, k) * dec_strict
    eg = jnp.exp(gc)[..., None]
    rhs = beta[..., None] * jnp.concatenate([v, k * eg], axis=-1)
    sol = lax.linalg.triangular_solve(a_mat, rhs, left_side=True, lower=True, unit_diagonal=True)
    u, w = sol[..., :dv], sol[..., dv:]
    qk = jnp.einsum('bhnik,bhnjk->bhnij', q, k) * dec_incl
    q_dec = q * eg
    k_dec = k * jnp.exp(gc[..., -1:] - gc)[..., None]
    c_dec = jnp.exp(gc[..., -1])
    xs = tuple(jnp.moveaxis(t, 2, 0) for t in (u, w, q_dec, qk, k_dec, c_dec))

    def step(s, inp):
        u_c, w_c, q_c, qk_c, k_c, d_c = inp
        delta = u_c - jnp.einsum('bhck,bhkv->bhcv', w_c, s)
        o_c = jnp.einsum('bhck,bhkv->bhcv', q_c, s) + jnp.einsum('bhij,bhjv->bhiv', qk_c, delta)
        s = d_c[..., None, None] * s + jnp.einsum('bhck,bhcv->bhkv', k_c, delta)
        return s, o_c

    s_fin, o = lax.scan(step, s0, xs)
    o = jnp.moveaxis(o, 0, 2).reshape(b, h, l, dv)
    return jnp.moveaxis(o, 1, 2), s_fin

def gdn_prep(p, conv_w, a_log, dt_bias):
    b, l, _ = p.shape
    p = p.astype(jnp.float32)
    qkv = jax.nn.silu(dwconv3(p[..., :GDN_QKV], conv_w.astype(jnp.float32)))
    hk = GDN_HEADS * GDN_DK
    q = qkv[..., :hk].reshape(b, l, GDN_HEADS, GDN_DK)
    k = qkv[..., hk:2 * hk].reshape(b, l, GDN_HEADS, GDN_DK)
    v = qkv[..., 2 * hk:].reshape(b, l, GDN_HEADS, GDN_DV)
    q = q * lax.rsqrt(jnp.sum(q * q, axis=-1, keepdims=True) + EPS) * (GDN_DK ** -0.5)
    k = k * lax.rsqrt(jnp.sum(k * k, axis=-1, keepdims=True) + EPS)
    z = p[..., GDN_QKV:GDN_QKV + GDN_WIDTH].reshape(b, l, GDN_HEADS, GDN_DV)
    ab = p[..., GDN_QKV + GDN_WIDTH:].reshape(b, l, 2, 2, GDN_HEADS)
    g = -jnp.exp(a_log.astype(jnp.float32)) * jax.nn.softplus(ab[:, :, 0] + dt_bias.astype(jnp.float32))
    beta = jax.nn.sigmoid(ab[:, :, 1])
    return q, k, v, z, g, beta

def gdn_mixer(p_ctx, p_lat, conv_w, a_log, dt_bias, norm_g):
    qc, kc, vc, zc, gc, bc = gdn_prep(p_ctx, conv_w, a_log, dt_bias)
    ql, kl, vl, zl, gl, bl = gdn_prep(p_lat, conv_w, a_log, dt_bias)
    s0 = jnp.zeros((ql.shape[0], GDN_HEADS, GDN_DK, GDN_DV), jnp.float32)
    same = lambda t: t
    rev = lambda t: t[:, ::-1]
    outs_c, outs_l = [], []
    for d, fl in ((0, same), (1, rev)):
        oc, s_ctx = gdn_chunked(fl(qc), fl(kc), fl(vc), fl(gc[:, :, d]), fl(bc[:, :, d]), s0)
        ol, _ = gdn_chunked(fl(ql), fl(kl), fl(vl), fl(gl[:, :, d]), fl(bl[:, :, d]), s_ctx)
        outs_c.append(fl(oc))
        outs_l.append(fl(ol))

    def gated_out(o, z):
        y = rms_norm(o, norm_g) * jax.nn.silu(z)
        return y.reshape(o.shape[0], o.shape[1], GDN_WIDTH)

    return gated_out(outs_c[0] + outs_c[1], zc), gated_out(outs_l[0] + outs_l[1], zl)

def mla_heads(p, q_norm_g, w_uq, kv_norm_g, w_ukv, q_head_g, k_head_g, rope):
    b, l, _ = p.shape
    c_q = rms_norm(p[..., :MLA_Q_RANK], q_norm_g)
    c_kv = rms_norm(p[..., MLA_Q_RANK:MLA_Q_RANK + MLA_KV_RANK], kv_norm_g)
    k_rope = p[..., MLA_Q_RANK + MLA_KV_RANK:]
    q = (c_q @ w_uq).reshape(b, l, MLA_HEADS, MLA_QK)
    kv = (c_kv @ w_ukv).reshape(b, l, MLA_HEADS, MLA_NOPE + MLA_V)
    k = jnp.concatenate([kv[..., :MLA_NOPE],
                         jnp.broadcast_to(k_rope[:, :, None, :], (b, l, MLA_HEADS, MLA_ROPE))], axis=-1)
    v = kv[..., MLA_NOPE:]
    q = rms_norm(q, q_head_g)
    k = rms_norm(k, k_head_g)
    if rope is not None:
        cos, sin = rope
        q = jnp.concatenate([q[..., :MLA_NOPE], apply_rope(q[..., MLA_NOPE:], cos, sin)], axis=-1)
        k = jnp.concatenate([k[..., :MLA_NOPE], apply_rope(k[..., MLA_NOPE:], cos, sin)], axis=-1)
    return q, k, v

def softmax_attend(q, k, v, scale):
    s = jnp.einsum('bqhd,bkhd->bhqk', q, k).astype(jnp.float32) * scale
    p = jax.nn.softmax(s, axis=-1).astype(v.dtype)
    return jnp.einsum('bhqk,bkhd->bqhd', p, v)

def mla_mixer(p_ctx, p_lat, q_norm_g, w_uq, kv_norm_g, w_ukv, q_head_g, k_head_g, rope, with_ctx):
    qc, kc, vc = mla_heads(p_ctx, q_norm_g, w_uq, kv_norm_g, w_ukv, q_head_g, k_head_g, None)
    ql, kl, vl = mla_heads(p_lat, q_norm_g, w_uq, kv_norm_g, w_ukv, q_head_g, k_head_g, rope)
    scale = MLA_QK ** -0.5
    k_all = jnp.concatenate([kl, kc], axis=1)
    v_all = jnp.concatenate([vl, vc], axis=1)
    b, l = ql.shape[0], ql.shape[1]
    nb = l // ATTN_BLOCK
    q_blocks = jnp.moveaxis(ql.reshape(b, nb, ATTN_BLOCK, MLA_HEADS, MLA_QK), 1, 0)
    o_lat = lax.map(lambda qb: softmax_attend(qb, k_all, v_all, scale), q_blocks)
    o_lat = jnp.moveaxis(o_lat, 0, 1).reshape(b, l, MLA_WIDTH)
    if not with_ctx:
        return None, o_lat
    o_ctx = softmax_attend(qc, kc, vc, scale).reshape(b, qc.shape[1], MLA_WIDTH)
    return o_ctx, o_lat

def hyena_filter(l, w1, b1, w2, b2, w3, b3):
    t = jnp.arange(l, dtype=jnp.float32)
    t_norm = t / max(l - 1, 1)
    bands = jnp.linspace(1e-4, HY_BANDS - 1, HY_BANDS, dtype=jnp.float32)
    ang = 2.0 * math.pi * t[:, None] * bands[None, :] / l
    z = jnp.concatenate([t_norm[:, None], jnp.cos(ang), jnp.sin(ang)], axis=-1)
    h = jnp.sin(z @ w1 + b1)
    h = jnp.sin(h @ w2 + b2)
    h = (h @ w3 + b3).reshape(l, 2, HY_CH).astype(jnp.float32)
    deltas = jnp.abs(jnp.linspace(HY_MIN_DECAY, HY_MAX_DECAY, HY_CH, dtype=jnp.float32))
    h = h * jnp.exp(-t_norm[:, None, None] * deltas)
    buf = jnp.concatenate([h[:, 0], jnp.zeros((1, HY_CH), jnp.float32), h[:0:-1, 1]], axis=0)
    return buf / jnp.sum(jnp.abs(buf), axis=0, keepdims=True)

def hyena_mixer(p, conv_w, conv_b, w1, b1, w2, b2, w3, b3, d_skip):
    b, l, _ = p.shape
    u = dwconv3(p, conv_w, conv_b)
    x0, x1, v = u[..., :HY_CH], u[..., HY_CH:2 * HY_CH], u[..., 2 * HY_CH:]
    z = (v * x1).astype(jnp.float32)
    buf = hyena_filter(l, w1, b1, w2, b2, w3, b3)
    zf = jnp.fft.rfft(z, n=2 * l, axis=1)
    hf = jnp.fft.rfft(buf, n=2 * l, axis=0)
    y = jnp.fft.irfft(zf * hf[None], n=2 * l, axis=1)[:, :l] + z * d_skip
    return x0 * y.astype(x0.dtype)

def conv_ffn(h, w_up, conv_w, conv_b, w_down):
    up = h @ w_up
    gate = dwconv3(up[..., :D_FF], conv_w, conv_b)
    return (jax.nn.silu(gate) * up[..., D_FF:]) @ w_down

def setup_inputs(seed: int = 0) -> dict:
    key = jax.random.key(seed)
    ks = jax.random.split(key, 33)

    def nrm(i, shape, scale):
        return jax.random.normal(ks[i], shape, jnp.float32) * scale

    def gain(i, n):
        return 1.0 + nrm(i, (DEPTH, n), 0.05)

    a_val = jax.random.uniform(ks[9], (DEPTH, 2, GDN_HEADS), jnp.float32, 1.0, 16.0)
    dt = jnp.exp(jax.random.uniform(ks[10], (DEPTH, 2, GDN_HEADS), jnp.float32,
                                    math.log(1e-3), math.log(1e-1)))
    return {
        'x': nrm(0, (BATCH, SEQ, D_MODEL), 1.0),
        'c': nrm(1, (BATCH, D_MODEL), 1.0),
        'ctx': nrm(2, (BATCH, CTX_LEN, D_MODEL), 1.0),
        'c_ctx': nrm(3, (D_MODEL,), 1.0),
        'ada_w': nrm(4, (DEPTH, D_MODEL, 6 * D_MODEL), 0.5 * D_MODEL ** -0.5),
        'ada_b': nrm(5, (DEPTH, 6 * D_MODEL), 0.02),
        'mix_norm_g': gain(6, D_MODEL),
        'w_in': nrm(7, (DEPTH, D_MODEL, P_IN), D_MODEL ** -0.5),
        'gdn_conv_w': nrm(8, (DEPTH, 3, GDN_QKV), 3 ** -0.5),
        'gdn_a_log': jnp.log(a_val),
        'gdn_dt_bias': dt + jnp.log(-jnp.expm1(-dt)),
        'gdn_norm_g': gain(11, GDN_DV),
        'mla_q_norm_g': gain(12, MLA_Q_RANK),
        'mla_w_uq': nrm(13, (DEPTH, MLA_Q_RANK, MLA_HEADS * MLA_QK), MLA_Q_RANK ** -0.5),
        'mla_kv_norm_g': gain(14, MLA_KV_RANK),
        'mla_w_ukv': nrm(15, (DEPTH, MLA_KV_RANK, MLA_HEADS * (MLA_NOPE + MLA_V)), MLA_KV_RANK ** -0.5),
        'mla_q_head_g': gain(16, MLA_QK),
        'mla_k_head_g': gain(17, MLA_QK),
        'hy_conv_w': nrm(18, (DEPTH, 3, HY_IN), 3 ** -0.5),
        'hy_conv_b': nrm(19, (DEPTH, HY_IN), 0.02),
        'hy_w1': nrm(20, (DEPTH, HY_EMB, HY_HIDDEN), HY_EMB ** -0.5),
        'hy_b1': nrm(21, (DEPTH, HY_HIDDEN), 0.02),
        'hy_w2': nrm(22, (DEPTH, HY_HIDDEN, HY_HIDDEN), HY_HIDDEN ** -0.5),
        'hy_b2': nrm(23, (DEPTH, HY_HIDDEN), 0.02),
        'hy_w3': nrm(24, (DEPTH, HY_HIDDEN, 2 * HY_CH), HY_HIDDEN ** -0.5),
        'hy_b3': nrm(25, (DEPTH, 2 * HY_CH), 0.02),
        'hy_d': nrm(26, (DEPTH, HY_CH), 1.0),
        'w_out': nrm(27, (DEPTH, MIX_WIDTH, D_MODEL), MIX_WIDTH ** -0.5),
        'ffn_norm_g': gain(28, D_MODEL),
        'ffn_w_up': nrm(29, (DEPTH, D_MODEL, 2 * D_FF), D_MODEL ** -0.5),
        'ffn_conv_w': nrm(30, (DEPTH, 3, D_FF), 3 ** -0.5),
        'ffn_conv_b': nrm(31, (DEPTH, D_FF), 0.02),
        'ffn_w_down': nrm(32, (DEPTH, D_FF, D_MODEL), D_FF ** -0.5),
    }

def reference(x, c, ctx, c_ctx, ada_w, ada_b, mix_norm_g, w_in, gdn_conv_w, gdn_a_log, gdn_dt_bias,
              gdn_norm_g, mla_q_norm_g, mla_w_uq, mla_kv_norm_g, mla_w_ukv, mla_q_head_g, mla_k_head_g,
              hy_conv_w, hy_conv_b, hy_w1, hy_b1, hy_w2, hy_b2, hy_w3, hy_b3, hy_d, w_out,
              ffn_norm_g, ffn_w_up, ffn_conv_w, ffn_conv_b, ffn_w_down):
    rope = axial_rope(x.shape[1])
    s1, s2 = GDN_IN, GDN_IN + MLA_IN
    for i in range(DEPTH):
        last = i == DEPTH - 1
        mod_lat = (jax.nn.silu(c) @ ada_w[i] + ada_b[i])[:, None, :]
        mod_ctx = (jax.nn.silu(c_ctx) @ ada_w[i] + ada_b[i])[None, None, :]
        sa_l, ca_l, ga_l, sf_l, cf_l, gf_l = jnp.split(mod_lat, 6, axis=-1)
        sa_c, ca_c, ga_c, sf_c, cf_c, gf_c = jnp.split(mod_ctx, 6, axis=-1)

        p_lat = modulate(rms_norm(x, mix_norm_g[i]), sa_l, ca_l) @ w_in[i]
        p_ctx = modulate(rms_norm(ctx, mix_norm_g[i]), sa_c, ca_c) @ w_in[i]

        gdn_c, gdn_l = gdn_mixer(p_ctx[..., :s1], p_lat[..., :s1], gdn_conv_w[i], gdn_a_log[i],
                                 gdn_dt_bias[i], gdn_norm_g[i])
        mla_c, mla_l = mla_mixer(p_ctx[..., s1:s2], p_lat[..., s1:s2], mla_q_norm_g[i], mla_w_uq[i],
                                 mla_kv_norm_g[i], mla_w_ukv[i], mla_q_head_g[i], mla_k_head_g[i],
                                 rope, not last)
        hy_l = hyena_mixer(p_lat[..., s2:], hy_conv_w[i], hy_conv_b[i], hy_w1[i], hy_b1[i],
                           hy_w2[i], hy_b2[i], hy_w3[i], hy_b3[i], hy_d[i])
        mix_l = jnp.concatenate([gdn_l, mla_l, hy_l], axis=-1).astype(x.dtype)
        x = x + ga_l * (mix_l @ w_out[i])
        h_l = modulate(rms_norm(x, ffn_norm_g[i]), sf_l, cf_l)
        x = x + gf_l * conv_ffn(h_l, ffn_w_up[i], ffn_conv_w[i], ffn_conv_b[i], ffn_w_down[i])

        if not last:
            hy_c = hyena_mixer(p_ctx[..., s2:], hy_conv_w[i], hy_conv_b[i], hy_w1[i], hy_b1[i],
                               hy_w2[i], hy_b2[i], hy_w3[i], hy_b3[i], hy_d[i])
            mix_c = jnp.concatenate([gdn_c, mla_c, hy_c], axis=-1).astype(ctx.dtype)
            ctx = ctx + ga_c * (mix_c @ w_out[i])
            h_c = modulate(rms_norm(ctx, ffn_norm_g[i]), sf_c, cf_c)
            ctx = ctx + gf_c * conv_ffn(h_c, ffn_w_up[i], ffn_conv_w[i], ffn_conv_b[i], ffn_w_down[i])
    return x


_drawn_inputs = setup_inputs


def setup_inputs(seed=0):
    import zlib

    import numpy as np

    out = dict(_drawn_inputs(seed))
    spreads = {}
    factors = {'ctx': 4.021,
     'c_ctx': 3.476,
     'gdn_norm_g': 6.008,
     'mla_q_norm_g': 8.0,
     'mla_kv_norm_g': 8.0,
     'mla_q_head_g': 8.0,
     'mla_k_head_g': 8.0,
     'hy_conv_b': 7.764,
     'hy_w1': 3.581,
     'hy_b1': 8.0,
     'hy_w2': 3.507,
     'hy_b2': 26.647,
     'hy_w3': 3.538,
     'hy_b3': 42.869,
     'ffn_conv_b': 8.0}
    for name, (base, spread) in spreads.items():
        noise = np.random.default_rng([zlib.crc32(name.encode()), seed]).standard_normal(out[name].shape)
        drawn = base * np.exp(spread * noise) if base else spread * noise
        out[name] = jnp.asarray(drawn.astype(out[name].dtype))
    for name, factor in factors.items():
        out[name] = (out[name] * factor).astype(out[name].dtype)
    return out
```

```python
from contextlib import ExitStack

import numpy as np

import concourse.bass as bass
from concourse import mybir

F32 = mybir.dt.float32
ACT = mybir.ActivationFunctionType
ALU = mybir.AluOpType
AX = mybir.AxisListType

P = 128
D = 1024
DK = D // P
SEQ, CTX = 1024, 256
T = SEQ + CTX
DEPTH = 2
EPS = 1e-6
GRID_W = 64

HEADS = 6
PAIRS = 3
CH = 64
GDN_QKV = 1152
GDN_W = 384
N_CHUNK = T // CH
LAT_CHUNKS, CTX_CHUNKS = SEQ // CH, CTX // CH

QR, KVR, NOPE, ROPE, VD = 256, 128, 64, 32, 64
QK = NOPE + ROPE
HY = 256
HY_EMB, HY_HID = 33, 64
D_FF = 2816
FT = D_FF // P
GDN_IN = GDN_QKV + GDN_W + 4 * HEADS
MLA_COL = GDN_IN
HY_COL = GDN_IN + QR + KVR + ROPE
P_IN = HY_COL + 3 * HY

LEVELS = 6
NEG = -1e30
TWO_PI = 2 * np.pi
RAW = T + 4
RAW_AT = ((0, SEQ, 0), (SEQ, CTX, SEQ + 2))
GROUP = 1536
BANK = 512

K_ID = 0
K_BLOCK = K_ID + P
K_ONES = K_BLOCK + P
K_CUM = K_ONES + P
K_LEVEL = K_CUM + 2 * CH
K_NEG = K_LEVEL + LEVELS * 2 * CH
K_ROT = K_NEG + 2 * CH
K_ID64 = K_ROT + QK
K_T0 = K_ID64 + CH
K_TN = K_T0 + 1
K_DELTA = K_TN + SEQ // P + CTX // P
K_EPS = K_DELTA + HY
K_N = K_EPS + 1

VEC_A = (("ada_b", 48), ("mix_norm_g", 8), ("ffn_norm_g", 8), ("gdn_conv_w", 27), ("hy_conv_w", 18),
         ("hy_conv_b", 6), ("hy_d", 2), ("mla_q_norm_g", 2), ("mla_kv_norm_g", 1))
VEC_B = (("ffn_conv_w", 66), ("ffn_conv_b", 22), ("c", 8), ("c_ctx", 8))
VCOL, _at = {}, 0
for _n, _k in VEC_A + VEC_B:
    VCOL[_n] = _at
    _at += _k
N_VEC = _at
N_ROWS = len(VEC_A) + len(VEC_B) + 6 + 4
N_VEC_A = sum(k for _, k in VEC_A)
N_VEC_B = sum(k for _, k in VEC_B)
SMALL = N_VEC + 96 + 2 * 2 * 8 + 12 + 8


def tables():
    k = np.zeros((P, K_N), np.float32)
    k[:, K_ID:K_ID + P] = np.eye(P)
    for h in range(2):
        k[h * 64:h * 64 + 64, K_BLOCK + h * 64:K_BLOCK + h * 64 + 64] = 1
    k[:, K_ONES:K_ONES + P] = 1
    j, i = np.meshgrid(np.arange(CH), np.arange(CH), indexing="ij")
    for d in range(2):
        before = (i >= j) if d == 0 else (i <= j)
        k[:, K_CUM + d * CH:K_CUM + d * CH + CH] = np.tile(before, (2, 1))
        k[:, K_NEG + d * CH:K_NEG + d * CH + CH] = np.tile(np.where(before, 0, NEG), (2, 1))
        for l in range(LEVELS):
            b = 1 << l
            same = (i // (2 * b)) == (j // (2 * b))
            first, second = (j, i) if d == 0 else (i, j)
            m = same & ((first // b) % 2 == 0) & ((second // b) % 2 == 1)
            c = K_LEVEL + (l * 2 + d) * CH
            k[:, c:c + CH] = np.tile(m, (2, 1))
    half = ROPE // 2
    for r in range(half):
        k[NOPE + half + r, K_ROT + NOPE + r] = -1
        k[NOPE + r, K_ROT + NOPE + half + r] = 1
    k[:, K_ID64:K_ID64 + CH] = np.tile(np.eye(CH), (2, 1))
    k[:, K_T0] = 1
    k[0, K_T0] = 0
    lo, hi = np.log(1e-2) / 1.5, np.log(1e-2) / 0.3
    k[:, K_DELTA:K_DELTA + HY] = np.abs(np.linspace(lo, hi, HY, dtype=np.float32))
    k[:, K_EPS] = EPS
    out = {"k_table": k}
    at = 0
    for name, length in (("lat", SEQ), ("ctx", CTX)):
        t = np.arange(length, dtype=np.float32)
        tn = t / np.float32(max(length - 1, 1))
        k[:, K_TN + at:K_TN + at + length // P] = -tn.reshape(-1, P).T
        at += length // P
        bands = np.linspace(1e-4, 15, 16, dtype=np.float32)
        ang = (np.float32(2.0 * np.pi) * t[:, None] * bands[None, :] / np.float32(length)).astype(np.float32)
        z = np.concatenate([tn[:, None], np.cos(ang), np.sin(ang)], axis=-1)
        out["k_z_" + name] = np.ascontiguousarray(z.T.astype(np.float32))
        th = np.pi * np.outer(np.arange(length), 2 * np.arange(length) + 1) / (2 * length)
        cs = np.stack([np.cos(th), np.sin(th)])
        out["k_dft_" + name] = cs.astype(np.float32)
        out["k_idft_" + name] = np.ascontiguousarray((cs / length).transpose(0, 2, 1).astype(np.float32))
    rows = SEQ // GRID_W
    row = np.repeat(np.arange(rows, dtype=np.float32), GRID_W)
    col = np.tile(np.arange(GRID_W, dtype=np.float32), rows)
    inv = (np.float32(10000.0) ** (-np.arange(0, 16, 2, dtype=np.float32) / 16)).astype(np.float32)
    ang = np.concatenate([row[:, None] * inv, col[:, None] * inv], axis=-1).T
    rope = np.zeros((2, QK, SEQ), np.float32)
    rope[0, :NOPE] = 1
    rope[0, NOPE:] = np.tile(np.cos(ang), (2, 1))
    rope[1, NOPE:] = np.tile(np.sin(ang), (2, 1))
    out["k_rope"] = rope
    return out


class Signal:

    def __init__(self, sem):
        self.sem, self.total = sem, 0


class Ref:

    def __init__(self, signal, n, unit):
        self.sem, self.base, self.unit = signal.sem, signal.total, unit
        signal.total += n * unit
        self.end = signal.total

    def at(self, k):
        return k * self.unit + self.base


def build(nc, a, out):
    with ExitStack() as ctx:
        def sb(name, n):
            return ctx.enter_context(nc.sbuf_tensor(name, [P, n], F32))

        X = sb("X", DK * T)
        H = sb("H", DK * T)
        C = sb("C", FT * T)
        W = sb("W", 2 * DK * P)
        K = sb("K", K_N)
        S = sb("S", SMALL)
        ps = ctx.enter_context(nc.psum_tensor("ps", [P, 8 * BANK], F32))
        x_dram = nc.dram_tensor("x_stream", [P, DK * T], F32, kind="Internal").ap()

        signals = {}
        every = []

        def signal(name):
            if name not in signals:
                signals[name] = Signal(ctx.enter_context(nc.semaphore(name)))
            return signals[name]

        class Phase:

            def __init__(self):
                self.ends = []
                self.parts = {}
                every.append(self)

            def sig(self, name, n, unit=1):
                r = Ref(signal(name), n, unit)
                self.ends.append((r.sem, r.end))
                return r

        tile_done = signal("tile_done")
        w_loaded = [signal("w_loaded_0"), signal("w_loaded_1")]
        tiles = [0]

        x3 = X[:, :].rearrange("p (k t) -> p k t", k=DK)
        h3 = H[:, :].rearrange("p (k t) -> p k t", k=DK)
        w3 = W[:, :].rearrange("p (s k n) -> p s k n", s=2, k=DK)
        ident = K[:, K_ID:K_ID + P]
        eps = K[:, K_EPS:K_EPS + 1]
        mod = S[:, N_VEC:N_VEC + 96].rearrange("p (m v) -> p m v", v=2)
        gain = S[:, N_VEC + 96:N_VEC + 128].rearrange("p (w k v) -> p w k v", w=2, v=2)
        AL = S[:, N_VEC + 128:N_VEC + 134]
        DT = S[:, N_VEC + 134:N_VEC + 140]
        gdn_g = S[:, N_VEC + 140:N_VEC + 141]
        q_g = S[0:QK, N_VEC + 141:N_VEC + 142]
        k_g = S[0:QK, N_VEC + 142:N_VEC + 143]
        b1 = S[0:HY_HID, N_VEC + 143:N_VEC + 144]
        b2 = S[0:HY_HID, N_VEC + 144:N_VEC + 145]
        inv_norm = S[:, N_VEC + 145:N_VEC + 147]

        def vec(name, j=0):
            c = VCOL[name] + j
            return S[:, c:c + 1]

        def region(t, at, n):
            return t[:, at:at + n]

        class Chain:

            def __init__(self, name):
                self.s = signal(name)
                self.base, self.c, self.i, self.per = 0, 0, None, 0

            def link(self, eng, ins):
                self.c += 1
                ins.then_inc(self.s.sem, 1)
                v = self.base + self.c if self.i is None else self.i * self.per + (self.base + self.c)
                eng.wait_ge(self.s.sem, v)

            def loop(self, i, per):
                self.base, self.c = self.base + self.c, 0
                self.i, self.per = i, per

            def end(self, times):
                assert self.c == self.per, (self.c, self.per)
                self.base, self.c, self.i = self.base + self.per * times, 0, None

        chain = {e: Chain(e + "_own") for e in ("dve", "act", "pool")}

        def tok(last):
            return [(0, BANK), (BANK, BANK)] + ([] if last else [(SEQ, CTX)])

        def group(g, n, lo=0, hi=P):
            return ps[lo:hi, g * GROUP:g * GROUP + n]

        def tile(base, i=0, u=0, per=2):
            b = base + u
            return b % 2, i * per + b, i * (per // 2) + b // 2

        def load_tile(sp, num, src, col, k, width):
            slot, n, _ = num
            c = col if isinstance(col, int) else sp.snap(col)
            if not isinstance(n, int) or n >= 2:
                sp.wait_ge(tile_done.sem, n - 1)
            sp.dma_start(w3[:, slot, 0:k, 0:width], src[:, :, bass.ds(c, width)]).then_inc(w_loaded[slot].sem, 16)

        def product(pe, num, k, width, rhs, last, free=None, lo=0):
            g, n, loads = num
            pe.wait_ge(w_loaded[g].sem, loads * 16 + 16)
            if free is not None:
                pe.wait_ge(free[0].sem, free[0].at(free[1]))
            for b, (t0, tn) in enumerate(tok(last)):
                for kk in range(k):
                    ins = pe.matmul(ps[lo:lo + width, g * GROUP + b * BANK:g * GROUP + b * BANK + tn],
                                    w3[:, g, kk, 0:width], rhs(kk, t0, tn), start=(kk == 0), stop=(kk == k - 1))
            ins.then_inc(tile_done.sem, 1)

        def h_rhs(kk, t0, tn):
            return h3[:, kk, t0:t0 + tn]

        def keep_raw(act, g, raw, width, ready):
            for t0, tn, r0 in RAW_AT:
                if t0 < width:
                    ins = act.activation(raw[:, r0 + 1:r0 + 1 + tn], ps[:, g * GROUP + t0:g * GROUP + t0 + tn], ACT.Copy)
            ins.then_inc(ready.sem, 1)

        def conv(dve, raw, w, bias, dst, width, done):
            for step in range(3):
                for t0, tn, r0 in RAW_AT:
                    if t0 >= width:
                        continue
                    src = raw[:, r0 + step:r0 + step + tn]
                    o = dst[:, t0:t0 + tn]
                    if step == 0 and bias is None:
                        ins = dve.tensor_scalar(o, src, w[0], None, ALU.mult)
                    elif step == 0:
                        ins = dve.tensor_scalar(o, src, w[0], bias, ALU.mult, ALU.add)
                    else:
                        ins = dve.scalar_tensor_tensor(o, src, w[step], o, ALU.mult, ALU.add)
                if step < 2:
                    chain["dve"].link(dve, ins)
            ins.then_inc(done.sem, 1)

        def settle(eng, k):
            if k:
                for sem, end in every[k - 1].ends:
                    eng.wait_ge(sem, end)

        def phase_input():
            ph = Phase()
            table = ph.sig("table_loaded", 1, 16)
            rows = ph.sig("rows_loaded", 10, 16)
            turned = ph.sig("rows_turned", 20)
            kept = ph.sig("rows_kept", 20)
            ring = [region(C, s * D, D) for s in range(10)]

            def sp(e):
                e.dma_start(K[:, :], a["k_table"]).then_inc(table.sem, 16)
                for n in range(10):
                    src = a["x"][0, n * P:n * P + P, :] if n < 8 else a["ctx"][0, (n - 8) * P:(n - 7) * P, :]
                    if n:
                        e.wait_ge(rows.sem, rows.at(n))
                    e.dma_start(ring[n], src).then_inc(rows.sem, 16)

            def pe(e):
                e.wait_ge(table.sem, table.at(1))
                for n in range(10):
                    e.wait_ge(rows.sem, rows.at(n + 1))
                    for half in range(2):
                        c = 2 * n + half
                        if c >= 4:
                            e.wait_ge(kept.sem, kept.at(c - 3))
                        for q in range(4):
                            k = half * 4 + q
                            ins = e.transpose(ps[:, (c % 4) * BANK + q * P:(c % 4) * BANK + q * P + P],
                                              ring[n][:, k * P:k * P + P], ident)
                        ins.then_inc(turned.sem, 1)

            def act(e):
                for n in range(10):
                    for half in range(2):
                        c = 2 * n + half
                        e.wait_ge(turned.sem, turned.at(c + 1))
                        e.activation(x3[:, half * 4:half * 4 + 4, n * P:n * P + P],
                                     ps[:, (c % 4) * BANK:(c % 4 + 1) * BANK].rearrange("p (k t) -> p k t", k=4),
                                     ACT.Copy).then_inc(kept.sem, 1)
            ph.parts = dict(sp=sp, pe=pe, act=act)

        def phase_modulation(l):
            ph = Phase()
            NC = 12
            rows = ph.sig("vectors_loaded", N_ROWS, 16)
            turned = ph.sig("vectors_turned", 1)
            kept = ph.sig("vectors_kept", 2)
            silu = ph.sig("c_silu", 1)
            loaded = [ph.sig("ada_loaded_0", NC // 2, 16), ph.sig("ada_loaded_1", NC // 2, 16)]
            used = ph.sig("ada_used", NC)
            moved = ph.sig("mod_made", 3)
            rows_a = region(C, 0, P)
            rows_b = region(C, P, P)
            cT = S[:, VCOL["c"]:VCOL["c"] + 16].rearrange("p (v k) -> p k v", v=2)
            cS = region(C, 2 * P + 16, 16).rearrange("p (k v) -> p k v", v=2)
            ring = [region(C, 1024 + s * 4096, 4096).rearrange("p (k n) -> p k n", k=DK) for s in range(2)]

            def pool(e):
                at = 0
                for dst, names in ((rows_a, VEC_A), (rows_b, VEC_B)):
                    at = 0
                    for name, k in names:
                        src = a[name] if name == "c_ctx" else a[name][0 if name == "c" else l]
                        src = src.rearrange("w (k p) -> (w k) p", p=P) if len(src.shape) == 2 \
                            else src.rearrange("(k p) -> k p", p=P)
                        e.dma_start(dst[at:at + k, :], src).then_inc(rows.sem, 16)
                        at += k
                for h in range(2):
                    r = slice(h * 64, h * 64 + 64)
                    for dst, name in ((AL, "gdn_a_log"), (DT, "gdn_dt_bias")):
                        src = a[name][l].rearrange("d (p h) -> h d p", h=2)[h:h + 1]
                        e.dma_start(dst[r, :].rearrange("q (d p) -> q d p", d=2),
                                    src.broadcast_to([64, 2, PAIRS]), allow_slow_non_contiguous=True)\
                            .then_inc(rows.sem, 16)
                    e.dma_start(gdn_g[r, :], a["gdn_norm_g"][l].rearrange("(p o) -> p o", o=1)).then_inc(rows.sem, 16)
                for dst, name in ((q_g, "mla_q_head_g"), (k_g, "mla_k_head_g")):
                    e.dma_start(dst, a[name][l].rearrange("(p o) -> p o", o=1)).then_inc(rows.sem, 16)
                for dst, name in ((b1, "hy_b1"), (b2, "hy_b2")):
                    e.dma_start(dst, a[name][l].rearrange("(p o) -> p o", o=1)).then_inc(rows.sem, 16)

            def sp(e):
                w = a["ada_w"][l].rearrange("(k p) n -> p k n", p=P)
                for n in range(NC):
                    if n >= 2:
                        e.wait_ge(used.sem, used.at(n - 1))
                    e.dma_start(ring[n % 2], w[:, :, n * 512:n * 512 + 512]).then_inc(loaded[n % 2].sem, 16)

            def pe(e):
                e.wait_ge(rows.sem, rows.at(N_ROWS))
                e.transpose(ps[:, 0:N_VEC_A], rows_a[0:N_VEC_A, :], ident[0:N_VEC_A, 0:N_VEC_A])
                e.transpose(ps[:, P:P + N_VEC_B], rows_b[0:N_VEC_B, :], ident[0:N_VEC_B, 0:N_VEC_B])\
                    .then_inc(turned.sem, 1)
                e.wait_ge(silu.sem, silu.at(1))
                for n in range(NC):
                    e.wait_ge(loaded[n % 2].sem, loaded[n % 2].at(n // 2 + 1))
                    for q in range(4):
                        c = 4 * n + q
                        for k in range(DK):
                            ins = e.matmul(ps[:, BANK + 2 * c:BANK + 2 * c + 2], ring[n % 2][:, k, q * P:q * P + P],
                                           cS[:, k, :], start=(k == 0), stop=(k == DK - 1))
                    ins.then_inc(used.sem, 1)

            def act(e):
                e.wait_ge(kept.sem, kept.at(2))
                e.activation(cS, cT, ACT.Silu).then_inc(silu.sem, 1)

            def dve(e):
                e.wait_ge(turned.sem, turned.at(1))
                e.tensor_copy(S[:, 0:N_VEC_A], ps[:, 0:N_VEC_A]).then_inc(kept.sem, 1)
                e.tensor_copy(S[:, N_VEC_A:N_VEC], ps[:, P:P + N_VEC_B]).then_inc(kept.sem, 1)
                e.wait_ge(kept.sem, kept.at(2))
                e.wait_ge(used.sem, used.at(NC))
                e.tensor_tensor(mod, ps[:, BANK:BANK + 96].rearrange("p (m v) -> p m v", v=2),
                                S[:, 0:48].unsqueeze(2).broadcast_to([P, 48, 2]), ALU.add).then_inc(moved.sem, 1)
                e.wait_ge(moved.sem, moved.at(1))
                for w, (name, sc) in enumerate((("mix_norm_g", 8), ("ffn_norm_g", 32))):
                    g = S[:, VCOL[name]:VCOL[name] + 8]
                    e.scalar_tensor_tensor(gain[:, w], mod[:, sc:sc + 8, :], 1.0,
                                           g.unsqueeze(2).broadcast_to([P, 8, 2]), ALU.add, ALU.mult)\
                        .then_inc(moved.sem, 1)
            ph.parts = dict(sp=sp, pe=pe, act=act, dve=dve, pool=pool)

        def phase_norm(l, which, last):
            ph = Phase()
            width = SEQ if last else T
            squared = ph.sig("squared", DK)
            summed = ph.sig("squares_summed", DK)
            root = ph.sig("root_made", 1)
            inv = ph.sig("rstd_made", 1)
            scaled = ph.sig("h_scaled", DK)
            made = ph.sig("h_made", DK * (1 if last else 2))
            saved = ph.sig("x_saved", 1, 16)
            sq = [region(C, 0, T), region(C, T, T)]
            rt, rs = region(C, 2 * T, T), region(C, 3 * T, T)
            segs = [(0, SEQ, 0)] + ([] if last else [(SEQ, CTX, 1)])
            shift = 0 if which == 0 else 24

            def pool(e):
                e.dma_start(x_dram, X[:, :]).then_inc(saved.sem, 16)

            def act(e):
                for k in range(DK):
                    if k >= 2:
                        e.wait_ge(summed.sem, summed.at(k - 1))
                    e.activation(sq[k % 2][:, 0:width], x3[:, k, 0:width], ACT.Square).then_inc(squared.sem, 1)
                e.wait_ge(summed.sem, summed.at(DK))
                e.activation(rt[:, 0:width], group(0, width), ACT.Sqrt, bias=eps, scale=1.0 / D).then_inc(root.sem, 1)
                for k in range(DK):
                    e.wait_ge(scaled.sem, scaled.at(k + 1))
                    for t0, tn, v in segs:
                        e.activation(h3[:, k, t0:t0 + tn], h3[:, k, t0:t0 + tn], ACT.Identity,
                                     bias=mod[:, shift + k, v:v + 1]).then_inc(made.sem, 1)

            def pe(e):
                for k in range(DK):
                    e.wait_ge(squared.sem, squared.at(k + 1))
                    for b, (t0, tn) in enumerate(tok(last)):
                        ins = e.matmul(ps[:, b * BANK:b * BANK + tn], K[:, K_ONES:K_ONES + P], sq[k % 2][:, t0:t0 + tn],
                                       start=(k == 0), stop=(k == DK - 1))
                    ins.then_inc(summed.sem, 1)

            def dve(e):
                e.wait_ge(root.sem, root.at(1))
                e.reciprocal(rs[:, 0:width], rt[:, 0:width]).then_inc(inv.sem, 1)
                e.wait_ge(inv.sem, inv.at(1))
                for k in range(DK):
                    for t0, tn, v in segs:
                        ins = e.scalar_tensor_tensor(h3[:, k, t0:t0 + tn], x3[:, k, t0:t0 + tn],
                                                     gain[:, which, k, v:v + 1], rs[:, t0:t0 + tn], ALU.mult, ALU.mult)
                    ins.then_inc(scaled.sem, 1)
            ph.parts = dict(pe=pe, act=act, dve=dve, pool=pool)

        HY_OUT = region(C, 0, 2 * T)
        MLA_OUT = region(C, 2 * T, 3 * T)
        FREE = 5 * T
        hy3 = HY_OUT.rearrange("p (c t) -> p c t", c=2)
        mla3 = MLA_OUT.rearrange("p (c t) -> p c t", c=3)

        def raws():
            return [region(X, s * RAW, RAW) for s in range(2)]

        def zero_pads(e, sigref):
            for s in range(2):
                for c in (0, SEQ + 1, SEQ + 2, RAW - 1):
                    e.memset(raws()[s][:, c:c + 1], 0.0).then_inc(sigref.sem, 1)

        zt = region(C, FREE, 2 * T)
        z3 = zt.rearrange("p (c t) -> p c t", c=2)

        def phase_hyena_in(l):
            ph = Phase()
            n0 = tiles[0]
            tiles[0] += 6
            ph.ends.append((tile_done.sem, tiles[0]))
            zeroed = ph.sig("pads_zeroed", 8)
            raw_ready = ph.sig("raw_ready", 6)
            conv_done = ph.sig("conv_done", 6)
            z_made = ph.sig("z_made", 2)
            order = [0, 2, 4, 1, 3, 5]
            tmp = region(X, 2 * RAW, T)
            src = a["w_in"][l].rearrange("(k p) n -> p k n", p=P)

            def pool(e):
                zero_pads(e, zeroed)

            def sp(e):
                for j, t in enumerate(order):
                    c = HY_COL + t * P
                    load_tile(e, tile(n0, 0, j), src, c, DK, P)

            def pe(e):
                for j in range(6):
                    product(e, tile(n0, 0, j), DK, P, h_rhs, False, (raw_ready, j - 1) if j >= 2 else None)

            def act(e):
                e.wait_ge(zeroed.sem, zeroed.at(8))
                for j in range(6):
                    n = n0 + j
                    e.wait_ge(tile_done.sem, n + 1)
                    if j >= 2:
                        e.wait_ge(conv_done.sem, conv_done.at(j - 1))
                    keep_raw(e, n % 2, raws()[j % 2], T, raw_ready)

            def dve(e):
                e.wait_ge(zeroed.sem, zeroed.at(8))
                for j, t in enumerate(order):
                    e.wait_ge(raw_ready.sem, raw_ready.at(j + 1))
                    kind, c = t // 2, t % 2
                    dst = hy3[:, c] if kind == 0 else (z3[:, c] if kind == 1 else tmp)
                    w = [vec("hy_conv_w", s * 6 + t) for s in range(3)]
                    conv(e, raws()[j % 2], w, vec("hy_conv_b", t), dst, T, conv_done)
                    if kind == 2:
                        e.wait_ge(conv_done.sem, conv_done.at(j + 1))
                        e.tensor_tensor(z3[:, c], z3[:, c], tmp, ALU.mult).then_inc(z_made.sem, 1)
                        e.wait_ge(z_made.sem, z_made.at(c + 1))
            ph.parts = dict(sp=sp, pe=pe, act=act, dve=dve, pool=pool)

        def phase_hyena_filter(l, length, at):
            ph = Phase()
            NT = length // P
            name = "lat" if length == SEQ else "ctx"
            HN = min(BANK, length)
            NH = length // HN
            ld = ph.sig("filter_loaded", 6, 16)
            ones = ph.sig("ones_row", 1)
            l1 = ph.sig("layer1", NH)
            s1 = ph.sig("sin1", NH)
            l2 = ph.sig("layer2", NH)
            s2 = ph.sig("sin2", NH)
            l3 = ph.sig("layer3", NT)
            dec = ph.sig("decay_made", NT)
            hh = ph.sig("filter_made", NT)
            ab = ph.sig("filter_abs", NT)
            nrm = ph.sig("norm_summed", NT)
            zt_ = ph.sig("z_turned", NT)
            zk = ph.sig("z_kept", NT)
            fin = ph.sig("inv_norm_made", 1)
            o = FREE + 2 * T
            zf = region(C, o, SEQ)
            h1 = region(C, o + SEQ, SEQ)
            h2 = region(C, o + 2 * SEQ, SEQ)
            t1 = region(C, o + 3 * SEQ, SEQ)
            t2 = region(C, o + 4 * SEQ, SEQ)
            o += 5 * SEQ
            w1 = region(C, o, HY_HID)
            w2 = region(C, o + 64, HY_HID)
            w3_ = region(C, o + 128, 2 * HY)
            o += 128 + 512
            hf = [region(C, o + s * 512, 512) for s in range(2)]
            ha = [region(C, o + 1024 + s * 512, 512) for s in range(2)]
            dc = [region(C, o + 2048 + s * 256, 256) for s in range(2)]
            nsum = region(C, o + 2560, 4)
            assert o + 2564 <= FT * T
            ezo = region(X, 0, NT * 768).rearrange("p (t w c) -> p t w c", w=3, c=HY)

            def pool(e):
                e.dma_start(zf[0:HY_EMB, 0:length], a["k_z_" + name]).then_inc(ld.sem, 16)
                e.dma_start(w1[0:HY_EMB, :], a["hy_w1"][l]).then_inc(ld.sem, 16)
                e.dma_start(w2[0:HY_HID, :], a["hy_w2"][l]).then_inc(ld.sem, 16)
                e.dma_start(w3_[0:HY_HID, :], a["hy_w3"][l]).then_inc(ld.sem, 16)
                e.dma_start(w3_[HY_HID:HY_HID + 1, :], a["hy_b3"][l:l + 1, :]).then_inc(ld.sem, 16)
                e.dma_start(t2[0:1, 0:1], a["c"][0:1, 0:1]).then_inc(ld.sem, 16)
                e.memset(h2[HY_HID:HY_HID + 1, 0:length], 1.0).then_inc(ones.sem, 1)

            def pe(e):
                e.wait_ge(ld.sem, ld.at(6))
                e.wait_ge(ones.sem, ones.at(1))
                for b in range(NH):
                    e.matmul(ps[0:64, b * BANK:b * BANK + HN], w1[0:HY_EMB, :], zf[0:HY_EMB, b * HN:b * HN + HN],
                             start=True, stop=True).then_inc(l1.sem, 1)
                for b in range(NH):
                    e.wait_ge(s1.sem, s1.at(b + 1))
                    e.matmul(ps[0:64, (2 + b) * BANK:(2 + b) * BANK + HN], w2[0:HY_HID, :],
                             h1[0:HY_HID, b * HN:b * HN + HN], start=True, stop=True).then_inc(l2.sem, 1)
                e.wait_ge(s2.sem, s2.at(NH))
                for t in range(NT):
                    if t >= 2:
                        e.wait_ge(hh.sem, hh.at(t - 1))
                    e.matmul(ps[:, (t % 2) * BANK:(t % 2) * BANK + 512], h2[0:HY_HID + 1, t * P:t * P + P],
                             w3_[0:HY_HID + 1, :], start=True, stop=True).then_inc(l3.sem, 1)
                    if t >= 2:
                        e.wait_ge(zk.sem, zk.at(t - 1))
                    for c in range(2):
                        ins = e.transpose(ps[:, (4 + t % 2) * BANK + c * P:(4 + t % 2) * BANK + c * P + P],
                                          z3[:, c, at + t * P:at + t * P + P], ident)
                    ins.then_inc(zt_.sem, 1)
                    if t >= 1:
                        sum_tile(e, t - 1)
                sum_tile(e, NT - 1)

            def sum_tile(e, t):
                e.wait_ge(ab.sem, ab.at(t + 1))
                for c in range(4):
                    ins = e.matmul(ps[:, 6 * BANK + c * 8 + t:6 * BANK + c * 8 + t + 1],
                                   ha[t % 2][:, c * P:c * P + P], K[:, K_ONES:K_ONES + 1], start=True, stop=True)
                ins.then_inc(nrm.sem, 1)

            def act(e):
                e.wait_ge(ld.sem, ld.at(6))
                for w, (pre, post, bank, hout) in enumerate(((sm1, s1, 0, h1), (sm2, s2, 2, h2))):
                    for b in range(NH):
                        e.wait_ge(pre.sem, pre.at(b + 1))
                        e.activation(hout[0:HY_HID, b * HN:b * HN + HN], t1[0:HY_HID, b * HN:b * HN + HN], ACT.Sin)\
                            .then_inc(post.sem, 1)
                for t in range(NT):
                    if t >= 2:
                        e.wait_ge(hh.sem, hh.at(t - 1))
                    c = K_TN + (0 if length == SEQ else SEQ // P) + t
                    e.activation(dc[t % 2], K[:, K_DELTA:K_DELTA + HY], ACT.Exp, scale=K[:, c:c + 1])\
                        .then_inc(dec.sem, 1)
                    e.wait_ge(zt_.sem, zt_.at(t + 1))
                    e.activation(ezo[:, t, 1, :], ps[:, (4 + t % 2) * BANK:(4 + t % 2) * BANK + HY], ACT.Copy)\
                        .then_inc(zk.sem, 1)
                    e.wait_ge(hh.sem, hh.at(t + 1))
                    if t >= 2:
                        e.wait_ge(nrm.sem, nrm.at(t - 1))
                    e.activation(ha[t % 2], hf[t % 2], ACT.Abs).then_inc(ab.sem, 1)

            sm1 = ph.sig("reduced1", NH)
            sm2 = ph.sig("reduced2", NH)
            ez = ph.sig("ezo_made", NT)

            def dve(e):
                link = chain["dve"].link
                MAGIC = 1.5 * 2.0 ** 23
                A1 = 6.28125
                A2 = float(np.float32(TWO_PI - A1))
                A3 = float(TWO_PI - A1 - A2)
                for w, (pre, post, bank, bias) in enumerate(((l1, sm1, 0, b1), (l2, sm2, 2, b2))):
                    for b in range(NH):
                        sl = slice(b * HN, b * HN + HN)
                        u, r = t1[0:HY_HID, sl], t2[0:HY_HID, sl]
                        e.wait_ge(pre.sem, pre.at(b + 1))
                        if w:
                            e.wait_ge(s1.sem, s1.at(b + 1))
                        link(e, e.tensor_scalar(u, ps[0:64, (bank + b) * BANK:(bank + b) * BANK + HN], bias, None, ALU.add))
                        link(e, e.tensor_scalar(r, u, float(1 / TWO_PI), MAGIC, ALU.mult, ALU.add))
                        link(e, e.tensor_scalar(r, r, -MAGIC, None, ALU.add))
                        link(e, e.scalar_tensor_tensor(u, r, -A1, u, ALU.mult, ALU.add))
                        link(e, e.scalar_tensor_tensor(u, r, -A2, u, ALU.mult, ALU.add))
                        link(e, e.scalar_tensor_tensor(u, r, -A3, u, ALU.mult, ALU.add))
                        e.tensor_scalar(u, u, 3.1415925, -3.1415925, ALU.min, ALU.max).then_inc(post.sem, 1)
                for t in range(NT):
                    e.wait_ge(l3.sem, l3.at(t + 1))
                    e.wait_ge(dec.sem, dec.at(t + 1))
                    if t >= 2:
                        e.wait_ge(ab.sem, ab.at(t - 1))
                    o_, i_ = hf[t % 2].rearrange("p (w c) -> p w c", w=2), \
                        ps[:, (t % 2) * BANK:(t % 2) * BANK + 512].rearrange("p (w c) -> p w c", w=2)
                    ins = e.tensor_tensor(o_, i_, dc[t % 2].unsqueeze(1).broadcast_to([P, 2, HY]), ALU.mult)
                    if t == 0:
                        link(e, ins)
                        ins = e.tensor_scalar(o_[:, 1, :], o_[:, 1, :], K[:, K_T0:K_T0 + 1], None, ALU.mult)
                    ins.then_inc(hh.sem, 1)
                    e.wait_ge(hh.sem, hh.at(t + 1))
                    e.tensor_tensor(ezo[:, t, 0, :], o_[:, 0, :], o_[:, 1, :], ALU.add)
                    e.tensor_tensor(ezo[:, t, 2, :], o_[:, 0, :], o_[:, 1, :], ALU.subtract).then_inc(ez.sem, 1)
                e.wait_ge(nrm.sem, nrm.at(NT))
                link(e, e.tensor_reduce(nsum, ps[:, 6 * BANK:6 * BANK + 32].rearrange("p (c t) -> p c t", t=8)[:, :, 0:NT],
                                        AX.X, ALU.add))
                link(e, e.tensor_tensor(nsum[:, 0:2], nsum[:, 0:2], nsum[:, 2:4], ALU.add))
                e.reciprocal(inv_norm, nsum[:, 0:2]).then_inc(fin.sem, 1)
            ph.parts = dict(pe=pe, act=act, dve=dve, pool=pool)

        def phase_hyena_conv(l, length, at):
            ph = Phase()
            NT = length // P
            name = "lat" if length == SEQ else "ctx"
            HN = min(BANK, length)
            NH = length // HN
            n0 = tiles[0]
            tiles[0] += 4 * NT
            ph.ends.append((tile_done.sem, tiles[0]))
            spec = ph.sig("spectrum_kept", NT)
            yy = ph.sig("products_made", NT)
            fin = ph.sig("hyena_out", 2)
            ezo = region(X, 0, NT * 768).rearrange("p (t w c) -> p t w c", w=3, c=HY)
            o = FREE + 2 * T
            y = region(C, o, NT * 512).rearrange("p (f r c) -> p f r c", r=2, c=HY)
            o += 4096
            sp_ = [region(C, o + s * 1024, 1024).rearrange("p (r c) -> p r c", r=4) for s in range(2)]
            ta = region(C, o + 2048, 256)
            tmp = region(C, o + 2304, T)

            def sp(e):
                for f in range(NT):
                    for r in range(2):
                        src = a["k_dft_" + name][r].rearrange("(k p) n -> p k n", p=P)
                        load_tile(e, tile(n0, 0, 2 * f + r), src, f * P, NT, P)
                for f in range(NT):
                    for r in range(2):
                        n = n0 + 2 * NT + 2 * f + r
                        e.wait_ge(tile_done.sem, n - 1)
                        e.dma_start(W[:, (n % 2) * D:(n % 2) * D + length], a["k_idft_" + name][r, f * P:f * P + P, :])\
                            .then_inc(w_loaded[n % 2].sem, 16)

            def pe(e):
                for f in range(NT):
                    if f >= 2:
                        e.wait_ge(spec.sem, spec.at(f - 1))
                    for r in range(2):
                        n = n0 + 2 * f + r
                        e.wait_ge(w_loaded[n % 2].sem, (n // 2 + 1) * 16)
                        b = 2 * (f % 2) + r
                        for t in range(NT):
                            ins = e.matmul(ps[:, b * BANK:b * BANK + 512], w3[:, n % 2, t, :],
                                           ezo[:, t, r:r + 2, :], start=(t == 0), stop=(t == NT - 1))
                        ins.then_inc(tile_done.sem, 1)
                for f in range(NT):
                    for r in range(2):
                        n = n0 + 2 * NT + 2 * f + r
                        e.wait_ge(w_loaded[n % 2].sem, (n // 2 + 1) * 16)
                        e.wait_ge(yy.sem, yy.at(f + 1))
                        for c in range(2):
                            for b in range(NH):
                                ins = e.matmul(ps[:, (4 + 2 * c + b) * BANK:(4 + 2 * c + b) * BANK + HN],
                                               y[:, f, r, c * P:c * P + P],
                                               W[:, (n % 2) * D + b * HN:(n % 2) * D + b * HN + HN],
                                               start=(f == 0 and r == 0), stop=(f == NT - 1 and r == 1))
                        ins.then_inc(tile_done.sem, 1)

            def act(e):
                for f in range(NT):
                    n = n0 + 2 * f + 1
                    e.wait_ge(tile_done.sem, n + 1)
                    if f >= 2:
                        e.wait_ge(yy.sem, yy.at(f - 1))
                    b = 2 * (f % 2)
                    e.activation(sp_[f % 2], ps[:, b * BANK:b * BANK + 1024].rearrange("p (r c) -> p r c", r=4),
                                 ACT.Copy).then_inc(spec.sem, 1)

            def dve(e):
                link = chain["dve"].link
                for f in range(NT):
                    e.wait_ge(spec.sem, spec.at(f + 1))
                    hr, zr, zs, hs = (sp_[f % 2][:, i] for i in range(4))
                    link(e, e.tensor_tensor(ta, zs, hs, ALU.mult))
                    link(e, e.tensor_tensor(y[:, f, 0], zr, hr, ALU.mult))
                    link(e, e.tensor_tensor(y[:, f, 0], y[:, f, 0], ta, ALU.subtract))
                    link(e, e.tensor_tensor(ta, zr, hs, ALU.mult))
                    link(e, e.tensor_tensor(y[:, f, 1], zs, hr, ALU.mult))
                    e.tensor_tensor(y[:, f, 1], y[:, f, 1], ta, ALU.add).then_inc(yy.sem, 1)
                    e.wait_ge(yy.sem, yy.at(f + 1))
                e.wait_ge(tile_done.sem, tiles_end)
                for c in range(2):
                    t_ = tmp[:, 0:length]
                    zz, oo = z3[:, c, at:at + length], hy3[:, c, at:at + length]
                    link(e, e.tensor_scalar(t_, zz, vec("hy_d", c), None, ALU.mult))
                    link(e, e.scalar_tensor_tensor(t_, ps[:, (4 + 2 * c) * BANK:(4 + 2 * c) * BANK + length],
                                                   inv_norm[:, c:c + 1], t_, ALU.mult, ALU.add))
                    e.tensor_tensor(oo, oo, t_, ALU.mult).then_inc(fin.sem, 1)
                    e.wait_ge(fin.sem, fin.at(c + 1))
            tiles_end = tiles[0]
            ph.parts = dict(sp=sp, pe=pe, act=act, dve=dve)

        CQ = region(C, FREE, 2 * T).rearrange("p (k t) -> p k t", k=2)
        CKV = region(C, FREE + 2 * T, T)
        KRAW = region(C, FREE + 3 * T, T)
        ATT = FREE + 4 * T

        def phase_mla_in(l):
            ph = Phase()
            n0 = tiles[0]
            tiles[0] += 4
            ph.ends.append((tile_done.sem, tiles[0]))
            kept = ph.sig("latents_kept", 4)
            src = a["w_in"][l].rearrange("(k p) n -> p k n", p=P)

            def sp(e):
                for j in range(4):
                    c = MLA_COL + j * P
                    w = P if j < 3 else ROPE
                    load_tile(e, tile(n0, 0, j), src, c, DK, w)

            def pe(e):
                for j in range(4):
                    product(e, tile(n0, 0, j), DK, P if j < 3 else ROPE, h_rhs, False,
                            (kept, j - 1) if j >= 2 else None, lo=0 if j < 3 else NOPE)

            def act(e):
                for j in range(4):
                    n = n0 + j
                    e.wait_ge(tile_done.sem, n + 1)
                    dst = (CQ[:, 0], CQ[:, 1], CKV, KRAW[NOPE:QK, :])[j]
                    src_ = group(n % 2, T) if j < 3 else group(n % 2, T, NOPE, QK)
                    e.activation(dst, src_, ACT.Copy).then_inc(kept.sem, 1)
            ph.parts = dict(sp=sp, pe=pe, act=act)

        def phase_mla_norm(l):
            ph = Phase()
            squared = ph.sig("squared", 3)
            summed = ph.sig("squares_summed", 2)
            root = ph.sig("root_made", 2)
            inv = ph.sig("rstd_made", 2)
            made = ph.sig("latents_normed", 3)
            sq = [region(X, s * T, T) for s in range(3)]
            rt = [region(X, (3 + s) * T, T) for s in range(2)]
            src = (CQ[:, 0], CQ[:, 1], CKV)

            def act(e):
                for j in range(3):
                    e.activation(sq[j], src[j], ACT.Square).then_inc(squared.sem, 1)
                for w, r in enumerate((QR, KVR)):
                    e.wait_ge(summed.sem, summed.at(w + 1))
                    e.activation(rt[w], group(w, T), ACT.Sqrt, bias=eps, scale=1.0 / r).then_inc(root.sem, 1)

            def pe(e):
                for w, js in enumerate(((0, 1), (2,))):
                    e.wait_ge(squared.sem, squared.at(js[-1] + 1))
                    for b, (t0, tn) in enumerate(tok(False)):
                        for j in js:
                            ins = e.matmul(ps[:, w * GROUP + b * BANK:w * GROUP + b * BANK + tn],
                                           K[:, K_ONES:K_ONES + P], sq[j][:, t0:t0 + tn],
                                           start=(j == js[0]), stop=(j == js[-1]))
                    ins.then_inc(summed.sem, 1)

            def dve(e):
                for w, js in enumerate(((0, 1), (2,))):
                    e.wait_ge(root.sem, root.at(w + 1))
                    e.reciprocal(rt[w], rt[w]).then_inc(inv.sem, 1)
                    e.wait_ge(inv.sem, inv.at(w + 1))
                    for j in js:
                        g = vec("mla_q_norm_g", j) if j < 2 else vec("mla_kv_norm_g")
                        e.scalar_tensor_tensor(src[j], src[j], g, rt[w], ALU.mult, ALU.mult).then_inc(made.sem, 1)
            ph.parts = dict(pe=pe, act=act, dve=dve)

        def phase_mla_heads(l, last):
            ph = Phase()
            NQ = 8 if last else 10
            SCALE = float(QK) ** -0.5
            HD = HEADS
            rope_ld = ph.sig("rope_loaded", 2, 16)
            wl = [ph.sig("head_w_0", 3, 32), ph.sig("head_w_1", 3, 32)]
            proj = ph.sig("head_projected", 3 * HD)
            kept = ph.sig("head_kept", 3 * HD)
            squared = ph.sig("head_squared", 2 * HD)
            summed = ph.sig("head_summed", 2 * HD)
            root = ph.sig("head_root", 2 * HD)
            inv = ph.sig("head_rstd", 2 * HD)
            normed = ph.sig("head_normed", 2 * HD)
            turned = ph.sig("head_turned", 2 * HD)
            sined = ph.sig("head_sined", 2 * HD)
            cosed = ph.sig("head_cosed", 2 * HD)
            roped = ph.sig("head_roped", 2 * HD)
            scored = ph.sig("scored", NQ * HD)
            maxed = ph.sig("maxed", NQ * HD)
            shifted = ph.sig("shift_made", NQ * HD)
            exped = ph.sig("exped", NQ * HD)
            rsum = ph.sig("sum_inverted", NQ * HD)
            scaled = ph.sig("probs_scaled", NQ * HD)
            pturned = ph.sig("probs_turned", 3 * NQ * HD)
            pkept_a = ph.sig("probs_kept_act", 2 * NQ * HD)
            pkept_d = ph.sig("probs_kept_dve", NQ * HD)
            mixed = ph.sig("values_mixed", NQ * HD)
            okept = ph.sig("attention_kept", NQ * HD)
            o = ATT
            Q, Kh, SQ0, SQ1, RT0, RT1, QRAW = (region(C, o + j * T, T) for j in range(7))
            o += 7 * T
            cos, sin = region(C, o, SEQ), region(C, o + SEQ, SEQ)
            o += 2 * SEQ
            V = region(C, o, 10 * VD).rearrange("p (t v) -> p t v", v=VD)
            o += 10 * VD
            assert o + 2 * T <= FT * T
            PR = [region(C, o + s * T, T) for s in range(2)]
            PT = [region(X, s * T, T).rearrange("p (b q) -> p b q", q=P) for s in range(2)]
            TM = [region(X, (2 + s) * T, T) for s in range(2)]
            wq = [region(X, 4 * T + s * 320, 192).rearrange("p (k n) -> p k n", k=2) for s in range(2)]
            wkv = [region(X, 4 * T + s * 320 + 192, 128) for s in range(2)]
            st = region(X, 4 * T + 640, 8)
            raws_, outs_, sqs, rts = (QRAW, KRAW), (Q, Kh), (SQ0, SQ1), (RT0, RT1)

            def blocks(t):
                return (0, T) if t < 8 else (SEQ, CTX)

            def sp(e):
                for r, t_ in enumerate((cos, sin)):
                    e.dma_start(t_[0:QK, :], a["k_rope"][r]).then_inc(rope_ld.sem, 16)
                uq = a["mla_w_uq"][l].rearrange("(k p) n -> p k n", p=P)
                ukv = a["mla_w_ukv"][l]

                def load(u, cq, ckv):
                    e.dma_start(wq[u], uq[:, :, bass.ds(cq, QK)]).then_inc(wl[u].sem, 16)
                    e.dma_start(wkv[u], ukv[:, bass.ds(ckv, 2 * VD)]).then_inc(wl[u].sem, 16)

                for u in range(2):
                    load(u, u * QK, u * 2 * VD)
                with e.Fori(1, 3) as i:
                    for u in range(2):
                        cq, ckv = e.snap(i * (2 * QK) + u * QK), e.snap(i * (4 * VD) + u * 2 * VD)
                        e.wait_ge(proj.sem, proj.at(i * 6 + (3 * u - 3)))
                        load(u, cq, ckv)

            def pe(e):
                e.wait_ge(rope_ld.sem, rope_ld.at(2))
                with e.Fori(0, 3) as i:
                    for u in range(2):
                        h2 = i * 2 + u
                        e.wait_ge(wl[u].sem, wl[u].at(i + 1))
                        for b, (t0, tn) in enumerate(tok(False)):
                            for k in range(2):
                                ins = e.matmul(ps[0:QK, b * BANK:b * BANK + tn], wq[u][:, k, :], CQ[:, k, t0:t0 + tn],
                                               start=(k == 0), stop=(k == 1))
                        ins.then_inc(proj.sem, 1)
                        for b, (t0, tn) in enumerate(tok(False)):
                            ins = e.matmul(ps[0:NOPE, GROUP + b * BANK:GROUP + b * BANK + tn], wkv[u][:, 0:NOPE],
                                           CKV[:, t0:t0 + tn], start=True, stop=True)
                        ins.then_inc(proj.sem, 1)
                        for t in range(10):
                            ins = e.matmul(ps[:, 6 * BANK + t * VD:6 * BANK + t * VD + VD], CKV[:, t * P:t * P + P],
                                           wkv[u][:, NOPE:NOPE + VD], start=True, stop=True)
                        ins.then_inc(proj.sem, 1)
                        for j in range(2):
                            e.wait_ge(squared.sem, squared.at(h2 * 2 + j + 1))
                            for b, (t0, tn) in enumerate(tok(False)):
                                ins = e.matmul(ps[0:QK, j * GROUP + b * BANK:j * GROUP + b * BANK + tn],
                                               K[0:QK, K_ONES:K_ONES + QK], sqs[j][0:QK, t0:t0 + tn], start=True, stop=True)
                            ins.then_inc(summed.sem, 1)
                        for j in range(2):
                            e.wait_ge(normed.sem, normed.at(h2 * 2 + j + 1))
                            for b in range(2):
                                ins = e.matmul(ps[0:QK, j * GROUP + b * BANK:j * GROUP + b * BANK + BANK],
                                               K[0:QK, K_ROT:K_ROT + QK], outs_[j][0:QK, b * BANK:b * BANK + BANK],
                                               start=True, stop=True)
                            ins.then_inc(turned.sem, 1)
                        e.wait_ge(roped.sem, roped.at(h2 * 2 + 2))

                        def score(t):
                            k0, kn = blocks(t)
                            g = t % 2
                            for b in range(0, kn, BANK):
                                n = min(BANK, kn - b)
                                ins = e.matmul(ps[:, g * GROUP + b:g * GROUP + b + n], Q[0:QK, t * P:t * P + P],
                                               Kh[0:QK, k0 + b:k0 + b + n], start=True, stop=True)
                            ins.then_inc(scored.sem, 1)

                        score(0)
                        score(1)
                        for t in range(NQ):
                            at = h2 * NQ + t
                            k0, kn = blocks(t)
                            g = t % 2
                            nb = kn // P
                            e.wait_ge(scaled.sem, scaled.at(at + 1))
                            for c in range(3):
                                if c == 0 and t:
                                    e.wait_ge(pkept_a.sem, pkept_a.at(at * 2))
                                if c == 1 and t:
                                    e.wait_ge(pkept_d.sem, pkept_d.at(at))
                                if c == 2:
                                    e.wait_ge(pkept_a.sem, pkept_a.at(at * 2 + 1))
                                bank = 6 + c % 2
                                last_ = None
                                for q in range(4):
                                    b = 4 * c + q
                                    if b < nb:
                                        last_ = e.transpose(ps[:, bank * BANK + q * P:bank * BANK + q * P + P],
                                                            PR[g][:, b * P:b * P + P], ident)
                                    elif last_ is None:
                                        last_ = e.transpose(ps[:, bank * BANK + q * P:bank * BANK + q * P + P],
                                                            PR[g][:, 0:P], ident)
                                last_.then_inc(pturned.sem, 1)
                            e.wait_ge(pkept_a.sem, pkept_a.at(at * 2 + 2))
                            e.wait_ge(pkept_d.sem, pkept_d.at(at + 1))
                            at_col = g * GROUP + 2 * BANK + CTX
                            for b in range(nb):
                                ins = e.matmul(ps[u * 64:u * 64 + 64, at_col:at_col + P], V[:, k0 // P + b, :],
                                               PT[g][:, b, :], start=(b == 0), stop=(b == nb - 1))
                            ins.then_inc(mixed.sem, 1)
                            if t + 2 < NQ:
                                e.wait_ge(okept.sem, okept.at(at + 1))
                                score(t + 2)
                        e.wait_ge(okept.sem, okept.at(h2 * NQ + NQ))

            def act(e):
                with e.Fori(0, 3) as i:
                    for u in range(2):
                        h2 = i * 2 + u
                        e.wait_ge(proj.sem, proj.at(h2 * 3 + 1))
                        e.activation(QRAW[0:QK, :], group(0, T, 0, QK), ACT.Copy).then_inc(kept.sem, 1)
                        e.wait_ge(proj.sem, proj.at(h2 * 3 + 2))
                        e.activation(KRAW[0:NOPE, :], group(1, T, 0, NOPE), ACT.Copy).then_inc(kept.sem, 1)
                        e.wait_ge(proj.sem, proj.at(h2 * 3 + 3))
                        e.activation(V, ps[:, 6 * BANK:6 * BANK + 10 * VD].rearrange("p (t v) -> p t v", v=VD), ACT.Copy)\
                            .then_inc(kept.sem, 1)
                        e.wait_ge(kept.sem, kept.at(h2 * 3 + 3))
                        for j in range(2):
                            e.activation(sqs[j][0:QK, :], raws_[j][0:QK, :], ACT.Square).then_inc(squared.sem, 1)
                        for j in range(2):
                            e.wait_ge(summed.sem, summed.at(h2 * 2 + j + 1))
                            e.activation(rts[j][0:QK, :], group(j, T, 0, QK), ACT.Sqrt, bias=eps[0:QK, :], scale=1.0 / QK)\
                                .then_inc(root.sem, 1)

                        for t in range(NQ):
                            at = h2 * NQ + t
                            kn = blocks(t)[1]
                            nb = kn // P
                            g = t % 2
                            e.wait_ge(shifted.sem, shifted.at(at + 1))
                            e.activation(PR[g][:, 0:kn], ps[:, g * GROUP:g * GROUP + kn], ACT.Exp, bias=st[:, 2 + g:3 + g],
                                         scale=SCALE, accum_out=st[:, 4 + g:5 + g]).then_inc(exped.sem, 1)
                            for c in (0, 2):
                                n = max(1, min(4, nb - 4 * c))
                                e.wait_ge(pturned.sem, pturned.at(at * 3 + c + 1))
                                b0 = 4 * c if 4 * c < nb else 9
                                e.activation(PT[g][:, b0:b0 + n, :],
                                             ps[:, 6 * BANK:6 * BANK + n * P].rearrange("p (b q) -> p b q", q=P), ACT.Copy)\
                                    .then_inc(pkept_a.sem, 1)
                            e.wait_ge(mixed.sem, mixed.at(at + 1))
                            col = g * GROUP + 2 * BANK + CTX
                            e.activation(MLA_OUT[u * 64:u * 64 + 64, bass.ds(i * T + t * P, P)],
                                         ps[u * 64:u * 64 + 64, col:col + P], ACT.Copy).then_inc(okept.sem, 1)

            def dve(e):
                with e.Fori(0, 3) as i:
                    for u in range(2):
                        h2 = i * 2 + u
                        for j in range(2):
                            at = h2 * 2 + j + 1
                            e.wait_ge(root.sem, root.at(at))
                            e.reciprocal(rts[j][0:QK, :], rts[j][0:QK, :]).then_inc(inv.sem, 1)
                            e.wait_ge(inv.sem, inv.at(at))
                            e.scalar_tensor_tensor(outs_[j][0:QK, :], raws_[j][0:QK, :], (q_g, k_g)[j],
                                                   rts[j][0:QK, :], ALU.mult, ALU.mult).then_inc(normed.sem, 1)
                        for j in range(2):
                            at = h2 * 2 + j + 1
                            e.wait_ge(turned.sem, turned.at(at))
                            e.tensor_tensor(TM[j][0:QK, 0:SEQ], group(j, SEQ, 0, QK), sin[0:QK, :], ALU.mult)\
                                .then_inc(sined.sem, 1)
                            lat = outs_[j][0:QK, 0:SEQ]
                            e.tensor_tensor(lat, lat, cos[0:QK, :], ALU.mult).then_inc(cosed.sem, 1)
                            e.wait_ge(cosed.sem, cosed.at(at))
                            e.wait_ge(sined.sem, sined.at(at))
                            e.tensor_tensor(lat, lat, TM[j][0:QK, 0:SEQ], ALU.add).then_inc(roped.sem, 1)

                        def shift(t):
                            at = h2 * NQ + t + 1
                            g, kn = t % 2, blocks(t)[1]
                            e.wait_ge(scored.sem, scored.at(at))
                            e.tensor_reduce(st[:, g:g + 1], ps[:, g * GROUP:g * GROUP + kn], AX.X, ALU.max)\
                                .then_inc(maxed.sem, 1)
                            e.wait_ge(maxed.sem, maxed.at(at))
                            e.tensor_scalar(st[:, 2 + g:3 + g], st[:, g:g + 1], -SCALE, None, ALU.mult)\
                                .then_inc(shifted.sem, 1)

                        shift(0)
                        for t in range(NQ):
                            at = h2 * NQ + t + 1
                            g, kn = t % 2, blocks(t)[1]
                            nb = kn // P
                            if t + 1 < NQ:
                                shift(t + 1)
                            e.wait_ge(exped.sem, exped.at(at))
                            e.reciprocal(st[:, 6 + g:7 + g], st[:, 4 + g:5 + g]).then_inc(rsum.sem, 1)
                            e.wait_ge(rsum.sem, rsum.at(at))
                            e.tensor_scalar(PR[g][:, 0:kn], PR[g][:, 0:kn], st[:, 6 + g:7 + g], None, ALU.mult)\
                                .then_inc(scaled.sem, 1)
                            n = max(1, min(4, nb - 4))
                            b0 = 4 if nb > 4 else 8
                            e.wait_ge(pturned.sem, pturned.at(at * 3 - 1))
                            e.tensor_copy(PT[g][:, b0:b0 + n, :],
                                          ps[:, 7 * BANK:7 * BANK + n * P].rearrange("p (b q) -> p b q", q=P))\
                                .then_inc(pkept_d.sem, 1)
                        e.wait_ge(okept.sem, okept.at(h2 * NQ + NQ))
            ph.parts = dict(sp=sp, pe=pe, act=act, dve=dve)

        GQ = FREE
        qkv = region(C, GQ, 9 * T).rearrange("p (n t) -> p n t", n=9)
        zz3 = region(C, GQ + 9 * T, 3 * T).rearrange("p (n t) -> p n t", n=3)
        O_OUT = region(C, GQ + 12 * T, 3 * T)
        o3 = O_OUT.rearrange("p (n t) -> p n t", n=3)
        abT = region(C, GQ + 15 * T, T)
        GT = region(C, GQ + 16 * T, N_CHUNK * 36)
        assert GQ + 16 * T + N_CHUNK * 36 <= FT * T
        gt5 = GT.rearrange("p (n d k q) -> p n d k q", n=N_CHUNK, d=2, k=6)

        def phase_gdn_in(l):
            ph = Phase()
            n0 = tiles[0]
            tiles[0] += 13
            ph.ends.append((tile_done.sem, tiles[0]))
            zeroed = ph.sig("pads_zeroed", 8)
            raw_ready = ph.sig("raw_ready", 9)
            conv_done = ph.sig("conv_done", 9)
            silu = ph.sig("silu_made", 9)
            zk = ph.sig("z_gate_kept", 4)
            src = a["w_in"][l].rearrange("(k p) n -> p k n", p=P)
            cv = [region(X, 2 * RAW + s * T, T) for s in range(2)]

            def pool(e):
                zero_pads(e, zeroed)

            def sp(e):
                with e.Fori(0, 4) as i:
                    for u in range(2):
                        load_tile(e, tile(n0, i, u), src, i * 256 + u * P, DK, P)
                for j in range(8, 13):
                    w = P if j < 12 else 4 * HEADS
                    load_tile(e, tile(n0, 0, j), src, j * P, DK, w)

            def pe(e):
                product(e, tile(n0, 0, 0), DK, P, h_rhs, False)
                product(e, tile(n0, 0, 1), DK, P, h_rhs, False)
                with e.Fori(1, 4) as i:
                    for u in range(2):
                        product(e, tile(n0, i, u), DK, P, h_rhs, False, (raw_ready, i * 2 + (u - 1)))
                for j in range(8, 13):
                    free = (raw_ready, j - 1) if j < 11 else (zk, j - 10)
                    product(e, tile(n0, 0, j), DK, P if j < 12 else 4 * HEADS, h_rhs, False, free)

            def conv_act(e, i, u, j):
                g, n, _ = tile(n0, i, u)
                e.wait_ge(tile_done.sem, n + 1)
                keep_raw(e, g, raws()[u], T, raw_ready)
                e.wait_ge(conv_done.sem, conv_done.at(j + 1))
                dst = region(C, GQ, 9 * T)[:, bass.ds(j * T, T)] if not isinstance(j, int) else qkv[:, j]
                e.activation(dst, cv[u], ACT.Silu).then_inc(silu.sem, 1)

            def act(e):
                e.wait_ge(zeroed.sem, zeroed.at(8))
                with e.Fori(0, 4) as i:
                    for u in range(2):
                        conv_act(e, i, u, i * 2 + u)
                conv_act(e, 4, 0, 8)
                for j in range(9, 13):
                    n = n0 + j
                    e.wait_ge(tile_done.sem, n + 1)
                    if j < 12:
                        e.activation(zz3[:, j - 9], group(n % 2, T), ACT.Silu).then_inc(zk.sem, 1)
                    else:
                        e.activation(abT[0:24, :], group(n % 2, T, 0, 24), ACT.Copy).then_inc(zk.sem, 1)

            def one_conv(e, u, j):
                e.wait_ge(raw_ready.sem, raw_ready.at(j + 1))
                w = [S[:, bass.ds(VCOL["gdn_conv_w"] + s * 9 + j, 1)] if not isinstance(j, int)
                     else vec("gdn_conv_w", s * 9 + j) for s in range(3)]
                conv(e, raws()[u], w, None, cv[u], T, conv_done)
                e.wait_ge(silu.sem, silu.at(j + 1))

            def dve(e):
                e.wait_ge(zeroed.sem, zeroed.at(8))
                with e.Fori(0, 4) as i:
                    chain["dve"].loop(i, 4)
                    for u in range(2):
                        one_conv(e, u, i * 2 + u)
                chain["dve"].end(4)
                one_conv(e, 0, 8)
            ph.parts = dict(sp=sp, pe=pe, act=act, dve=dve, pool=pool)

        def phase_head_norm(l, kind):
            ph = Phase()
            n = 6 if kind == "qk" else 3
            squared = ph.sig("squared", n)
            summed = ph.sig("squares_summed", n)
            root = ph.sig("root_made", n)
            inv = ph.sig("rstd_made", n)
            made = ph.sig("heads_normed", n)
            sq = [region(X, s * T, T) for s in range(2)]
            rt = [region(X, (2 + s) * T, T) for s in range(2)]

            def part(j):
                return qkv[:, j] if kind == "qk" else o3[:, j]

            def act(e):
                for j in range(n + 1):
                    if j < n:
                        if j >= 2:
                            e.wait_ge(summed.sem, summed.at(j - 1))
                        e.activation(sq[j % 2], part(j), ACT.Square).then_inc(squared.sem, 1)
                    if j >= 1:
                        e.wait_ge(summed.sem, summed.at(j))
                        if j >= 3:
                            e.wait_ge(made.sem, made.at(j - 2))
                        e.activation(rt[(j - 1) % 2], group((j - 1) % 2, T), ACT.Sqrt, bias=eps,
                                     scale=1.0 if kind == "qk" else 1.0 / CH).then_inc(root.sem, 1)

            def pe(e):
                for j in range(n):
                    e.wait_ge(squared.sem, squared.at(j + 1))
                    if j >= 2:
                        e.wait_ge(root.sem, root.at(j - 1))
                    for b, (t0, tn) in enumerate(tok(False)):
                        ins = e.matmul(ps[:, (j % 2) * GROUP + b * BANK:(j % 2) * GROUP + b * BANK + tn],
                                       K[:, K_BLOCK:K_BLOCK + P], sq[j % 2][:, t0:t0 + tn], start=True, stop=True)
                    ins.then_inc(summed.sem, 1)

            def dve(e):
                for j in range(n):
                    r = rt[j % 2]
                    e.wait_ge(root.sem, root.at(j + 1))
                    e.reciprocal(r, r).then_inc(inv.sem, 1)
                    e.wait_ge(inv.sem, inv.at(j + 1))
                    if kind == "qk":
                        e.scalar_tensor_tensor(part(j), part(j), CH ** -0.5 if j < 3 else 1.0, r, ALU.mult, ALU.mult)\
                            .then_inc(made.sem, 1)
                    else:
                        chain["dve"].link(e, e.scalar_tensor_tensor(part(j), part(j), gdn_g, r, ALU.mult, ALU.mult))
                        e.tensor_tensor(part(j), part(j), zz3[:, j], ALU.mult).then_inc(made.sem, 1)
            ph.parts = dict(pe=pe, act=act, dve=dve)

        def phase_gates(l):
            ph = Phase()
            abm = ph.sig("gates_turned", 1)
            cut = ph.sig("gates_cut", 2)
            biased = ph.sig("gate_biased", 1)
            absd = ph.sig("gate_abs", 1)
            e1 = ph.sig("gate_exp", 2)
            ln = ph.sig("gate_log", 1)
            sig_ = ph.sig("beta_made", 1)
            sp_ = ph.sig("softplus_made", 1)
            gm = ph.sig("g_made", 1)
            summed = ph.sig("g_summed", 1)
            gk = ph.sig("gc_kept", 2)
            ex = ph.sig("gate_exps", 3)
            be = ph.sig("beta_decay_made", 1)
            NU = N_CHUNK * 2 * PAIRS
            AB = region(X, 0, N_CHUNK * 12)
            ab4 = AB.rearrange("p (n x q) -> p n x q", n=N_CHUNK, x=4)
            t1, t2, t3, t4 = (region(X, 240 + j * NU, NU).rearrange("p (n x q) -> p n x q", n=N_CHUNK, x=2)
                              for j in range(4))
            ea = region(X, 240 + 4 * NU, 6)

            def pe(e):
                for n in range(N_CHUNK):
                    for h in range(2):
                        ins = e.matmul(ps[h * 64:h * 64 + 64, n * 24:n * 24 + 24], abT[0:24, n * CH:n * CH + CH],
                                       ident[0:24, 0:24], start=True, stop=True)
                ins.then_inc(abm.sem, 1)
                e.wait_ge(gm.sem, gm.at(1))
                for h in range(2):
                    r = slice(h * 64, h * 64 + 64)
                    for d in range(2):
                        g = gt5[r, :, d, 0, :]
                        e.matmul(ps[r, BANK + d * 60:BANK + d * 60 + 60], K[r, K_CUM + d * CH:K_CUM + d * CH + CH], g,
                                 start=True, stop=True)
                        ins = e.matmul(ps[r, 2 * BANK + d * 60:2 * BANK + d * 60 + 60], K[r, K_ONES:K_ONES + CH], g,
                                       start=True, stop=True)
                ins.then_inc(summed.sem, 1)

            def act(e):
                e.activation(ea, AL, ACT.Exp).then_inc(e1.sem, 1)
                e.wait_ge(absd.sem, absd.at(1))
                e.activation(t3, t2, ACT.Exp, scale=-1.0).then_inc(e1.sem, 1)
                e.wait_ge(e1.sem, e1.at(2))
                e.activation(t4, t3, ACT.Ln, bias=1.0).then_inc(ln.sem, 1)
                e.activation(gt5[:, :, :, 2, :], ab4[:, :, 2:4, :], ACT.Sigmoid).then_inc(sig_.sem, 1)
                e.wait_ge(gk.sem, gk.at(2))
                e.activation(gt5[:, :, :, 4, :], t1, ACT.Exp).then_inc(ex.sem, 1)
                e.activation(gt5[:, :, :, 5, :], t3, ACT.Exp).then_inc(ex.sem, 1)
                e.activation(gt5[:, :, :, 3, :], gt5[:, :, :, 1, :], ACT.Exp).then_inc(ex.sem, 1)

            def dve(e):
                e.wait_ge(abm.sem, abm.at(1))
                for h in range(2):
                    r = slice(h * 64, h * 64 + 64)
                    v = ps[r, 0:N_CHUNK * 24].rearrange("p (n x q h) -> p n x q h", n=N_CHUNK, x=4, h=2)[:, :, :, :, h]
                    e.tensor_copy(ab4[r], v).then_inc(cut.sem, 1)
                e.wait_ge(cut.sem, cut.at(2))
                dt_ = DT.rearrange("p (x q) -> p x q", x=2).unsqueeze(1).broadcast_to([P, N_CHUNK, 2, PAIRS])
                e.tensor_tensor(t1, ab4[:, :, 0:2, :], dt_, ALU.add).then_inc(biased.sem, 1)
                e.wait_ge(biased.sem, biased.at(1))
                e.scalar_tensor_tensor(t2, t1, -1.0, t1, ALU.mult, ALU.max).then_inc(absd.sem, 1)
                e.wait_ge(ln.sem, ln.at(1))
                e.scalar_tensor_tensor(t1, t1, 0.0, t4, ALU.max, ALU.add).then_inc(sp_.sem, 1)
                e.wait_ge(sp_.sem, sp_.at(1))
                ea_ = ea.rearrange("p (x q) -> p x q", x=2).unsqueeze(1).broadcast_to([P, N_CHUNK, 2, PAIRS])
                chain["dve"].link(e, e.tensor_tensor(t1, t1, ea_, ALU.mult))
                e.tensor_scalar(gt5[:, :, :, 0, :], t1, -1.0, None, ALU.mult).then_inc(gm.sem, 1)
                e.wait_ge(summed.sem, summed.at(1))
                sums = [ps[:, b * BANK:b * BANK + 120].rearrange("p (x n q) -> p n x q", x=2, q=PAIRS) for b in (1, 2)]
                chain["dve"].link(e, e.tensor_copy(gt5[:, :, :, 1, :], sums[0]))
                e.tensor_copy(t3, sums[1]).then_inc(gk.sem, 1)
                e.wait_ge(gk.sem, gk.at(1))
                e.tensor_tensor(t1, t3, gt5[:, :, :, 1, :], ALU.subtract).then_inc(gk.sem, 1)
                e.wait_ge(ex.sem, ex.at(3))
                e.tensor_tensor(gt5[:, :, :, 3, :], gt5[:, :, :, 3, :], gt5[:, :, :, 2, :], ALU.mult).then_inc(be.sem, 1)
            ph.parts = dict(pe=pe, act=act, dve=dve)

        def phase_scan(l):
            ph = Phase()
            NS = N_CHUNK
            U3 = PAIRS * CH
            zeroed = ph.sig("scan_zeroed", 2)
            staged = ph.sig("staged", 2 * NS)
            prods = ph.sig("kk_kq_made", 2 * NS)
            rbs = ph.sig("rows_spread", 2 * NS)
            tms = ph.sig("kv_turned", 2 * NS)
            eg = ph.sig("decay_row_made", 2 * NS)
            decin = ph.sig("decay_arg_made", 2 * NS)
            dec = ph.sig("decay_mat_made", 2 * NS)
            rvw = ph.sig("rhs_made", 2 * NS)
            kqd = ph.sig("kq_decayed", 2 * NS)
            att = ph.sig("a_made", 2 * NS)
            qd = ph.sig("q_decayed", 2 * NS)
            xt0 = ph.sig("xt0_made", 2 * NS)
            am = ph.sig("a_levels", 2 * (LEVELS - 1) * NS)
            x0 = ph.sig("x0_turned", 2 * NS)
            x0k = ph.sig("x0_kept", 2 * NS)
            t1 = ph.sig("ax_made", 2 * (LEVELS - 1) * NS)
            t1k = ph.sig("ax_kept", 2 * (LEVELS - 1) * NS)
            dx = ph.sig("xax_made", 2 * (LEVELS - 1) * NS)
            xup = ph.sig("x_updated", 2 * (LEVELS - 1) * NS)
            uw = ph.sig("uw_made", 2 * NS)
            uwk = ph.sig("uw_kept", 2 * NS)
            ws = ph.sig("ws_made", 2 * NS)
            dl = ph.sig("delta_made", 2 * NS)
            om = ph.sig("o_made", 2 * NS)
            ds_ = ph.sig("ds_made", 2 * NS)
            snew = ph.sig("state_made", 2 * NS)
            oadd = ph.sig("o_added", 2 * NS)
            o = 0

            def buf(n=2 * U3):
                nonlocal o
                r = region(X, o, n)
                o += n
                return r

            def mats(r):
                return r.rearrange("p (d q i) -> p d q i", d=2, q=PAIRS)

            ST = buf(2 * 9 * CH)
            st4 = ST.rearrange("p (d n i) -> p d n i", d=2, n=9)
            GS = buf(36)
            gs4 = GS.rearrange("p (d k q) -> p d k q", d=2, k=6)
            DEC, EG, AT, KQD, QD, T0, XT, XX, T1S, RV, RW, KD, DL, SS, SC = (mats(buf()) for _ in range(15))
            AM = buf(5 * 2 * U3).rearrange("p (m d q i) -> p m d q i", m=5, d=2, q=PAIRS)
            UWb = buf(4 * U3).rearrange("p (d w q i) -> p d w q i", d=2, w=2, q=PAIRS)
            assert o <= DK * T

            def bank(d, b, w=U3, at=0, lo=0, hi=P):
                c = (4 * d + b) * BANK + at
                return ps[lo:hi, c:c + w]

            def bank3(d, b, at=0):
                return bank(d, b, U3, at).rearrange("p (q i) -> p q i", q=PAIRS)

            def each():
                for q in range(PAIRS):
                    for h in range(2):
                        yield q, slice(h * 64, h * 64 + 64)

            def col(k, d):
                return gs4[:, d, k, :].unsqueeze(2).broadcast_to([P, PAIRS, CH])

            def const3(c):
                return K[:, c:c + CH].unsqueeze(1).broadcast_to([P, PAIRS, CH])

            def spans():
                return ((CTX_CHUNKS, 0, (lambda i: i + LAT_CHUNKS, lambda i: i * -1 + (N_CHUNK - 1))),
                        (LAT_CHUNKS, CTX_CHUNKS, (lambda i: i, lambda i: i * -1 + (LAT_CHUNKS - 1))))

            def pool(e):
                e.memset(O_OUT, 0.0).then_inc(zeroed.sem, 1)
                e.memset(SS, 0.0).then_inc(zeroed.sem, 1)
                qf = region(C, GQ, 9 * T).rearrange("p (n t) -> p n t", n=9)
                for n, s0, chunk in spans():
                    with e.Fori(0, n) as i:
                        s = i + s0
                        for d in range(2):
                            e.tensor_copy(st4[:, d], qf[:, :, bass.ds(chunk[d](i) * CH, CH)])
                            e.tensor_copy(gs4[:, d].rearrange("p k q -> p (k q)"),
                                          GT[:, bass.ds(chunk[d](i) * 36 + d * 18, 18)]).then_inc(staged.sem, 1)
                        e.wait_ge(staged.sem, staged.at(s * 2 + 2))
                        for d in range(2):
                            e.wait_ge(eg.sem, eg.at(s * 2 + d + 1))
                            e.tensor_tensor(QD[:, d], st4[:, d, 0:3], EG[:, d], ALU.mult).then_inc(qd.sem, 1)
                        for m in range(1, LEVELS):
                            for d in range(2):
                                if m == 1:
                                    e.wait_ge(att.sem, att.at(s * 2 + d + 1))
                                e.tensor_tensor(AM[:, m - 1, d], AT[:, d], const3(K_LEVEL + (m * 2 + d) * CH), ALU.mult)\
                                    .then_inc(am.sem, 1)
                        e.wait_ge(qd.sem, qd.at(s * 2 + 2))
                        e.wait_ge(tms.sem, tms.at(s * 2 + 2))
                        e.wait_ge(xt0.sem, xt0.at(s * 2 + 2))
                        e.wait_ge(om.sem, om.at(s * 2 + 2))
                        e.wait_ge(am.sem, am.at(s * 10 + 10))

            def await_(e, *waits):
                counts = [e.to_reg(v) for _, v in waits]
                e.wait_ge(zeroed.sem, zeroed.at(2))
                for (r, _), v in zip(waits, counts):
                    e.wait_ge(r.sem, v)

            def pe(e):
                e.wait_ge(zeroed.sem, zeroed.at(2))
                for n, s0, _ in spans():
                    with e.Fori(0, n) as i:
                        s = i + s0

                        def at(r, d, j=0, per=1):
                            return r.at(s * (2 * per) + j * 2 + d + 1)

                        for d in range(2):
                            await_(e, (staged, at(staged, d)))
                            for q, r in each():
                                ins = e.matmul(bank(d, 0, 2 * CH, q * 2 * CH)[r], st4[r, d, 3 + q, :],
                                               st4[r, d, q:q + 4:3, :], start=True, stop=True)
                            ins.then_inc(prods.sem, 1)
                            for q, r in each():
                                e.matmul(bank(d, 1, CH, q * CH)[r], gs4[r, d, 0, q:q + 1].broadcast_to([64, CH]),
                                         K[r, K_CUM + d * CH:K_CUM + d * CH + CH], start=True, stop=True)
                                ins = e.matmul(bank(d, 1, CH, U3 + q * CH)[r], gs4[r, d, 2, q:q + 1].broadcast_to([64, CH]),
                                               K[r, K_ID64:K_ID64 + CH], start=True, stop=True)
                            ins.then_inc(rbs.sem, 1)
                            for q, r in each():
                                for w in range(2):
                                    ins = e.matmul(bank(d, 2, CH, w * U3 + q * CH)[r], st4[r, d, 3 + 3 * w + q, :],
                                                   K[r, K_ID64:K_ID64 + CH], start=True, stop=True)
                            ins.then_inc(tms.sem, 1)
                        for d in range(2):
                            await_(e, (xt0, at(xt0, d)))
                            for q, r in each():
                                ins = e.matmul(bank(d, 3, CH, q * CH)[r], XT[r, d, q, :], K[r, K_ID64:K_ID64 + CH],
                                               start=True, stop=True)
                            ins.then_inc(x0.sem, 1)
                        for m in range(1, LEVELS):
                            for d in range(2):
                                if m == 1:
                                    await_(e, (am, at(am, d, 0, 5)), (x0k, at(x0k, d)), (kqd, at(kqd, d)))
                                else:
                                    await_(e, (am, at(am, d, m - 1, 5)), (xup, at(xup, d, m - 2, 5)))
                                for q, r in each():
                                    ins = e.matmul(bank(d, 0, CH, q * CH)[r], AM[r, m - 1, d, q, :], XX[r, d, q, :],
                                                   start=True, stop=True)
                                ins.then_inc(t1.sem, 1)
                            for d in range(2):
                                await_(e, (t1k, at(t1k, d, m - 1, 5)))
                                for q, r in each():
                                    if m < LEVELS - 1:
                                        e.matmul(bank(d, 1, CH, q * CH)[r], XT[r, d, q, :], T1S[r, d, q, :],
                                                 start=True, stop=True)
                                    ins = e.matmul(bank(d, 1, CH, U3 + q * CH)[r], T1S[r, d, q, :], XT[r, d, q, :],
                                                   start=True, stop=True)
                                ins.then_inc(dx.sem, 1)
                        for d in range(2):
                            await_(e, (xup, at(xup, d, LEVELS - 2, 5)), (rvw, at(rvw, d)))
                            for q, r in each():
                                e.matmul(bank(d, 3, CH, q * CH)[r], XT[r, d, q, :], RV[r, d, q, :], start=True, stop=True)
                                ins = e.matmul(bank(d, 3, CH, U3 + q * CH)[r], RW[r, d, q, :], XT[r, d, q, :],
                                               start=True, stop=True)
                            ins.then_inc(uw.sem, 1)
                        for d in range(2):
                            await_(e, (uwk, at(uwk, d)))
                            for q, r in each():
                                ins = e.matmul(bank(d, 0, CH, q * CH)[r], UWb[r, d, 1, q, :], SS[r, d, q, :],
                                               start=True, stop=True)
                            ins.then_inc(ws.sem, 1)
                        for d in range(2):
                            await_(e, (dl, at(dl, d)), (qd, at(qd, d)))
                            for q, r in each():
                                ins = e.matmul(bank(d, 3, CH, q * CH)[r], KD[r, d, q, :], DL[r, d, q, :],
                                               start=True, stop=True)
                            ins.then_inc(ds_.sem, 1)
                            for q, r in each():
                                e.matmul(bank(d, 1, CH, q * CH)[r], SS[r, d, q, :], QD[r, d, q, :], start=True, stop=False)
                                ins = e.matmul(bank(d, 1, CH, q * CH)[r], DL[r, d, q, :], KQD[r, d, q, :],
                                               start=False, stop=True)
                            ins.then_inc(om.sem, 1)
                        e.wait_ge(snew.sem, at(snew, 1))
                        e.wait_ge(oadd.sem, at(oadd, 1))

            def act(e):
                for n, s0, _ in spans():
                    with e.Fori(0, n) as i:
                        s = i + s0

                        def at(r, d, j=0, per=1):
                            return r.at(s * (2 * per) + j * 2 + d + 1)

                        for d in range(2):
                            e.wait_ge(rbs.sem, at(rbs, d))
                            e.activation(EG[:, d], bank3(d, 1), ACT.Exp).then_inc(eg.sem, 1)
                        for d in range(2):
                            e.wait_ge(decin.sem, at(decin, d))
                            e.activation(DEC[:, d], DEC[:, d], ACT.Exp).then_inc(dec.sem, 1)
                        for d in range(2):
                            e.wait_ge(x0.sem, at(x0, d))
                            e.activation(XX[:, d], bank3(d, 3), ACT.Copy).then_inc(x0k.sem, 1)
                        for m in range(1, LEVELS):
                            for d in range(2):
                                e.wait_ge(t1.sem, at(t1, d, m - 1, 5))
                                e.activation(T1S[:, d], bank3(d, 0), ACT.Copy).then_inc(t1k.sem, 1)
                        for d in range(2):
                            e.wait_ge(uw.sem, at(uw, d))
                            e.activation(UWb[:, d].rearrange("p w q i -> p (w q i)"), bank(d, 3, 2 * U3), ACT.Copy)\
                                .then_inc(uwk.sem, 1)
                        e.wait_ge(om.sem, at(om, 1))
                        e.wait_ge(snew.sem, at(snew, 1))

            def dve(e):
                link = chain["dve"].link
                for n, s0, chunk in spans():
                    with e.Fori(0, n) as i:
                        chain["dve"].loop(i, 12)
                        s = i + s0

                        def at(r, d, j=0, per=1):
                            return r.at(s * (2 * per) + j * 2 + d + 1)

                        for d in range(2):
                            e.wait_ge(eg.sem, at(eg, d))
                            link(e, e.tensor_tensor(DEC[:, d], bank3(d, 1), const3(K_NEG + d * CH), ALU.add))
                            e.tensor_tensor(DEC[:, d], DEC[:, d], col(1, d), ALU.subtract).then_inc(decin.sem, 1)
                        for d in range(2):
                            e.wait_ge(tms.sem, at(tms, d))
                            link(e, e.tensor_tensor(RV[:, d], bank3(d, 2, U3), col(2, d), ALU.mult))
                            link(e, e.tensor_tensor(KD[:, d], bank3(d, 2), col(4, d), ALU.mult))
                            e.tensor_tensor(RW[:, d], bank3(d, 2), col(3, d), ALU.mult).then_inc(rvw.sem, 1)
                            link(e, e.tensor_tensor(SC[:, d], SS[:, d], col(5, d), ALU.mult))
                        for d in range(2):
                            kq = bank(d, 0, 2 * U3).rearrange("p (q w i) -> p w q i", q=PAIRS, w=2)
                            e.wait_ge(dec.sem, at(dec, d))
                            link(e, e.tensor_tensor(AT[:, d], kq[:, 1], DEC[:, d], ALU.mult))
                            e.tensor_tensor(KQD[:, d], kq[:, 0], DEC[:, d], ALU.mult).then_inc(kqd.sem, 1)
                            e.tensor_tensor(AT[:, d], bank3(d, 1, U3), AT[:, d], ALU.mult).then_inc(att.sem, 1)
                            e.wait_ge(att.sem, at(att, d))
                            link(e, e.tensor_tensor(T0[:, d], AT[:, d], const3(K_LEVEL + d * CH), ALU.mult))
                            e.tensor_tensor(XT[:, d], const3(K_ID64), T0[:, d], ALU.subtract).then_inc(xt0.sem, 1)
                        for m in range(1, LEVELS):
                            for d in range(2):
                                e.wait_ge(dx.sem, at(dx, d, m - 1, 5))
                                if m < LEVELS - 1:
                                    e.tensor_tensor(XX[:, d], XX[:, d], bank3(d, 1), ALU.subtract)
                                e.tensor_tensor(XT[:, d], XT[:, d], bank3(d, 1, U3), ALU.subtract).then_inc(xup.sem, 1)
                                e.wait_ge(xup.sem, at(xup, d, m - 1, 5))
                        for d in range(2):
                            e.wait_ge(ws.sem, at(ws, d))
                            e.tensor_tensor(DL[:, d], UWb[:, d, 0], bank3(d, 0), ALU.subtract).then_inc(dl.sem, 1)
                        for d in range(2):
                            e.wait_ge(om.sem, at(om, d))
                            e.tensor_tensor(SS[:, d], SC[:, d], bank3(d, 3), ALU.add).then_inc(snew.sem, 1)
                            oo = o3[:, :, bass.ds(chunk[d](i) * CH, CH)]
                            e.tensor_tensor(oo, oo, bank3(d, 1), ALU.add).then_inc(oadd.sem, 1)
                        e.wait_ge(snew.sem, at(snew, 1))
                        e.wait_ge(oadd.sem, at(oadd, 1))
                    chain["dve"].end(n)
            ph.parts = dict(pe=pe, act=act, dve=dve, pool=pool)

        def residual(e, i, u, m, g, which, last, dst=None):
            for t0, tn, v in [(0, SEQ, 0)] + ([] if last else [(SEQ, CTX, 1)]):
                x_ = X[:, bass.ds(m * T + t0, tn)] if not isinstance(m, int) else x3[:, m, t0:t0 + tn]
                gate = S[:, bass.ds((N_VEC + 2 * which + v) + m * 2, 1)]
                ins = e.scalar_tensor_tensor(x_ if dst is None else dst, ps[:, g * GROUP + t0:g * GROUP + t0 + tn],
                                             gate, x_, ALU.mult, ALU.add)
            return ins

        def phase_out(l, last):
            ph = Phase()
            n0 = tiles[0]
            tiles[0] += 8
            ph.ends.append((tile_done.sem, tiles[0]))
            back = ph.sig("x_back", 1, 16)
            added = ph.sig("x_added", 8)
            src = a["w_out"][l].rearrange("(k p) n -> p k n", p=P)
            mix = [o3[:, j] for j in range(3)] + [mla3[:, j] for j in range(3)] + [hy3[:, j] for j in range(2)]

            def rhs(kk, t0, tn):
                return mix[kk][:, t0:t0 + tn]

            def pool(e):
                e.dma_start(X[:, :], x_dram).then_inc(back.sem, 16)

            def sp(e):
                with e.Fori(0, 4) as i:
                    for u in range(2):
                        load_tile(e, tile(n0, i, u), src, i * 256 + u * P, DK, P)

            def pe(e):
                product(e, tile(n0, 0, 0), DK, P, rhs, last)
                product(e, tile(n0, 0, 1), DK, P, rhs, last)
                with e.Fori(1, 4) as i:
                    for u in range(2):
                        product(e, tile(n0, i, u), DK, P, rhs, last, (added, i * 2 + (u - 1)))

            def dve(e):
                e.wait_ge(back.sem, back.at(1))
                with e.Fori(0, 4) as i:
                    for u in range(2):
                        g, n, _ = tile(n0, i, u)
                        e.wait_ge(tile_done.sem, n + 1)
                        residual(e, i, u, i * 2 + u, g, 16, last).then_inc(added.sem, 1)
            ph.parts = dict(sp=sp, pe=pe, dve=dve, pool=pool)

        def phase_ffn_up(l, last):
            ph = Phase()
            n0 = tiles[0]
            assert n0 % 2 == 0 or True
            tiles[0] += 2 * FT
            ph.ends.append((tile_done.sem, tiles[0]))
            width = SEQ if last else T
            zeroed = ph.sig("pads_zeroed", 8)
            raw_ready = ph.sig("raw_ready", FT)
            conv_done = ph.sig("conv_done", FT)
            silu = ph.sig("silu_made", FT)
            act_made = ph.sig("hidden_made", FT)
            src = a["ffn_w_up"][l].rearrange("(k p) n -> p k n", p=P)
            cv = [region(X, 2 * RAW + s * T, T) for s in range(2)]
            sl = [region(X, 2 * RAW + (2 + s) * T, T) for s in range(2)]

            def pool(e):
                zero_pads(e, zeroed)

            def sp(e):
                with e.Fori(0, FT) as i:
                    load_tile(e, tile(n0, i, 0), src, i * P, DK, P)
                    load_tile(e, tile(n0, i, 1), src, i * P + D_FF, DK, P)

            def pe(e):
                product(e, tile(n0, 0, 0), DK, P, h_rhs, last)
                product(e, tile(n0, 0, 1), DK, P, h_rhs, last)
                with e.Fori(1, FT) as i:
                    product(e, tile(n0, i, 0), DK, P, h_rhs, last, (raw_ready, i))
                    product(e, tile(n0, i, 1), DK, P, h_rhs, last, (act_made, i))

            def act(e):
                e.wait_ge(zeroed.sem, zeroed.at(8))
                with e.Fori(0, FT // 2) as i:
                    for u in range(2):
                        j = i * 2 + u
                        g, n, _ = tile(n0, i, 2 * u, 4)
                        e.wait_ge(tile_done.sem, n + 1)
                        keep_raw(e, g, raws()[u], width, raw_ready)
                        e.wait_ge(conv_done.sem, conv_done.at(j + 1))
                        e.activation(sl[u][:, 0:width], cv[u][:, 0:width], ACT.Silu).then_inc(silu.sem, 1)

            def dve(e):
                e.wait_ge(zeroed.sem, zeroed.at(8))
                with e.Fori(0, FT // 2) as i:
                    chain["dve"].loop(i, 4)
                    for u in range(2):
                        j = i * 2 + u
                        e.wait_ge(raw_ready.sem, raw_ready.at(j + 1))
                        w = [S[:, bass.ds(j + (VCOL["ffn_conv_w"] + s * FT), 1)] for s in range(3)]
                        conv(e, raws()[u], w, S[:, bass.ds(j + VCOL["ffn_conv_b"], 1)], cv[u], width, conv_done)
                        e.wait_ge(silu.sem, silu.at(j + 1))
                        g, n, _ = tile(n0, i, 2 * u + 1, 4)
                        e.wait_ge(tile_done.sem, n + 1)
                        e.tensor_tensor(C[:, bass.ds(j * T, width)], sl[u][:, 0:width], group(g, width), ALU.mult)\
                            .then_inc(act_made.sem, 1)
                chain["dve"].end(FT // 2)
            ph.parts = dict(sp=sp, pe=pe, act=act, dve=dve, pool=pool)

        def phase_ffn_down(l, last):
            ph = Phase()
            loaded = [ph.sig("down_loaded_0", 4, 16), ph.sig("down_loaded_1", 4, 16)]
            done = ph.sig("down_done", 8)
            back = ph.sig("x_back", 1, 16)
            added = ph.sig("x_added", 8)
            ring = [region(H, s * FT * P, FT * P).rearrange("p (k n) -> p k n", k=FT) for s in range(2)]
            src = a["ffn_w_down"][l].rearrange("(k p) n -> p k n", p=P)
            c3 = C[:, :].rearrange("p (k t) -> p k t", k=FT)
            if last:
                turned = ph.sig("out_turned", 16)
                kept = ph.sig("out_kept", 16)
                stored = [ph.sig("out_stored_0", 4, 16), ph.sig("out_stored_1", 4, 16)]
            xo = [region(H, 2 * FT * P + s * SEQ, SEQ) for s in range(2)]
            xr = [region(H, 2 * FT * P + (2 + s) * SEQ, SEQ).rearrange("p (t f) -> p t f", f=P) for s in range(2)]

            def pool(e):
                e.dma_start(X[:, :], x_dram).then_inc(back.sem, 16)

            def sp(e):
                for u in range(2):
                    e.dma_start(ring[u], src[:, :, u * P:u * P + P]).then_inc(loaded[u].sem, 16)
                with e.Fori(1, 4) as i:
                    for u in range(2):
                        c = e.snap(i * 256 + u * P)
                        e.wait_ge(done.sem, done.at(i * 2 + (u - 1)))
                        e.dma_start(ring[u], src[:, :, bass.ds(c, P)]).then_inc(loaded[u].sem, 16)

            def one(e, i, u, free):
                e.wait_ge(loaded[u].sem, loaded[u].at(i + 1))
                if free:
                    e.wait_ge(added.sem, added.at(i * 2 + (u - 1)))
                for b, (t0, tn) in enumerate(tok(last)):
                    for k in range(FT):
                        ins = e.matmul(ps[:, u * GROUP + b * BANK:u * GROUP + b * BANK + tn], ring[u][:, k, :],
                                       c3[:, k, t0:t0 + tn], start=(k == 0), stop=(k == FT - 1))
                ins.then_inc(done.sem, 1)

            def turn(e, j, u):
                e.wait_ge(added.sem, added.at(j + 1))
                for half in range(2):
                    if not (isinstance(j, int) and j == 0):
                        e.wait_ge(kept.sem, kept.at(j * 2 + (half - 1)))
                    for q in range(4):
                        b = 4 * half + q
                        ins = e.transpose(ps[:, (6 + half) * BANK + q * P:(6 + half) * BANK + q * P + P],
                                          xo[u][:, b * P:b * P + P], ident)
                    ins.then_inc(turned.sem, 1)

            def pe(e):
                one(e, 0, 0, False)
                one(e, 0, 1, False)
                if last:
                    turn(e, 0, 0)
                with e.Fori(1, 4) as i:
                    one(e, i, 0, True)
                    if last:
                        turn(e, i * 2 - 1, 1)
                    one(e, i, 1, True)
                    if last:
                        turn(e, i * 2, 0)
                if last:
                    turn(e, 7, 1)

            def dve(e):
                e.wait_ge(back.sem, back.at(1))
                with e.Fori(0, 4) as i:
                    for u in range(2):
                        j = i * 2 + u
                        e.wait_ge(done.sem, done.at(j + 1))
                        if last:
                            e.wait_ge(turned.sem, turned_before(j))
                        residual(e, i, u, j, u, 40, last, xo[u] if last else None).then_inc(added.sem, 1)

            def turned_before(j):
                return turned.at(j * 2 - 2)

            def dve_last(e):
                e.wait_ge(back.sem, back.at(1))
                for u in range(2):
                    e.wait_ge(done.sem, done.at(u + 1))
                    residual(e, 0, u, u, u, 40, True, xo[u]).then_inc(added.sem, 1)
                with e.Fori(1, 4) as i:
                    for u in range(2):
                        j = i * 2 + u
                        e.wait_ge(done.sem, done.at(j + 1))
                        e.wait_ge(turned.sem, turned.at(j * 2 - 2))
                        residual(e, i, u, j, u, 40, True, xo[u]).then_inc(added.sem, 1)

            def act(e):
                o_ = out[0].rearrange("(t p) f -> p t f", p=P)

                def one_out(i, u, again):
                    j = i * 2 + u
                    if again:
                        e.wait_ge(stored[u].sem, stored[u].at(i))
                    for half in range(2):
                        e.wait_ge(turned.sem, turned.at(j * 2 + half + 1))
                        e.activation(xr[u][:, 4 * half:4 * half + 4, :],
                                     ps[:, (6 + half) * BANK:(7 + half) * BANK].rearrange("p (t f) -> p t f", f=P),
                                     ACT.Copy).then_inc(kept.sem, 1)
                    e.wait_ge(kept.sem, kept.at(j * 2 + 2))
                    dst = o_[:, :, bass.ds(j * P, P)] if not isinstance(j, int) else o_[:, :, j * P:j * P + P]
                    e.dma_start(dst, xr[u]).then_inc(stored[u].sem, 16)

                one_out(0, 0, False)
                one_out(0, 1, False)
                with e.Fori(1, 4) as i:
                    one_out(i, 0, True)
                    one_out(i, 1, True)
                for u in range(2):
                    e.wait_ge(stored[u].sem, stored[u].at(4))
            ph.parts = dict(sp=sp, pe=pe, dve=dve_last if last else dve, pool=pool)
            if last:
                ph.parts["act"] = act

        phase_input()
        for l in range(DEPTH):
            last = l == DEPTH - 1
            phase_modulation(l)
            phase_norm(l, 0, False)
            phase_hyena_in(l)
            phase_hyena_filter(l, SEQ, 0)
            phase_hyena_conv(l, SEQ, 0)
            if not last:
                phase_hyena_filter(l, CTX, SEQ)
                phase_hyena_conv(l, CTX, SEQ)
            phase_mla_in(l)
            phase_mla_norm(l)
            phase_mla_heads(l, last)
            phase_gdn_in(l)
            phase_head_norm(l, "qk")
            phase_gates(l)
            phase_scan(l)
            phase_head_norm(l, "out")
            phase_out(l, last)
            phase_norm(l, 1, last)
            phase_ffn_up(l, last)
            phase_ffn_down(l, last)
        block = ctx.enter_context(nc.Block())

        def run(eng, name):
            for k, ph in enumerate(every):
                if name in ph.parts:
                    settle(eng, k)
                    ph.parts[name](eng)

        @block.sync
        def _(e):
            run(e, "sp")

        @block.tensor
        def _(e):
            run(e, "pe")

        @block.scalar
        def _(e):
            run(e, "act")

        @block.vector
        def _(e):
            run(e, "dve")

        @block.gpsimd
        def _(e):
            run(e, "pool")


_INS = ["x", "c", "ctx", "c_ctx", "ada_w", "ada_b", "mix_norm_g", "w_in", "gdn_conv_w", "gdn_a_log",
        "gdn_dt_bias", "gdn_norm_g", "mla_q_norm_g", "mla_w_uq", "mla_kv_norm_g", "mla_w_ukv",
        "mla_q_head_g", "mla_k_head_g", "hy_conv_w", "hy_conv_b", "hy_w1", "hy_b1", "hy_w2", "hy_b2",
        "hy_w3", "hy_b3", "hy_d", "w_out", "ffn_norm_g", "ffn_w_up", "ffn_conv_w", "ffn_conv_b",
        "ffn_w_down"]


def kernel(**inputs):
    import concourse.bacc as _bacc
    from concourse.bass_utils import run_bass_kernel_spmd as _run

    nc = _bacc.Bacc("TRN2", target_bir_lowering=False, num_devices=1)
    arrays = {n: np.ascontiguousarray(inputs[n]) for n in _INS}
    arrays.update(tables())
    aps = {n: nc.dram_tensor("in_" + n, v.shape, mybir.dt.from_np(v.dtype), kind="ExternalInput").ap()
           for n, v in arrays.items()}
    out = nc.dram_tensor("out_0", (1, SEQ, D), F32, kind="ExternalOutput").ap()
    build(nc, aps, out)
    r = _run(nc, [{"in_" + n: v for n, v in arrays.items()}], core_ids=[0])
    return r.results[0]["out_0"]
```

```python
from contextlib import ExitStack

import numpy as np

import concourse.bass as bass
from concourse import mybir

F32 = mybir.dt.float32
BF16 = mybir.dt.bfloat16
ACT = mybir.ActivationFunctionType
ALU = mybir.AluOpType
AX = mybir.AxisListType

P = 128
D = 1024
DK = D // P
SEQ, CTX = 1024, 256
T = SEQ + CTX
DEPTH = 2
EPS = 1e-6
GRID_W = 64

HEADS = 6
PAIRS = 3
CH = 64
GDN_QKV = 1152
GDN_W = 384
N_CHUNK = T // CH
LAT_CHUNKS, CTX_CHUNKS = SEQ // CH, CTX // CH

QR, KVR, NOPE, ROPE, VD = 256, 128, 64, 32, 64
QK = NOPE + ROPE
HY = 256
HY_EMB, HY_HID = 33, 64
D_FF = 2816
FT = D_FF // P
GDN_IN = GDN_QKV + GDN_W + 4 * HEADS
MLA_COL = GDN_IN
HY_COL = GDN_IN + QR + KVR + ROPE
P_IN = HY_COL + 3 * HY

HALVES = ((0, 0), (0, 1), (1, 0))

LEVELS = 6
NEG = -1e30
TWO_PI = 2 * np.pi
RAW = T + 4
RAW_AT = ((0, SEQ, 0), (SEQ, CTX, SEQ + 2))
GROUP = 1536
BANK = 512

K_ID = 0
K_BLOCK = K_ID + P
K_ONES = K_BLOCK + P
K_CUM = K_ONES + P
K_LEVEL = K_CUM + 2 * CH
K_NEG = K_LEVEL + LEVELS * 2 * CH
K_ROT = K_NEG + 2 * CH
K_ID64 = K_ROT + QK
K_T0 = K_ID64 + CH
K_TN = K_T0 + 1
K_DELTA = K_TN + SEQ // P + CTX // P
K_EPS = K_DELTA + HY
K_N = K_EPS + 1

VEC_A = (("ada_b", 48), ("mix_norm_g", 8), ("ffn_norm_g", 8), ("gdn_conv_w", 27), ("hy_conv_w", 18),
         ("hy_conv_b", 6), ("hy_d", 2), ("mla_q_norm_g", 2), ("mla_kv_norm_g", 1))
VEC_B = (("ffn_conv_w", 66), ("ffn_conv_b", 22), ("c", 8), ("c_ctx", 8))
VCOL, _at = {}, 0
for _n, _k in VEC_A + VEC_B:
    VCOL[_n] = _at
    _at += _k
N_VEC = _at
N_ROWS = len(VEC_A) + len(VEC_B) + 6 + 4
N_VEC_A = sum(k for _, k in VEC_A)
N_VEC_B = sum(k for _, k in VEC_B)
SMALL = N_VEC + 96 + 2 * 2 * 8 + 12 + 8


def tables():
    k = np.zeros((P, K_N), np.float32)
    k[:, K_ID:K_ID + P] = np.eye(P)
    for h in range(2):
        k[h * 64:h * 64 + 64, K_BLOCK + h * 64:K_BLOCK + h * 64 + 64] = 1
    k[:, K_ONES:K_ONES + P] = 1
    j, i = np.meshgrid(np.arange(CH), np.arange(CH), indexing="ij")
    for d in range(2):
        before = (i >= j) if d == 0 else (i <= j)
        k[:, K_CUM + d * CH:K_CUM + d * CH + CH] = np.tile(before, (2, 1))
        k[:, K_NEG + d * CH:K_NEG + d * CH + CH] = np.tile(np.where(before, 0, NEG), (2, 1))
        for l in range(LEVELS):
            b = 1 << l
            same = (i // (2 * b)) == (j // (2 * b))
            first, second = (j, i) if d == 0 else (i, j)
            m = same & ((first // b) % 2 == 0) & ((second // b) % 2 == 1)
            c = K_LEVEL + (l * 2 + d) * CH
            k[:, c:c + CH] = np.tile(m, (2, 1))
    half = ROPE // 2
    for r in range(half):
        k[NOPE + half + r, K_ROT + NOPE + r] = -1
        k[NOPE + r, K_ROT + NOPE + half + r] = 1
    k[:, K_ID64:K_ID64 + CH] = np.tile(np.eye(CH), (2, 1))
    k[:, K_T0] = 1
    k[0, K_T0] = 0
    lo, hi = np.log(1e-2) / 1.5, np.log(1e-2) / 0.3
    k[:, K_DELTA:K_DELTA + HY] = np.abs(np.linspace(lo, hi, HY, dtype=np.float32))
    k[:, K_EPS] = EPS
    out = {"k_table": k}
    at = 0
    for name, length in (("lat", SEQ), ("ctx", CTX)):
        t = np.arange(length, dtype=np.float32)
        tn = t / np.float32(max(length - 1, 1))
        k[:, K_TN + at:K_TN + at + length // P] = -tn.reshape(-1, P).T
        at += length // P
        bands = np.linspace(1e-4, 15, 16, dtype=np.float32)
        ang = (np.float32(2.0 * np.pi) * t[:, None] * bands[None, :] / np.float32(length)).astype(np.float32)
        z = np.concatenate([tn[:, None], np.cos(ang), np.sin(ang)], axis=-1)
        out["k_z_" + name] = np.ascontiguousarray(z.T.astype(np.float32))
        th = np.pi * np.outer(np.arange(length), 2 * np.arange(length) + 1) / (2 * length)
        cs = np.stack([np.cos(th), np.sin(th)])
        out["k_dft_" + name] = cs.astype(np.float32)
        out["k_idft_" + name] = np.ascontiguousarray((cs / length).transpose(0, 2, 1).astype(np.float32))
    rows = SEQ // GRID_W
    row = np.repeat(np.arange(rows, dtype=np.float32), GRID_W)
    col = np.tile(np.arange(GRID_W, dtype=np.float32), rows)
    inv = (np.float32(10000.0) ** (-np.arange(0, 16, 2, dtype=np.float32) / 16)).astype(np.float32)
    ang = np.concatenate([row[:, None] * inv, col[:, None] * inv], axis=-1).T
    rope = np.zeros((2, QK, SEQ), np.float32)
    rope[0, :NOPE] = 1
    rope[0, NOPE:] = np.tile(np.cos(ang), (2, 1))
    rope[1, NOPE:] = np.tile(np.sin(ang), (2, 1))
    out["k_rope"] = rope
    return out


class Signal:

    def __init__(self, sem):
        self.sem, self.total = sem, 0


class Ref:

    def __init__(self, signal, n, unit):
        self.sem, self.base, self.unit = signal.sem, signal.total, unit
        signal.total += n * unit
        self.end = signal.total

    def at(self, k):
        return k * self.unit + self.base


def build(nc, a, out):
    with ExitStack() as ctx:
        def sb(name, n):
            return ctx.enter_context(nc.sbuf_tensor(name, [P, n], F32))

        X = sb("X", DK * T)
        H = sb("H", DK * T)
        C = sb("C", FT * T)
        W = sb("W", 2 * DK * P)
        K = sb("K", K_N)
        S = sb("S", SMALL)
        ps = ctx.enter_context(nc.psum_tensor("ps", [P, 8 * BANK], F32))
        x_dram = nc.dram_tensor("x_stream", [P, DK * T], F32, kind="Internal").ap()

        signals = {}
        every = []

        def signal(name):
            if name not in signals:
                signals[name] = Signal(ctx.enter_context(nc.semaphore(name)))
            return signals[name]

        class Phase:

            def __init__(self):
                self.ends = []
                self.parts = {}
                every.append(self)

            def sig(self, name, n, unit=1):
                r = Ref(signal(name), n, unit)
                self.ends.append((r.sem, r.end))
                return r

        tile_done = signal("tile_done")
        w_loaded = [signal("w_loaded_0"), signal("w_loaded_1")]
        tiles = [0]

        x3 = X[:, :].rearrange("p (k t) -> p k t", k=DK)
        h3 = H[:, :].rearrange("p (k t) -> p k t", k=DK)
        w3 = W[:, :].rearrange("p (s k n) -> p s k n", s=2, k=DK)
        ident = K[:, K_ID:K_ID + P]
        eps = K[:, K_EPS:K_EPS + 1]
        mod = S[:, N_VEC:N_VEC + 96].rearrange("p (m v) -> p m v", v=2)
        gain = S[:, N_VEC + 96:N_VEC + 128].rearrange("p (w k v) -> p w k v", w=2, v=2)
        AL = S[:, N_VEC + 128:N_VEC + 134]
        DT = S[:, N_VEC + 134:N_VEC + 140]
        gdn_g = S[:, N_VEC + 140:N_VEC + 141]
        q_g = S[0:QK, N_VEC + 141:N_VEC + 142]
        k_g = S[0:QK, N_VEC + 142:N_VEC + 143]
        b1 = S[0:HY_HID, N_VEC + 143:N_VEC + 144]
        b2 = S[0:HY_HID, N_VEC + 144:N_VEC + 145]
        inv_norm = S[:, N_VEC + 145:N_VEC + 147]

        def vec(name, j=0):
            c = VCOL[name] + j
            return S[:, c:c + 1]

        def region(t, at, n):
            return t[:, at:at + n]

        class Chain:

            def __init__(self, name):
                self.s = signal(name)
                self.base, self.c, self.i, self.per, self.first = 0, 0, None, 0, 0

            def link(self, eng, ins):
                self.c += 1
                ins.then_inc(self.s.sem, 1)
                v = self.base + self.c if self.i is None else self.i * self.per + (self.base + self.c)
                eng.wait_ge(self.s.sem, v)

            def loop(self, i, per):
                self.base, self.c = self.base + self.c, 0
                self.i, self.per = i, per

            def loop_from(self, i, per, first):
                self.base, self.c = self.base + self.c - first * per, 0
                self.i, self.per, self.first = i, per, first

            def end(self, times):
                assert self.c == self.per, (self.c, self.per)
                self.base, self.c, self.i = self.base + self.per * (times + self.first), 0, None
                self.first = 0

        hb, cb = H[:, :].bitcast(BF16), C[:, :].bitcast(BF16)

        def halves(t, at, n):
            b = t[:, at:at + n].bitcast(BF16)
            return b[:, 0:n], b[:, n:2 * n]

        def split_ring(t, at):
            return [[x.rearrange("p (k n) -> p k n", k=DK) for x in halves(t, at + s * D, D)] for s in range(2)]

        chain = {e: Chain(e + "_own") for e in ("dve", "act", "pool")}

        def tok(last):
            return [(0, BANK), (BANK, BANK)] + ([] if last else [(SEQ, CTX)])

        def group(g, n, lo=0, hi=P):
            return ps[lo:hi, g * GROUP:g * GROUP + n]

        def tile(base, i=0, u=0, per=2):
            b = base + u
            return b % 2, i * per + b, i * (per // 2) + b // 2

        def load_tile(sp, num, src, col, k, width, split=None, j=0):
            slot, n, _ = num
            c = col if isinstance(col, int) else sp.snap(col)
            if split is not None and not (isinstance(j, int) and j < 2):
                sp.wait_ge(split.sem, split.at(j - 1))
            elif split is None and not (isinstance(n, int) and n < 2):
                sp.wait_ge(tile_done.sem, n - 1)
            sp.dma_start(w3[:, slot, 0:k, 0:width], src[:, :, bass.ds(c, width)]).then_inc(w_loaded[slot].sem, 16)

        def copy_waits(pool, *waits):
            counts = [v if isinstance(v, int) else pool.to_reg(v) for _, v in waits]
            pool.wait_ge(signal("table_loaded").sem, 16)
            for (sem, _), v in zip(waits, counts):
                pool.wait_ge(sem, v)

        def split_tile(pool, num, j, k, width, ring, split):
            g, n, loads = num
            if isinstance(j, int) and j < 2:
                copy_waits(pool, (w_loaded[g].sem, loads * 16 + 16))
            else:
                copy_waits(pool, (w_loaded[g].sem, loads * 16 + 16), (tile_done.sem, n - 1))
            hi, lo = (x[:, 0:k, 0:width] for x in ring[g])
            chain["pool"].link(pool, pool.tensor_copy(hi, w3[:, g, 0:k, 0:width]))
            pool.tensor_tensor(lo, w3[:, g, 0:k, 0:width], hi, ALU.subtract).then_inc(split.sem, 1)

        def whole_product(pe, num, k, width, rhs, last, free=None, lo=0):
            g, n, loads = num
            pe.wait_ge(w_loaded[g].sem, loads * 16 + 16)
            if free is not None:
                pe.wait_ge(free[0].sem, free[0].at(free[1]))
            for b, (t0, tn) in enumerate(tok(last)):
                for kk in range(k):
                    ins = pe.matmul(ps[lo:lo + width, g * GROUP + b * BANK:g * GROUP + b * BANK + tn],
                                    w3[:, g, kk, 0:width], rhs(kk, t0, tn), start=(kk == 0), stop=(kk == k - 1))
            ins.then_inc(tile_done.sem, 1)

        def whole_h(kk, t0, tn):
            return h3[:, kk, t0:t0 + tn]

        def product(pe, num, j, k, width, rhs, last, ring, split, free=None, lo=0):
            g, n, _ = num
            pe.wait_ge(split.sem, split.at(j + 1))
            if free is not None:
                pe.wait_ge(free[0].sem, free[0].at(free[1]))
            for b, (t0, tn) in enumerate(tok(last)):
                for kk in range(k):
                    for q, (w_, r_) in enumerate(HALVES):
                        ins = pe.matmul(ps[lo:lo + width, g * GROUP + b * BANK:g * GROUP + b * BANK + tn],
                                        ring[g][w_][:, kk, 0:width], rhs(kk, t0, tn, r_),
                                        start=(kk == 0 and q == 0), stop=(kk == k - 1 and q == 2))
            ins.then_inc(tile_done.sem, 1)

        def h_rhs(kk, t0, tn, half):
            c = (2 * kk + half) * T + t0
            return hb[:, c:c + tn]

        x_ring = split_ring(X, 8 * D)

        def keep_raw(act, g, raw, width, ready):
            for t0, tn, r0 in RAW_AT:
                if t0 < width:
                    ins = act.activation(raw[:, r0 + 1:r0 + 1 + tn], ps[:, g * GROUP + t0:g * GROUP + t0 + tn], ACT.Copy)
            ins.then_inc(ready.sem, 1)

        def conv(dve, raw, w, bias, dst, width, done):
            for step in range(3):
                for t0, tn, r0 in RAW_AT:
                    if t0 >= width:
                        continue
                    src = raw[:, r0 + step:r0 + step + tn]
                    o = dst[:, t0:t0 + tn]
                    if step == 0 and bias is None:
                        ins = dve.tensor_scalar(o, src, w[0], None, ALU.mult)
                    elif step == 0:
                        ins = dve.tensor_scalar(o, src, w[0], bias, ALU.mult, ALU.add)
                    else:
                        ins = dve.scalar_tensor_tensor(o, src, w[step], o, ALU.mult, ALU.add)
                if step < 2:
                    chain["dve"].link(dve, ins)
            ins.then_inc(done.sem, 1)

        def settle(eng, k):
            if k:
                for sem, end in every[k - 1].ends:
                    eng.wait_ge(sem, end)

        def phase_input():
            ph = Phase()
            table = ph.sig("table_loaded", 1, 16)
            rows = ph.sig("rows_loaded", 10, 16)
            turned = ph.sig("rows_turned", 20)
            kept = ph.sig("rows_kept", 20)
            ring = [region(C, s * D, D) for s in range(10)]

            def sp(e):
                e.dma_start(K[:, :], a["k_table"]).then_inc(table.sem, 16)
                for n in range(10):
                    src = a["x"][0, n * P:n * P + P, :] if n < 8 else a["ctx"][0, (n - 8) * P:(n - 7) * P, :]
                    if n:
                        e.wait_ge(rows.sem, rows.at(n))
                    e.dma_start(ring[n], src).then_inc(rows.sem, 16)

            def pe(e):
                e.wait_ge(table.sem, table.at(1))
                for n in range(10):
                    e.wait_ge(rows.sem, rows.at(n + 1))
                    for half in range(2):
                        c = 2 * n + half
                        if c >= 4:
                            e.wait_ge(kept.sem, kept.at(c - 3))
                        for q in range(4):
                            k = half * 4 + q
                            ins = e.transpose(ps[:, (c % 4) * BANK + q * P:(c % 4) * BANK + q * P + P],
                                              ring[n][:, k * P:k * P + P], ident)
                        ins.then_inc(turned.sem, 1)

            def act(e):
                for n in range(10):
                    for half in range(2):
                        c = 2 * n + half
                        e.wait_ge(turned.sem, turned.at(c + 1))
                        e.activation(x3[:, half * 4:half * 4 + 4, n * P:n * P + P],
                                     ps[:, (c % 4) * BANK:(c % 4 + 1) * BANK].rearrange("p (k t) -> p k t", k=4),
                                     ACT.Copy).then_inc(kept.sem, 1)
            ph.parts = dict(sp=sp, pe=pe, act=act)

        def phase_modulation(l):
            ph = Phase()
            NC = 12
            rows = ph.sig("vectors_loaded", N_ROWS, 16)
            turned = ph.sig("vectors_turned", 1)
            kept = ph.sig("vectors_kept", 2)
            silu = ph.sig("c_silu", 1)
            loaded = [ph.sig("ada_loaded_0", NC // 2, 16), ph.sig("ada_loaded_1", NC // 2, 16)]
            used = ph.sig("ada_used", NC)
            moved = ph.sig("mod_made", 3)
            rows_a = region(C, 0, P)
            rows_b = region(C, P, P)
            cT = S[:, VCOL["c"]:VCOL["c"] + 16].rearrange("p (v k) -> p k v", v=2)
            cS = region(C, 2 * P + 16, 16).rearrange("p (k v) -> p k v", v=2)
            ring = [region(C, 1024 + s * 4096, 4096).rearrange("p (k n) -> p k n", k=DK) for s in range(2)]

            def pool(e):
                at = 0
                for dst, names in ((rows_a, VEC_A), (rows_b, VEC_B)):
                    at = 0
                    for name, k in names:
                        src = a[name] if name == "c_ctx" else a[name][0 if name == "c" else l]
                        src = src.rearrange("w (k p) -> (w k) p", p=P) if len(src.shape) == 2 \
                            else src.rearrange("(k p) -> k p", p=P)
                        e.dma_start(dst[at:at + k, :], src).then_inc(rows.sem, 16)
                        at += k
                for h in range(2):
                    r = slice(h * 64, h * 64 + 64)
                    for dst, name in ((AL, "gdn_a_log"), (DT, "gdn_dt_bias")):
                        src = a[name][l].rearrange("d (p h) -> h d p", h=2)[h:h + 1]
                        e.dma_start(dst[r, :].rearrange("q (d p) -> q d p", d=2),
                                    src.broadcast_to([64, 2, PAIRS]), allow_slow_non_contiguous=True)\
                            .then_inc(rows.sem, 16)
                    e.dma_start(gdn_g[r, :], a["gdn_norm_g"][l].rearrange("(p o) -> p o", o=1)).then_inc(rows.sem, 16)
                for dst, name in ((q_g, "mla_q_head_g"), (k_g, "mla_k_head_g")):
                    e.dma_start(dst, a[name][l].rearrange("(p o) -> p o", o=1)).then_inc(rows.sem, 16)
                for dst, name in ((b1, "hy_b1"), (b2, "hy_b2")):
                    e.dma_start(dst, a[name][l].rearrange("(p o) -> p o", o=1)).then_inc(rows.sem, 16)

            def sp(e):
                w = a["ada_w"][l].rearrange("(k p) n -> p k n", p=P)
                for n in range(NC):
                    if n >= 2:
                        e.wait_ge(used.sem, used.at(n - 1))
                    e.dma_start(ring[n % 2], w[:, :, n * 512:n * 512 + 512]).then_inc(loaded[n % 2].sem, 16)

            def pe(e):
                e.wait_ge(rows.sem, rows.at(N_ROWS))
                e.transpose(ps[:, 0:N_VEC_A], rows_a[0:N_VEC_A, :], ident[0:N_VEC_A, 0:N_VEC_A])
                e.transpose(ps[:, P:P + N_VEC_B], rows_b[0:N_VEC_B, :], ident[0:N_VEC_B, 0:N_VEC_B])\
                    .then_inc(turned.sem, 1)
                e.wait_ge(silu.sem, silu.at(1))
                for n in range(NC):
                    e.wait_ge(loaded[n % 2].sem, loaded[n % 2].at(n // 2 + 1))
                    for q in range(4):
                        c = 4 * n + q
                        for k in range(DK):
                            ins = e.matmul(ps[:, BANK + 2 * c:BANK + 2 * c + 2], ring[n % 2][:, k, q * P:q * P + P],
                                           cS[:, k, :], start=(k == 0), stop=(k == DK - 1))
                    ins.then_inc(used.sem, 1)

            def act(e):
                e.wait_ge(kept.sem, kept.at(2))
                e.activation(cS, cT, ACT.Silu).then_inc(silu.sem, 1)

            def dve(e):
                e.wait_ge(turned.sem, turned.at(1))
                e.tensor_copy(S[:, 0:N_VEC_A], ps[:, 0:N_VEC_A]).then_inc(kept.sem, 1)
                e.tensor_copy(S[:, N_VEC_A:N_VEC], ps[:, P:P + N_VEC_B]).then_inc(kept.sem, 1)
                e.wait_ge(kept.sem, kept.at(2))
                e.wait_ge(used.sem, used.at(NC))
                e.tensor_tensor(mod, ps[:, BANK:BANK + 96].rearrange("p (m v) -> p m v", v=2),
                                S[:, 0:48].unsqueeze(2).broadcast_to([P, 48, 2]), ALU.add).then_inc(moved.sem, 1)
                e.wait_ge(moved.sem, moved.at(1))
                for w, (name, sc) in enumerate((("mix_norm_g", 8), ("ffn_norm_g", 32))):
                    g = S[:, VCOL[name]:VCOL[name] + 8]
                    e.scalar_tensor_tensor(gain[:, w], mod[:, sc:sc + 8, :], 1.0,
                                           g.unsqueeze(2).broadcast_to([P, 8, 2]), ALU.add, ALU.mult)\
                        .then_inc(moved.sem, 1)
            ph.parts = dict(sp=sp, pe=pe, act=act, dve=dve, pool=pool)

        def phase_norm_mix(l):
            ph = Phase()
            which, last = 0, False
            width = SEQ if last else T
            squared = ph.sig("squared", DK)
            summed = ph.sig("squares_summed", DK)
            root = ph.sig("root_made", 1)
            inv = ph.sig("rstd_made", 1)
            scaled = ph.sig("h_scaled", DK)
            made = ph.sig("h_made", DK * (1 if last else 2))
            saved = ph.sig("x_saved", 1, 16)
            sq = [region(C, 0, T), region(C, T, T)]
            rt, rs = region(C, 2 * T, T), region(C, 3 * T, T)
            segs = [(0, SEQ, 0)] + ([] if last else [(SEQ, CTX, 1)])
            shift = 0 if which == 0 else 24

            def pool(e):
                e.dma_start(x_dram, X[:, :]).then_inc(saved.sem, 16)

            def act(e):
                for k in range(DK):
                    if k >= 2:
                        e.wait_ge(summed.sem, summed.at(k - 1))
                    e.activation(sq[k % 2][:, 0:width], x3[:, k, 0:width], ACT.Square).then_inc(squared.sem, 1)
                e.wait_ge(summed.sem, summed.at(DK))
                e.activation(rt[:, 0:width], group(0, width), ACT.Sqrt, bias=eps, scale=1.0 / D).then_inc(root.sem, 1)
                for k in range(DK):
                    e.wait_ge(scaled.sem, scaled.at(k + 1))
                    for t0, tn, v in segs:
                        e.activation(h3[:, k, t0:t0 + tn], h3[:, k, t0:t0 + tn], ACT.Identity,
                                     bias=mod[:, shift + k, v:v + 1]).then_inc(made.sem, 1)

            def pe(e):
                for k in range(DK):
                    e.wait_ge(squared.sem, squared.at(k + 1))
                    for b, (t0, tn) in enumerate(tok(last)):
                        ins = e.matmul(ps[:, b * BANK:b * BANK + tn], K[:, K_ONES:K_ONES + P], sq[k % 2][:, t0:t0 + tn],
                                       start=(k == 0), stop=(k == DK - 1))
                    ins.then_inc(summed.sem, 1)

            def dve(e):
                e.wait_ge(root.sem, root.at(1))
                e.reciprocal(rs[:, 0:width], rt[:, 0:width]).then_inc(inv.sem, 1)
                e.wait_ge(inv.sem, inv.at(1))
                for k in range(DK):
                    for t0, tn, v in segs:
                        ins = e.scalar_tensor_tensor(h3[:, k, t0:t0 + tn], x3[:, k, t0:t0 + tn],
                                                     gain[:, which, k, v:v + 1], rs[:, t0:t0 + tn], ALU.mult, ALU.mult)
                    ins.then_inc(scaled.sem, 1)
            ph.parts = dict(pe=pe, act=act, dve=dve, pool=pool)

        def phase_norm_ffn(l, last):
            ph = Phase()
            which = 1
            width = SEQ if last else T
            squared = ph.sig("squared", DK)
            summed = ph.sig("squares_summed", DK)
            root = ph.sig("root_made", 1)
            inv = ph.sig("rstd_made", 1)
            scaled = ph.sig("h_scaled", DK)
            made = ph.sig("h_high_made", DK)
            lows = ph.sig("h_low_made", DK)
            saved = ph.sig("x_saved", 1, 16)
            sq = [region(C, 0, T), region(C, T, T)]
            rt, rs = region(C, 2 * T, T), region(C, 3 * T, T)
            tmp = [region(C, (4 + s) * T, T) for s in range(3)]
            segs = [(0, SEQ, 0)] + ([] if last else [(SEQ, CTX, 1)])
            shift = 0 if which == 0 else 24

            def pool(e):
                e.dma_start(x_dram, X[:, :]).then_inc(saved.sem, 16)

            def act(e):
                for k in range(DK):
                    if k >= 2:
                        e.wait_ge(summed.sem, summed.at(k - 1))
                    e.activation(sq[k % 2][:, 0:width], x3[:, k, 0:width], ACT.Square).then_inc(squared.sem, 1)
                e.wait_ge(summed.sem, summed.at(DK))
                e.activation(rt[:, 0:width], group(0, width), ACT.Sqrt, bias=eps, scale=1.0 / D).then_inc(root.sem, 1)
                for k in range(DK):
                    e.wait_ge(scaled.sem, scaled.at(k + 1))
                    for t0, tn, v in segs:
                        ins = e.activation(h_rhs(k, t0, tn, 0), tmp[k % 3][:, t0:t0 + tn], ACT.Identity,
                                           bias=mod[:, shift + k, v:v + 1])
                    ins.then_inc(made.sem, 1)

            def pe(e):
                for k in range(DK):
                    e.wait_ge(squared.sem, squared.at(k + 1))
                    for b, (t0, tn) in enumerate(tok(last)):
                        ins = e.matmul(ps[:, b * BANK:b * BANK + tn], K[:, K_ONES:K_ONES + P], sq[k % 2][:, t0:t0 + tn],
                                       start=(k == 0), stop=(k == DK - 1))
                    ins.then_inc(summed.sem, 1)

            def dve(e):
                e.wait_ge(root.sem, root.at(1))
                e.reciprocal(rs[:, 0:width], rt[:, 0:width]).then_inc(inv.sem, 1)
                e.wait_ge(inv.sem, inv.at(1))
                for k in range(DK + 1):
                    if k < DK:
                        if k >= 3:
                            e.wait_ge(lows.sem, lows.at(k - 2))
                        for t0, tn, v in segs:
                            ins = e.scalar_tensor_tensor(tmp[k % 3][:, t0:t0 + tn], x3[:, k, t0:t0 + tn],
                                                         gain[:, which, k, v:v + 1], rs[:, t0:t0 + tn], ALU.mult, ALU.mult)
                        ins.then_inc(scaled.sem, 1)
                    if k:
                        e.wait_ge(scaled.sem, scaled.at(k))
                        e.wait_ge(made.sem, made.at(k))
                        for t0, tn, v in segs:
                            ins = e.scalar_tensor_tensor(h_rhs(k - 1, t0, tn, 1), tmp[(k - 1) % 3][:, t0:t0 + tn],
                                                         mod[:, shift + k - 1, v:v + 1], h_rhs(k - 1, t0, tn, 0),
                                                         ALU.add, ALU.subtract)
                        ins.then_inc(lows.sem, 1)
            ph.parts = dict(pe=pe, act=act, dve=dve, pool=pool)

        HY_OUT = region(C, 0, 2 * T)
        MLA_OUT = region(C, 2 * T, 3 * T)
        FREE = 5 * T
        hy3 = HY_OUT.rearrange("p (c t) -> p c t", c=2)
        mla3 = MLA_OUT.rearrange("p (c t) -> p c t", c=3)

        def raws():
            return [region(X, s * RAW, RAW) for s in range(2)]

        def zero_pads(e, sigref):
            for s in range(2):
                for c in (0, SEQ + 1, SEQ + 2, RAW - 1):
                    e.memset(raws()[s][:, c:c + 1], 0.0).then_inc(sigref.sem, 1)

        zt = region(C, FREE, 2 * T)
        z3 = zt.rearrange("p (c t) -> p c t", c=2)

        def phase_hyena_in(l):
            ph = Phase()
            n0 = tiles[0]
            tiles[0] += 6
            ph.ends.append((tile_done.sem, tiles[0]))
            zeroed = ph.sig("pads_zeroed", 8)
            raw_ready = ph.sig("raw_ready", 6)
            conv_done = ph.sig("conv_done", 6)
            z_made = ph.sig("z_made", 2)
            order = [0, 2, 4, 1, 3, 5]
            tmp = region(X, 2 * RAW, T)
            src = a["w_in"][l].rearrange("(k p) n -> p k n", p=P)

            def pool(e):
                zero_pads(e, zeroed)

            def sp(e):
                for j, t in enumerate(order):
                    c = HY_COL + t * P
                    load_tile(e, tile(n0, 0, j), src, c, DK, P)

            def pe(e):
                for j in range(6):
                    whole_product(e, tile(n0, 0, j), DK, P, whole_h, False, (raw_ready, j - 1) if j >= 2 else None)

            def act(e):
                e.wait_ge(zeroed.sem, zeroed.at(8))
                for j in range(6):
                    n = n0 + j
                    e.wait_ge(tile_done.sem, n + 1)
                    if j >= 2:
                        e.wait_ge(conv_done.sem, conv_done.at(j - 1))
                    keep_raw(e, n % 2, raws()[j % 2], T, raw_ready)

            def dve(e):
                e.wait_ge(zeroed.sem, zeroed.at(8))
                for j, t in enumerate(order):
                    e.wait_ge(raw_ready.sem, raw_ready.at(j + 1))
                    kind, c = t // 2, t % 2
                    dst = hy3[:, c] if kind == 0 else (z3[:, c] if kind == 1 else tmp)
                    w = [vec("hy_conv_w", s * 6 + t) for s in range(3)]
                    conv(e, raws()[j % 2], w, vec("hy_conv_b", t), dst, T, conv_done)
                    if kind == 2:
                        e.wait_ge(conv_done.sem, conv_done.at(j + 1))
                        e.tensor_tensor(z3[:, c], z3[:, c], tmp, ALU.mult).then_inc(z_made.sem, 1)
                        e.wait_ge(z_made.sem, z_made.at(c + 1))
            ph.parts = dict(sp=sp, pe=pe, act=act, dve=dve, pool=pool)

        def phase_hyena_filter(l, length, at):
            ph = Phase()
            NT = length // P
            name = "lat" if length == SEQ else "ctx"
            HN = min(BANK, length)
            NH = length // HN
            ld = ph.sig("filter_loaded", 6, 16)
            ones = ph.sig("ones_row", 1)
            l1 = ph.sig("layer1", NH)
            s1 = ph.sig("sin1", NH)
            l2 = ph.sig("layer2", NH)
            s2 = ph.sig("sin2", NH)
            l3 = ph.sig("layer3", NT)
            dec = ph.sig("decay_made", NT)
            hh = ph.sig("filter_made", NT)
            ab = ph.sig("filter_abs", NT)
            nrm = ph.sig("norm_summed", NT)
            zt_ = ph.sig("z_turned", NT)
            zk = ph.sig("z_kept", NT)
            fin = ph.sig("inv_norm_made", 1)
            o = FREE + 2 * T
            zf = region(C, o, SEQ)
            h1 = region(C, o + SEQ, SEQ)
            h2 = region(C, o + 2 * SEQ, SEQ)
            t1 = region(C, o + 3 * SEQ, SEQ)
            t2 = region(C, o + 4 * SEQ, SEQ)
            o += 5 * SEQ
            w1 = region(C, o, HY_HID)
            w2 = region(C, o + 64, HY_HID)
            w3_ = region(C, o + 128, 2 * HY)
            o += 128 + 512
            hf = [region(C, o + s * 512, 512) for s in range(2)]
            ha = [region(C, o + 1024 + s * 512, 512) for s in range(2)]
            dc = [region(C, o + 2048 + s * 256, 256) for s in range(2)]
            nsum = region(C, o + 2560, 4)
            assert o + 2564 <= FT * T
            ezo = region(X, 0, NT * 768).rearrange("p (t w c) -> p t w c", w=3, c=HY)

            def pool(e):
                e.dma_start(zf[0:HY_EMB, 0:length], a["k_z_" + name]).then_inc(ld.sem, 16)
                e.dma_start(w1[0:HY_EMB, :], a["hy_w1"][l]).then_inc(ld.sem, 16)
                e.dma_start(w2[0:HY_HID, :], a["hy_w2"][l]).then_inc(ld.sem, 16)
                e.dma_start(w3_[0:HY_HID, :], a["hy_w3"][l]).then_inc(ld.sem, 16)
                e.dma_start(w3_[HY_HID:HY_HID + 1, :], a["hy_b3"][l:l + 1, :]).then_inc(ld.sem, 16)
                e.dma_start(t2[0:1, 0:1], a["c"][0:1, 0:1]).then_inc(ld.sem, 16)
                e.memset(h2[HY_HID:HY_HID + 1, 0:length], 1.0).then_inc(ones.sem, 1)

            def pe(e):
                e.wait_ge(ld.sem, ld.at(6))
                e.wait_ge(ones.sem, ones.at(1))
                for b in range(NH):
                    e.matmul(ps[0:64, b * BANK:b * BANK + HN], w1[0:HY_EMB, :], zf[0:HY_EMB, b * HN:b * HN + HN],
                             start=True, stop=True).then_inc(l1.sem, 1)
                for b in range(NH):
                    e.wait_ge(s1.sem, s1.at(b + 1))
                    e.matmul(ps[0:64, (2 + b) * BANK:(2 + b) * BANK + HN], w2[0:HY_HID, :],
                             h1[0:HY_HID, b * HN:b * HN + HN], start=True, stop=True).then_inc(l2.sem, 1)
                e.wait_ge(s2.sem, s2.at(NH))
                for t in range(NT):
                    if t >= 2:
                        e.wait_ge(hh.sem, hh.at(t - 1))
                    e.matmul(ps[:, (t % 2) * BANK:(t % 2) * BANK + 512], h2[0:HY_HID + 1, t * P:t * P + P],
                             w3_[0:HY_HID + 1, :], start=True, stop=True).then_inc(l3.sem, 1)
                    if t >= 2:
                        e.wait_ge(zk.sem, zk.at(t - 1))
                    for c in range(2):
                        ins = e.transpose(ps[:, (4 + t % 2) * BANK + c * P:(4 + t % 2) * BANK + c * P + P],
                                          z3[:, c, at + t * P:at + t * P + P], ident)
                    ins.then_inc(zt_.sem, 1)
                    if t >= 1:
                        sum_tile(e, t - 1)
                sum_tile(e, NT - 1)

            def sum_tile(e, t):
                e.wait_ge(ab.sem, ab.at(t + 1))
                for c in range(4):
                    ins = e.matmul(ps[:, 6 * BANK + c * 8 + t:6 * BANK + c * 8 + t + 1],
                                   ha[t % 2][:, c * P:c * P + P], K[:, K_ONES:K_ONES + 1], start=True, stop=True)
                ins.then_inc(nrm.sem, 1)

            def act(e):
                e.wait_ge(ld.sem, ld.at(6))
                for w, (pre, post, bank, hout) in enumerate(((sm1, s1, 0, h1), (sm2, s2, 2, h2))):
                    for b in range(NH):
                        e.wait_ge(pre.sem, pre.at(b + 1))
                        e.activation(hout[0:HY_HID, b * HN:b * HN + HN], t1[0:HY_HID, b * HN:b * HN + HN], ACT.Sin)\
                            .then_inc(post.sem, 1)
                for t in range(NT):
                    if t >= 2:
                        e.wait_ge(hh.sem, hh.at(t - 1))
                    c = K_TN + (0 if length == SEQ else SEQ // P) + t
                    e.activation(dc[t % 2], K[:, K_DELTA:K_DELTA + HY], ACT.Exp, scale=K[:, c:c + 1])\
                        .then_inc(dec.sem, 1)
                    e.wait_ge(zt_.sem, zt_.at(t + 1))
                    e.activation(ezo[:, t, 1, :], ps[:, (4 + t % 2) * BANK:(4 + t % 2) * BANK + HY], ACT.Copy)\
                        .then_inc(zk.sem, 1)
                    e.wait_ge(hh.sem, hh.at(t + 1))
                    if t >= 2:
                        e.wait_ge(nrm.sem, nrm.at(t - 1))
                    e.activation(ha[t % 2], hf[t % 2], ACT.Abs).then_inc(ab.sem, 1)

            sm1 = ph.sig("reduced1", NH)
            sm2 = ph.sig("reduced2", NH)
            ez = ph.sig("ezo_made", NT)

            def dve(e):
                link = chain["dve"].link
                MAGIC = 1.5 * 2.0 ** 23
                A1 = 6.28125
                A2 = float(np.float32(TWO_PI - A1))
                A3 = float(TWO_PI - A1 - A2)
                for w, (pre, post, bank, bias) in enumerate(((l1, sm1, 0, b1), (l2, sm2, 2, b2))):
                    for b in range(NH):
                        sl = slice(b * HN, b * HN + HN)
                        u, r = t1[0:HY_HID, sl], t2[0:HY_HID, sl]
                        e.wait_ge(pre.sem, pre.at(b + 1))
                        if w:
                            e.wait_ge(s1.sem, s1.at(b + 1))
                        link(e, e.tensor_scalar(u, ps[0:64, (bank + b) * BANK:(bank + b) * BANK + HN], bias, None, ALU.add))
                        link(e, e.tensor_scalar(r, u, float(1 / TWO_PI), MAGIC, ALU.mult, ALU.add))
                        link(e, e.tensor_scalar(r, r, -MAGIC, None, ALU.add))
                        link(e, e.scalar_tensor_tensor(u, r, -A1, u, ALU.mult, ALU.add))
                        link(e, e.scalar_tensor_tensor(u, r, -A2, u, ALU.mult, ALU.add))
                        link(e, e.scalar_tensor_tensor(u, r, -A3, u, ALU.mult, ALU.add))
                        e.tensor_scalar(u, u, 3.1415925, -3.1415925, ALU.min, ALU.max).then_inc(post.sem, 1)
                for t in range(NT):
                    e.wait_ge(l3.sem, l3.at(t + 1))
                    e.wait_ge(dec.sem, dec.at(t + 1))
                    if t >= 2:
                        e.wait_ge(ab.sem, ab.at(t - 1))
                    o_, i_ = hf[t % 2].rearrange("p (w c) -> p w c", w=2), \
                        ps[:, (t % 2) * BANK:(t % 2) * BANK + 512].rearrange("p (w c) -> p w c", w=2)
                    ins = e.tensor_tensor(o_, i_, dc[t % 2].unsqueeze(1).broadcast_to([P, 2, HY]), ALU.mult)
                    if t == 0:
                        link(e, ins)
                        ins = e.tensor_scalar(o_[:, 1, :], o_[:, 1, :], K[:, K_T0:K_T0 + 1], None, ALU.mult)
                    ins.then_inc(hh.sem, 1)
                    e.wait_ge(hh.sem, hh.at(t + 1))
                    e.tensor_tensor(ezo[:, t, 0, :], o_[:, 0, :], o_[:, 1, :], ALU.add)
                    e.tensor_tensor(ezo[:, t, 2, :], o_[:, 0, :], o_[:, 1, :], ALU.subtract).then_inc(ez.sem, 1)
                e.wait_ge(nrm.sem, nrm.at(NT))
                link(e, e.tensor_reduce(nsum, ps[:, 6 * BANK:6 * BANK + 32].rearrange("p (c t) -> p c t", t=8)[:, :, 0:NT],
                                        AX.X, ALU.add))
                link(e, e.tensor_tensor(nsum[:, 0:2], nsum[:, 0:2], nsum[:, 2:4], ALU.add))
                e.reciprocal(inv_norm, nsum[:, 0:2]).then_inc(fin.sem, 1)
            ph.parts = dict(pe=pe, act=act, dve=dve, pool=pool)

        def phase_hyena_conv(l, length, at):
            ph = Phase()
            NT = length // P
            name = "lat" if length == SEQ else "ctx"
            HN = min(BANK, length)
            NH = length // HN
            n0 = tiles[0]
            tiles[0] += 4 * NT
            ph.ends.append((tile_done.sem, tiles[0]))
            spec = ph.sig("spectrum_kept", NT)
            yy = ph.sig("products_made", NT)
            fin = ph.sig("hyena_out", 2)
            ezo = region(X, 0, NT * 768).rearrange("p (t w c) -> p t w c", w=3, c=HY)
            o = FREE + 2 * T
            y = region(C, o, NT * 512).rearrange("p (f r c) -> p f r c", r=2, c=HY)
            o += 4096
            sp_ = [region(C, o + s * 1024, 1024).rearrange("p (r c) -> p r c", r=4) for s in range(2)]
            ta = region(C, o + 2048, 256)
            tmp = region(C, o + 2304, T)

            def sp(e):
                for f in range(NT):
                    for r in range(2):
                        src = a["k_dft_" + name][r].rearrange("(k p) n -> p k n", p=P)
                        load_tile(e, tile(n0, 0, 2 * f + r), src, f * P, NT, P)
                for f in range(NT):
                    for r in range(2):
                        n = n0 + 2 * NT + 2 * f + r
                        e.wait_ge(tile_done.sem, n - 1)
                        e.dma_start(W[:, (n % 2) * D:(n % 2) * D + length], a["k_idft_" + name][r, f * P:f * P + P, :])\
                            .then_inc(w_loaded[n % 2].sem, 16)

            def pe(e):
                for f in range(NT):
                    if f >= 2:
                        e.wait_ge(spec.sem, spec.at(f - 1))
                    for r in range(2):
                        n = n0 + 2 * f + r
                        e.wait_ge(w_loaded[n % 2].sem, (n // 2 + 1) * 16)
                        b = 2 * (f % 2) + r
                        for t in range(NT):
                            ins = e.matmul(ps[:, b * BANK:b * BANK + 512], w3[:, n % 2, t, :],
                                           ezo[:, t, r:r + 2, :], start=(t == 0), stop=(t == NT - 1))
                        ins.then_inc(tile_done.sem, 1)
                for f in range(NT):
                    for r in range(2):
                        n = n0 + 2 * NT + 2 * f + r
                        e.wait_ge(w_loaded[n % 2].sem, (n // 2 + 1) * 16)
                        e.wait_ge(yy.sem, yy.at(f + 1))
                        for c in range(2):
                            for b in range(NH):
                                ins = e.matmul(ps[:, (4 + 2 * c + b) * BANK:(4 + 2 * c + b) * BANK + HN],
                                               y[:, f, r, c * P:c * P + P],
                                               W[:, (n % 2) * D + b * HN:(n % 2) * D + b * HN + HN],
                                               start=(f == 0 and r == 0), stop=(f == NT - 1 and r == 1))
                        ins.then_inc(tile_done.sem, 1)

            def act(e):
                for f in range(NT):
                    n = n0 + 2 * f + 1
                    e.wait_ge(tile_done.sem, n + 1)
                    if f >= 2:
                        e.wait_ge(yy.sem, yy.at(f - 1))
                    b = 2 * (f % 2)
                    e.activation(sp_[f % 2], ps[:, b * BANK:b * BANK + 1024].rearrange("p (r c) -> p r c", r=4),
                                 ACT.Copy).then_inc(spec.sem, 1)

            def dve(e):
                link = chain["dve"].link
                for f in range(NT):
                    e.wait_ge(spec.sem, spec.at(f + 1))
                    hr, zr, zs, hs = (sp_[f % 2][:, i] for i in range(4))
                    link(e, e.tensor_tensor(ta, zs, hs, ALU.mult))
                    link(e, e.tensor_tensor(y[:, f, 0], zr, hr, ALU.mult))
                    link(e, e.tensor_tensor(y[:, f, 0], y[:, f, 0], ta, ALU.subtract))
                    link(e, e.tensor_tensor(ta, zr, hs, ALU.mult))
                    link(e, e.tensor_tensor(y[:, f, 1], zs, hr, ALU.mult))
                    e.tensor_tensor(y[:, f, 1], y[:, f, 1], ta, ALU.add).then_inc(yy.sem, 1)
                    e.wait_ge(yy.sem, yy.at(f + 1))
                e.wait_ge(tile_done.sem, tiles_end)
                for c in range(2):
                    t_ = tmp[:, 0:length]
                    zz, oo = z3[:, c, at:at + length], hy3[:, c, at:at + length]
                    link(e, e.tensor_scalar(t_, zz, vec("hy_d", c), None, ALU.mult))
                    link(e, e.scalar_tensor_tensor(t_, ps[:, (4 + 2 * c) * BANK:(4 + 2 * c) * BANK + length],
                                                   inv_norm[:, c:c + 1], t_, ALU.mult, ALU.add))
                    e.tensor_tensor(oo, oo, t_, ALU.mult).then_inc(fin.sem, 1)
                    e.wait_ge(fin.sem, fin.at(c + 1))
            tiles_end = tiles[0]
            ph.parts = dict(sp=sp, pe=pe, act=act, dve=dve)

        CQ = region(C, FREE, 2 * T).rearrange("p (k t) -> p k t", k=2)
        CKV = region(C, FREE + 2 * T, T)
        KRAW = region(C, FREE + 3 * T, T)
        ATT = FREE + 4 * T

        def phase_mla_in(l):
            ph = Phase()
            n0 = tiles[0]
            tiles[0] += 4
            ph.ends.append((tile_done.sem, tiles[0]))
            kept = ph.sig("latents_kept", 4)
            src = a["w_in"][l].rearrange("(k p) n -> p k n", p=P)

            def sp(e):
                for j in range(4):
                    c = MLA_COL + j * P
                    w = P if j < 3 else ROPE
                    load_tile(e, tile(n0, 0, j), src, c, DK, w)

            def pe(e):
                for j in range(4):
                    whole_product(e, tile(n0, 0, j), DK, P if j < 3 else ROPE, whole_h, False,
                            (kept, j - 1) if j >= 2 else None, lo=0 if j < 3 else NOPE)

            def act(e):
                for j in range(4):
                    n = n0 + j
                    e.wait_ge(tile_done.sem, n + 1)
                    dst = (CQ[:, 0], CQ[:, 1], CKV, KRAW[NOPE:QK, :])[j]
                    src_ = group(n % 2, T) if j < 3 else group(n % 2, T, NOPE, QK)
                    e.activation(dst, src_, ACT.Copy).then_inc(kept.sem, 1)
            ph.parts = dict(sp=sp, pe=pe, act=act)

        def phase_mla_norm(l):
            ph = Phase()
            squared = ph.sig("squared", 3)
            summed = ph.sig("squares_summed", 2)
            root = ph.sig("root_made", 2)
            inv = ph.sig("rstd_made", 2)
            made = ph.sig("latents_normed", 3)
            sq = [region(X, s * T, T) for s in range(3)]
            rt = [region(X, (3 + s) * T, T) for s in range(2)]
            src = (CQ[:, 0], CQ[:, 1], CKV)

            def act(e):
                for j in range(3):
                    e.activation(sq[j], src[j], ACT.Square).then_inc(squared.sem, 1)
                for w, r in enumerate((QR, KVR)):
                    e.wait_ge(summed.sem, summed.at(w + 1))
                    e.activation(rt[w], group(w, T), ACT.Sqrt, bias=eps, scale=1.0 / r).then_inc(root.sem, 1)

            def pe(e):
                for w, js in enumerate(((0, 1), (2,))):
                    e.wait_ge(squared.sem, squared.at(js[-1] + 1))
                    for b, (t0, tn) in enumerate(tok(False)):
                        for j in js:
                            ins = e.matmul(ps[:, w * GROUP + b * BANK:w * GROUP + b * BANK + tn],
                                           K[:, K_ONES:K_ONES + P], sq[j][:, t0:t0 + tn],
                                           start=(j == js[0]), stop=(j == js[-1]))
                    ins.then_inc(summed.sem, 1)

            def dve(e):
                for w, js in enumerate(((0, 1), (2,))):
                    e.wait_ge(root.sem, root.at(w + 1))
                    e.reciprocal(rt[w], rt[w]).then_inc(inv.sem, 1)
                    e.wait_ge(inv.sem, inv.at(w + 1))
                    for j in js:
                        g = vec("mla_q_norm_g", j) if j < 2 else vec("mla_kv_norm_g")
                        e.scalar_tensor_tensor(src[j], src[j], g, rt[w], ALU.mult, ALU.mult).then_inc(made.sem, 1)
            ph.parts = dict(pe=pe, act=act, dve=dve)

        def phase_mla_heads(l, last):
            ph = Phase()
            NQ = 8 if last else 10
            SCALE = float(QK) ** -0.5
            HD = HEADS
            steps = [(b * BANK, BANK, kt, 6 + b, b) for b in range(2) for kt in range(10)]
            if not last:
                steps += [(SEQ, CTX, kt, 6, 2) for kt in (8, 9)]
            NS, NB = len(steps), steps[-1][4] + 1
            PREP_AT = {0: 0, 1: 1, 3: 2, 5: 3, 12: 4, 15: 5}
            rope_ld = ph.sig("rope_loaded", 2, 16)
            wl = ph.sig("pair_w_loaded", PAIRS, 64)
            ready = ph.sig("head_buffers_ready", 3)
            proj = ph.sig("head_projected", 2 * HD)
            kept = ph.sig("head_kept", 2 * HD)
            squared = ph.sig("head_squared", 2 * HD)
            summed = ph.sig("head_summed", 2 * HD)
            rooted = ph.sig("head_root", 2 * HD)
            inv = ph.sig("head_rstd", 2 * HD)
            normed = ph.sig("head_normed", 2 * HD)
            turned = ph.sig("head_turned", 2 * HD)
            sined = ph.sig("head_sined", 2 * HD)
            cosed = ph.sig("head_cosed", 2 * HD)
            roped = ph.sig("head_roped", 2 * HD)
            vproj = ph.sig("values_projected", PAIRS)
            vkept = ph.sig("values_kept", PAIRS)
            scored = ph.sig("scored", NQ * HD)
            maxed = ph.sig("maxed", NQ * HD)
            rowed = ph.sig("maxima_rowed", HD)
            rowkept = ph.sig("maxima_kept", HD)
            keyed = ph.sig("scored_by_key", NS * HD)
            exped = ph.sig("exped", NS * HD + 1)
            onormed = ph.sig("attention_normed", NB * HD + 1)
            mixed = ph.sig("values_mixed", NS * HD)
            oinv = ph.sig("sum_inverted", NB * HD)
            o = ATT
            Q = [region(C, o + j * T, T) for j in range(2)]
            Kh = [region(C, o + (2 + j) * T, T) for j in range(2)]
            SQ0, SQ1, RT0, RT1, QRAW = (region(C, o + (4 + j) * T, T) for j in range(5))
            o += 9 * T
            cos, sin = region(C, o, SEQ), region(C, o + SEQ, SEQ)
            o += 2 * SEQ
            TM = region(C, o, SEQ)
            o += SEQ
            assert o <= FT * T
            V = region(X, 0, 10 * 4 * VD).rearrange("p (t w v) -> p t w v", w=4, v=VD)
            PT = [region(X, 2 * T + s * BANK, BANK) for s in range(4)]
            RB = [region(X, 4 * T + s * BANK, BANK) for s in range(3)]
            wq = [region(X, 6 * T + s * 192, 192).rearrange("p (k n) -> p k n", k=2) for s in range(2)]
            wkv = region(X, 6 * T + 384, 256).rearrange("p (h n) -> p h n", h=2)
            st = region(X, 6 * T + 640, 16)
            raws_, sqs, rts = (QRAW, KRAW), (SQ0, SQ1), (RT0, RT1)

            def blocks(t):
                return (0, T) if t < 8 else (SEQ, CTX)

            def pool(e):
                e.memset(V[:, :, 1:3, :], 1.0).then_inc(ready.sem, 1)
                for u in range(2):
                    e.wait_ge(ready.sem, ready.at(u + 1))
                    e.memset(Kh[u][QK:P, :], 0.0).then_inc(ready.sem, 1)
                e.wait_ge(ready.sem, ready.at(3))
                e.memset(Kh[0][QK:QK + 1, :], 1.0).then_inc(exped.sem, 1)
                e.wait_ge(exped.sem, exped.at(1))
                e.memset(Kh[1][QK:QK + 1, :], 1.0).then_inc(onormed.sem, 1)

            def sp(e):
                for r, t_ in enumerate((cos, sin)):
                    e.dma_start(t_[0:QK, :], a["k_rope"][r]).then_inc(rope_ld.sem, 16)
                uq = a["mla_w_uq"][l].rearrange("(k p) n -> p k n", p=P)
                ukv = a["mla_w_ukv"][l]

                def load(u, cq, ckv):
                    e.dma_start(wq[u], uq[:, :, bass.ds(cq, QK)]).then_inc(wl.sem, 16)
                    e.dma_start(wkv[:, u], ukv[:, bass.ds(ckv, 2 * VD)]).then_inc(wl.sem, 16)

                for u in range(2):
                    load(u, u * QK, u * 2 * VD)
                for i in range(1, PAIRS):
                    e.wait_ge(proj.sem, proj.at(i * 4))
                    for u in range(2):
                        load(u, (2 * i + u) * QK, (2 * i + u) * 2 * VD)

            def every_head(prep, main):
                for stage in range(6):
                    prep(stage, 0, 0, 0)

                def pair(i, final):
                    main(i, 0, i * 2, lambda stage: prep(stage, i * 2 + 1, 1, i))
                    main(i, 1, i * 2 + 1, (lambda stage: None) if final
                         else (lambda stage: prep(stage, i * 2 + 2, 0, i + 1)))
                return pair

            def pe(e):
                e.wait_ge(rope_ld.sem, rope_ld.at(2))
                e.wait_ge(exped.sem, exped.at(1))
                e.wait_ge(onormed.sem, onormed.at(1))

                def prep(stage, h, u, pair):
                    j = stage % 2
                    if stage < 2:
                        if stage == 0:
                            e.wait_ge(wl.sem, wl.at(pair + 1))
                        else:
                            e.wait_ge(kept.sem, kept.at(h * 2 + 1))
                        for b, (t0, tn) in enumerate(tok(False)):
                            c = GROUP + b * BANK
                            if stage == 0:
                                for k in range(2):
                                    ins = e.matmul(ps[0:QK, c:c + tn], wq[u][:, k, :], CQ[:, k, t0:t0 + tn],
                                                   start=(k == 0), stop=(k == 1))
                            else:
                                ins = e.matmul(ps[0:NOPE, c:c + tn], wkv[:, u, 0:NOPE], CKV[:, t0:t0 + tn],
                                               start=True, stop=True)
                        ins.then_inc(proj.sem, 1)
                    elif stage < 4:
                        if j == 0:
                            e.wait_ge(kept.sem, kept.at(h * 2 + 2))
                        else:
                            e.wait_ge(rooted.sem, rooted.at(h * 2 + 1))
                        e.wait_ge(squared.sem, squared.at(h * 2 + j + 1))
                        for b, (t0, tn) in enumerate(tok(False)):
                            ins = e.matmul(ps[0:QK, GROUP + b * BANK:GROUP + b * BANK + tn],
                                           K[0:QK, K_ONES:K_ONES + QK], sqs[j][0:QK, t0:t0 + tn], start=True, stop=True)
                        ins.then_inc(summed.sem, 1)
                    else:
                        if j == 0:
                            e.wait_ge(rooted.sem, rooted.at(h * 2 + 2))
                        else:
                            e.wait_ge(sined.sem, sined.at(h * 2 + 1))
                        e.wait_ge(normed.sem, normed.at(h * 2 + j + 1))
                        for b in range(2):
                            ins = e.matmul(ps[0:QK, GROUP + b * BANK:GROUP + b * BANK + BANK], K[0:QK, K_ROT:K_ROT + QK],
                                           (Q, Kh)[j][u][0:QK, b * BANK:b * BANK + BANK], start=True, stop=True)
                        ins.then_inc(turned.sem, 1)

                def score(t, u):
                    k0, kn = blocks(t)
                    c = (t + 1) % 2 * GROUP
                    for b in range(0, kn, BANK):
                        n = min(BANK, kn - b)
                        ins = e.matmul(ps[:, c + b:c + b + n], Q[u][0:QK, t * P:t * P + P],
                                       Kh[u][0:QK, k0 + b:k0 + b + n], start=True, stop=True)
                    ins.then_inc(scored.sem, 1)

                def row(t, h):
                    e.wait_ge(maxed.sem, maxed.at(h * NQ + t + 1))
                    if t == 0:
                        e.wait_ge(onormed.sem, onormed.at(h * NB + 1))
                    c = 6 * BANK + t * P if t < 8 else 2 * BANK + (t - 8) * P
                    ins = e.matmul(ps[QK:P, c:c + P], st[:, t:t + 1].broadcast_to([P, P - QK]), ident,
                                   start=True, stop=True)
                    if t == NQ - 1:
                        ins.then_inc(rowed.sem, 1)

                def by_key(s, u, h):
                    q0, n, kt, _, _ = steps[s]
                    if s >= 3:
                        e.wait_ge(exped.sem, exped.at(h * NS + s - 1))
                    e.matmul(ps[:, s % 3 * BANK:s % 3 * BANK + n], Kh[u][:, kt * P:kt * P + P], Q[u][:, q0:q0 + n],
                             start=True, stop=True).then_inc(keyed.sem, 1)

                def main(i, u, h, next_):
                    if u == 0:
                        e.wait_ge(exped.sem, exped.at(h * NS + 1))
                        for t in range(10):
                            ins = e.matmul(ps[:, t * P:t * P + P], CKV[:, t * P:t * P + P], wkv[:, :, NOPE:NOPE + VD],
                                           start=True, stop=True)
                        ins.then_inc(vproj.sem, 1)
                    e.wait_ge(roped.sem, roped.at(h * 2 + 2))
                    for t in range(NQ):
                        if t == 1 and u == 0:
                            e.wait_ge(vkept.sem, vkept.at(i + 1))
                        elif t == 1:
                            e.wait_ge(exped.sem, exped.at(h * NS + 1))
                        elif t >= 2:
                            e.wait_ge(maxed.sem, maxed.at(h * NQ + t - 1))
                        score(t, u)
                        if t >= 2:
                            row(t - 2, h)
                    row(NQ - 2, h)
                    row(NQ - 1, h)
                    e.wait_ge(rowkept.sem, rowkept.at(h + 1))
                    for s in range(3):
                        by_key(s, u, h)
                    for s, (_, n, kt, bank, b) in enumerate(steps):
                        e.wait_ge(exped.sem, exped.at(h * NS + s + 2))
                        if b == 2 and kt == 8:
                            e.wait_ge(onormed.sem, onormed.at(h * NB + 2))
                        first = s == 0 or steps[s - 1][4] != b
                        final = s == NS - 1 or steps[s + 1][4] != b
                        e.matmul(ps[:, bank * BANK:bank * BANK + n],
                                 V[:, kt, 2 * u:2 * u + 2, :].rearrange("p w v -> p (w v)"), PT[s % 4][:, 0:n],
                                 start=first, stop=final).then_inc(mixed.sem, 1)
                        if s + 3 < NS:
                            by_key(s + 3, u, h)
                        if s in PREP_AT:
                            next_(PREP_AT[s])

                pair = every_head(prep, main)
                with e.Fori(0, PAIRS - 1) as i:
                    pair(i, False)
                pair(PAIRS - 1, True)

            def act(e):
                def prep(stage, h, u, pair):
                    j = stage % 2
                    if stage < 2:
                        e.wait_ge(proj.sem, proj.at(h * 2 + j + 1))
                        n = (QK, NOPE)[j]
                        e.activation(raws_[j][0:n, :], group(1, T, 0, n), ACT.Copy).then_inc(kept.sem, 1)
                        e.wait_ge(kept.sem, kept.at(h * 2 + j + 1))
                        e.activation(sqs[j][0:QK, :], raws_[j][0:QK, :], ACT.Square).then_inc(squared.sem, 1)
                    elif stage < 4:
                        e.wait_ge(summed.sem, summed.at(h * 2 + j + 1))
                        e.activation(rts[j][0:QK, :], group(1, T, 0, QK), ACT.Sqrt, bias=eps[0:QK, :], scale=1.0 / QK)\
                            .then_inc(rooted.sem, 1)

                def main(i, u, h, next_):
                    if u == 0:
                        e.wait_ge(vproj.sem, vproj.at(i + 1))
                        e.activation(V[:, :, 0:4:3, :], group(0, T).rearrange("p (t w v) -> p t w v", w=2, v=VD), ACT.Copy)\
                            .then_inc(vkept.sem, 1)
                    e.wait_ge(rowed.sem, rowed.at(h + 1))
                    ins = e.activation(Q[u][QK:P, 0:SEQ], ps[QK:P, 6 * BANK:8 * BANK], ACT.Copy, scale=-1.0)
                    if not last:
                        ins = e.activation(Q[u][QK:P, SEQ:T], ps[QK:P, 2 * BANK:2 * BANK + CTX], ACT.Copy, scale=-1.0)
                    ins.then_inc(rowkept.sem, 1)

                    for s, (_, n, _, _, b) in enumerate(steps):
                        e.wait_ge(keyed.sem, keyed.at(h * NS + s + 1))
                        if s >= 4:
                            e.wait_ge(mixed.sem, mixed.at(h * NS + s - 3))
                        e.activation(PT[s % 4][:, 0:n], ps[:, s % 3 * BANK:s % 3 * BANK + n], ACT.Exp, scale=SCALE)\
                            .then_inc(exped.sem, 1)
                        if s - 2 in PREP_AT:
                            next_(PREP_AT[s - 2])

                pair = every_head(prep, main)
                with e.Fori(0, PAIRS - 1) as i:
                    pair(i, False)
                pair(PAIRS - 1, True)

            def dve(e):
                def prep(stage, h, u, pair):
                    j = stage % 2
                    at = h * 2 + j + 1
                    if 2 <= stage < 4:
                        e.wait_ge(rooted.sem, rooted.at(at))
                        e.reciprocal(rts[j][0:QK, :], rts[j][0:QK, :]).then_inc(inv.sem, 1)
                        e.wait_ge(inv.sem, inv.at(at))
                        e.scalar_tensor_tensor((Q, Kh)[j][u][0:QK, :], raws_[j][0:QK, :], (q_g, k_g)[j],
                                               rts[j][0:QK, :], ALU.mult, ALU.mult).then_inc(normed.sem, 1)
                    elif stage >= 4:
                        lat = (Q, Kh)[j][u][0:QK, 0:SEQ]
                        e.wait_ge(turned.sem, turned.at(at))
                        if j:
                            e.wait_ge(roped.sem, roped.at(h * 2 + 1))
                        e.tensor_tensor(TM[0:QK, :], group(1, SEQ, 0, QK), sin[0:QK, :], ALU.mult).then_inc(sined.sem, 1)
                        e.tensor_tensor(lat, lat, cos[0:QK, :], ALU.mult).then_inc(cosed.sem, 1)
                        e.wait_ge(sined.sem, sined.at(at))
                        e.wait_ge(cosed.sem, cosed.at(at))
                        e.tensor_tensor(lat, lat, TM[0:QK, :], ALU.add).then_inc(roped.sem, 1)

                def main(i, u, h, next_):
                    for t in range(NQ):
                        e.wait_ge(scored.sem, scored.at(h * NQ + t + 1))
                        c = (t + 1) % 2 * GROUP
                        e.tensor_reduce(st[:, t:t + 1], ps[:, c:c + blocks(t)[1]], AX.X, ALU.max).then_inc(maxed.sem, 1)

                    def norm(b):
                        mine = slice(u * 64, u * 64 + 64)
                        other = slice(64 - u * 64, 128 - u * 64)
                        n, bank = (BANK if b < 2 else CTX), 6 + b % 2
                        s_end = max(s for s in range(NS) if steps[s][4] == b)
                        e.wait_ge(mixed.sem, mixed.at(h * NS + s_end + 1))
                        e.reciprocal(RB[b][mine, 0:n], ps[other, bank * BANK:bank * BANK + n]).then_inc(oinv.sem, 1)
                        e.wait_ge(oinv.sem, oinv.at(h * NB + b + 1))
                        e.tensor_tensor(MLA_OUT[mine, bass.ds(i * T + b * BANK, n)], ps[mine, bank * BANK:bank * BANK + n],
                                        RB[b][mine, 0:n], ALU.mult).then_inc(onormed.sem, 1)

                    next_(2)
                    next_(3)
                    norm(0)
                    next_(4)
                    next_(5)
                    for b in range(1, NB):
                        norm(b)

                pair = every_head(prep, main)
                with e.Fori(0, PAIRS - 1) as i:
                    pair(i, False)
                pair(PAIRS - 1, True)
            ph.parts = dict(sp=sp, pe=pe, act=act, dve=dve, pool=pool)

        GQ = FREE
        qkv = region(C, GQ, 9 * T).rearrange("p (n t) -> p n t", n=9)
        zz3 = region(C, GQ + 9 * T, 3 * T).rearrange("p (n t) -> p n t", n=3)
        O_OUT = region(C, GQ + 12 * T, 3 * T)
        o3 = O_OUT.rearrange("p (n t) -> p n t", n=3)
        abT = region(C, GQ + 15 * T, T)
        GT = region(C, GQ + 16 * T, N_CHUNK * 36)
        assert GQ + 16 * T + N_CHUNK * 36 <= FT * T
        gt5 = GT.rearrange("p (n d k q) -> p n d k q", n=N_CHUNK, d=2, k=6)

        def phase_gdn_in(l):
            ph = Phase()
            n0 = tiles[0]
            tiles[0] += 13
            ph.ends.append((tile_done.sem, tiles[0]))
            zeroed = ph.sig("pads_zeroed", 8)
            raw_ready = ph.sig("raw_ready", 9)
            conv_done = ph.sig("conv_done", 9)
            silu = ph.sig("silu_made", 9)
            zk = ph.sig("z_gate_kept", 4)
            src = a["w_in"][l].rearrange("(k p) n -> p k n", p=P)
            cv = [region(X, 2 * RAW + s * T, T) for s in range(2)]

            def pool(e):
                zero_pads(e, zeroed)

            def sp(e):
                with e.Fori(0, 4) as i:
                    for u in range(2):
                        load_tile(e, tile(n0, i, u), src, i * 256 + u * P, DK, P)
                for j in range(8, 13):
                    w = P if j < 12 else 4 * HEADS
                    load_tile(e, tile(n0, 0, j), src, j * P, DK, w)

            def pe(e):
                whole_product(e, tile(n0, 0, 0), DK, P, whole_h, False)
                whole_product(e, tile(n0, 0, 1), DK, P, whole_h, False)
                with e.Fori(1, 4) as i:
                    for u in range(2):
                        whole_product(e, tile(n0, i, u), DK, P, whole_h, False, (raw_ready, i * 2 + (u - 1)))
                for j in range(8, 13):
                    free = (raw_ready, j - 1) if j < 11 else (zk, j - 10)
                    whole_product(e, tile(n0, 0, j), DK, P if j < 12 else 4 * HEADS, whole_h, False, free)

            def conv_act(e, i, u, j):
                g, n, _ = tile(n0, i, u)
                e.wait_ge(tile_done.sem, n + 1)
                keep_raw(e, g, raws()[u], T, raw_ready)
                e.wait_ge(conv_done.sem, conv_done.at(j + 1))
                dst = region(C, GQ, 9 * T)[:, bass.ds(j * T, T)] if not isinstance(j, int) else qkv[:, j]
                e.activation(dst, cv[u], ACT.Silu).then_inc(silu.sem, 1)

            def act(e):
                e.wait_ge(zeroed.sem, zeroed.at(8))
                with e.Fori(0, 4) as i:
                    for u in range(2):
                        conv_act(e, i, u, i * 2 + u)
                conv_act(e, 4, 0, 8)
                for j in range(9, 13):
                    n = n0 + j
                    e.wait_ge(tile_done.sem, n + 1)
                    if j < 12:
                        e.activation(zz3[:, j - 9], group(n % 2, T), ACT.Silu).then_inc(zk.sem, 1)
                    else:
                        e.activation(abT[0:24, :], group(n % 2, T, 0, 24), ACT.Copy).then_inc(zk.sem, 1)

            def one_conv(e, u, j):
                e.wait_ge(raw_ready.sem, raw_ready.at(j + 1))
                w = [S[:, bass.ds(VCOL["gdn_conv_w"] + s * 9 + j, 1)] if not isinstance(j, int)
                     else vec("gdn_conv_w", s * 9 + j) for s in range(3)]
                conv(e, raws()[u], w, None, cv[u], T, conv_done)
                e.wait_ge(silu.sem, silu.at(j + 1))

            def dve(e):
                e.wait_ge(zeroed.sem, zeroed.at(8))
                with e.Fori(0, 4) as i:
                    chain["dve"].loop(i, 4)
                    for u in range(2):
                        one_conv(e, u, i * 2 + u)
                chain["dve"].end(4)
                one_conv(e, 0, 8)
            ph.parts = dict(sp=sp, pe=pe, act=act, dve=dve, pool=pool)

        def phase_head_norm(l, kind):
            ph = Phase()
            n = 6 if kind == "qk" else 3
            squared = ph.sig("squared", n)
            summed = ph.sig("squares_summed", n)
            root = ph.sig("root_made", n)
            inv = ph.sig("rstd_made", n)
            made = ph.sig("heads_normed", n)
            sq = [region(X, s * T, T) for s in range(2)]
            rt = [region(X, (2 + s) * T, T) for s in range(2)]

            def part(j):
                return qkv[:, j] if kind == "qk" else o3[:, j]

            def act(e):
                for j in range(n + 1):
                    if j < n:
                        if j >= 2:
                            e.wait_ge(summed.sem, summed.at(j - 1))
                        e.activation(sq[j % 2], part(j), ACT.Square).then_inc(squared.sem, 1)
                    if j >= 1:
                        e.wait_ge(summed.sem, summed.at(j))
                        if j >= 3:
                            e.wait_ge(made.sem, made.at(j - 2))
                        e.activation(rt[(j - 1) % 2], group((j - 1) % 2, T), ACT.Sqrt, bias=eps,
                                     scale=1.0 if kind == "qk" else 1.0 / CH).then_inc(root.sem, 1)

            def pe(e):
                for j in range(n):
                    e.wait_ge(squared.sem, squared.at(j + 1))
                    if j >= 2:
                        e.wait_ge(root.sem, root.at(j - 1))
                    for b, (t0, tn) in enumerate(tok(False)):
                        ins = e.matmul(ps[:, (j % 2) * GROUP + b * BANK:(j % 2) * GROUP + b * BANK + tn],
                                       K[:, K_BLOCK:K_BLOCK + P], sq[j % 2][:, t0:t0 + tn], start=True, stop=True)
                    ins.then_inc(summed.sem, 1)

            def dve(e):
                for j in range(n):
                    r = rt[j % 2]
                    e.wait_ge(root.sem, root.at(j + 1))
                    e.reciprocal(r, r).then_inc(inv.sem, 1)
                    e.wait_ge(inv.sem, inv.at(j + 1))
                    if kind == "qk":
                        e.scalar_tensor_tensor(part(j), part(j), CH ** -0.5 if j < 3 else 1.0, r, ALU.mult, ALU.mult)\
                            .then_inc(made.sem, 1)
                    else:
                        chain["dve"].link(e, e.scalar_tensor_tensor(part(j), part(j), gdn_g, r, ALU.mult, ALU.mult))
                        e.tensor_tensor(part(j), part(j), zz3[:, j], ALU.mult).then_inc(made.sem, 1)
            ph.parts = dict(pe=pe, act=act, dve=dve)

        def phase_gates(l):
            ph = Phase()
            abm = ph.sig("gates_turned", 1)
            cut = ph.sig("gates_cut", 2)
            biased = ph.sig("gate_biased", 1)
            absd = ph.sig("gate_abs", 1)
            e1 = ph.sig("gate_exp", 2)
            ln = ph.sig("gate_log", 1)
            sig_ = ph.sig("beta_made", 1)
            sp_ = ph.sig("softplus_made", 1)
            gm = ph.sig("g_made", 1)
            summed = ph.sig("g_summed", 1)
            gk = ph.sig("gc_kept", 2)
            ex = ph.sig("gate_exps", 3)
            be = ph.sig("beta_decay_made", 1)
            NU = N_CHUNK * 2 * PAIRS
            AB = region(X, 0, N_CHUNK * 12)
            ab4 = AB.rearrange("p (n x q) -> p n x q", n=N_CHUNK, x=4)
            t1, t2, t3, t4 = (region(X, 240 + j * NU, NU).rearrange("p (n x q) -> p n x q", n=N_CHUNK, x=2)
                              for j in range(4))
            ea = region(X, 240 + 4 * NU, 6)

            def pe(e):
                for n in range(N_CHUNK):
                    for h in range(2):
                        ins = e.matmul(ps[h * 64:h * 64 + 64, n * 24:n * 24 + 24], abT[0:24, n * CH:n * CH + CH],
                                       ident[0:24, 0:24], start=True, stop=True)
                ins.then_inc(abm.sem, 1)
                e.wait_ge(gm.sem, gm.at(1))
                for h in range(2):
                    r = slice(h * 64, h * 64 + 64)
                    for d in range(2):
                        g = gt5[r, :, d, 0, :]
                        e.matmul(ps[r, BANK + d * 60:BANK + d * 60 + 60], K[r, K_CUM + d * CH:K_CUM + d * CH + CH], g,
                                 start=True, stop=True)
                        ins = e.matmul(ps[r, 2 * BANK + d * 60:2 * BANK + d * 60 + 60], K[r, K_ONES:K_ONES + CH], g,
                                       start=True, stop=True)
                ins.then_inc(summed.sem, 1)

            def act(e):
                e.activation(ea, AL, ACT.Exp).then_inc(e1.sem, 1)
                e.wait_ge(absd.sem, absd.at(1))
                e.activation(t3, t2, ACT.Exp, scale=-1.0).then_inc(e1.sem, 1)
                e.wait_ge(e1.sem, e1.at(2))
                e.activation(t4, t3, ACT.Ln, bias=1.0).then_inc(ln.sem, 1)
                e.activation(gt5[:, :, :, 2, :], ab4[:, :, 2:4, :], ACT.Sigmoid).then_inc(sig_.sem, 1)
                e.wait_ge(gk.sem, gk.at(2))
                e.activation(gt5[:, :, :, 4, :], t1, ACT.Exp).then_inc(ex.sem, 1)
                e.activation(gt5[:, :, :, 5, :], t3, ACT.Exp).then_inc(ex.sem, 1)
                e.activation(gt5[:, :, :, 3, :], gt5[:, :, :, 1, :], ACT.Exp).then_inc(ex.sem, 1)

            def dve(e):
                e.wait_ge(abm.sem, abm.at(1))
                for h in range(2):
                    r = slice(h * 64, h * 64 + 64)
                    v = ps[r, 0:N_CHUNK * 24].rearrange("p (n x q h) -> p n x q h", n=N_CHUNK, x=4, h=2)[:, :, :, :, h]
                    e.tensor_copy(ab4[r], v).then_inc(cut.sem, 1)
                e.wait_ge(cut.sem, cut.at(2))
                dt_ = DT.rearrange("p (x q) -> p x q", x=2).unsqueeze(1).broadcast_to([P, N_CHUNK, 2, PAIRS])
                e.tensor_tensor(t1, ab4[:, :, 0:2, :], dt_, ALU.add).then_inc(biased.sem, 1)
                e.wait_ge(biased.sem, biased.at(1))
                e.scalar_tensor_tensor(t2, t1, -1.0, t1, ALU.mult, ALU.max).then_inc(absd.sem, 1)
                e.wait_ge(ln.sem, ln.at(1))
                e.scalar_tensor_tensor(t1, t1, 0.0, t4, ALU.max, ALU.add).then_inc(sp_.sem, 1)
                e.wait_ge(sp_.sem, sp_.at(1))
                ea_ = ea.rearrange("p (x q) -> p x q", x=2).unsqueeze(1).broadcast_to([P, N_CHUNK, 2, PAIRS])
                chain["dve"].link(e, e.tensor_tensor(t1, t1, ea_, ALU.mult))
                e.tensor_scalar(gt5[:, :, :, 0, :], t1, -1.0, None, ALU.mult).then_inc(gm.sem, 1)
                e.wait_ge(summed.sem, summed.at(1))
                sums = [ps[:, b * BANK:b * BANK + 120].rearrange("p (x n q) -> p n x q", x=2, q=PAIRS) for b in (1, 2)]
                chain["dve"].link(e, e.tensor_copy(gt5[:, :, :, 1, :], sums[0]))
                e.tensor_copy(t3, sums[1]).then_inc(gk.sem, 1)
                e.wait_ge(gk.sem, gk.at(1))
                e.tensor_tensor(t1, t3, gt5[:, :, :, 1, :], ALU.subtract).then_inc(gk.sem, 1)
                e.wait_ge(ex.sem, ex.at(3))
                e.tensor_tensor(gt5[:, :, :, 3, :], gt5[:, :, :, 3, :], gt5[:, :, :, 2, :], ALU.mult).then_inc(be.sem, 1)
            ph.parts = dict(pe=pe, act=act, dve=dve)

        def phase_scan(l):
            ph = Phase()
            NS = N_CHUNK
            U3 = PAIRS * CH
            zeroed = ph.sig("scan_zeroed", 2)
            staged = ph.sig("staged", 2 * NS)
            prods = ph.sig("kk_kq_made", 2 * NS)
            rbs = ph.sig("rows_spread", 2 * NS)
            tms = ph.sig("kv_turned", 2 * NS)
            eg = ph.sig("decay_row_made", 2 * NS)
            decin = ph.sig("decay_arg_made", 2 * NS)
            dec = ph.sig("decay_mat_made", 2 * NS)
            rvw = ph.sig("rhs_made", 2 * NS)
            kqd = ph.sig("kq_decayed", 2 * NS)
            att = ph.sig("a_made", 2 * NS)
            qd = ph.sig("q_decayed", 2 * NS)
            xt0 = ph.sig("xt0_made", 2 * NS)
            am = ph.sig("a_levels", 2 * (LEVELS - 1) * NS)
            x0 = ph.sig("x0_turned", 2 * NS)
            x0k = ph.sig("x0_kept", 2 * NS)
            t1 = ph.sig("ax_made", 2 * (LEVELS - 1) * NS)
            t1k = ph.sig("ax_kept", 2 * (LEVELS - 1) * NS)
            dx = ph.sig("xax_made", 2 * (LEVELS - 1) * NS)
            xup = ph.sig("x_updated", 2 * (LEVELS - 1) * NS)
            uw = ph.sig("uw_made", 2 * NS)
            uwk = ph.sig("uw_kept", 2 * NS)
            ws = ph.sig("ws_made", 2 * NS)
            dl = ph.sig("delta_made", 2 * NS)
            om = ph.sig("o_made", 2 * NS)
            ds_ = ph.sig("ds_made", 2 * NS)
            snew = ph.sig("state_made", 2 * NS)
            oadd = ph.sig("o_added", 2 * NS)
            o = 0

            def buf(n=2 * U3):
                nonlocal o
                r = region(X, o, n)
                o += n
                return r

            def mats(r):
                return r.rearrange("p (d q i) -> p d q i", d=2, q=PAIRS)

            ST = buf(2 * 9 * CH)
            st4 = ST.rearrange("p (d n i) -> p d n i", d=2, n=9)
            GS = buf(36)
            gs4 = GS.rearrange("p (d k q) -> p d k q", d=2, k=6)
            DEC, EG, AT, KQD, QD, T0, XT, XX, T1S, RV, RW, KD, DL, SS, SC = (mats(buf()) for _ in range(15))
            AM = buf(5 * 2 * U3).rearrange("p (m d q i) -> p m d q i", m=5, d=2, q=PAIRS)
            UWb = buf(4 * U3).rearrange("p (d w q i) -> p d w q i", d=2, w=2, q=PAIRS)
            assert o <= DK * T

            def bank(d, b, w=U3, at=0, lo=0, hi=P):
                c = (4 * d + b) * BANK + at
                return ps[lo:hi, c:c + w]

            def bank3(d, b, at=0):
                return bank(d, b, U3, at).rearrange("p (q i) -> p q i", q=PAIRS)

            def each():
                for q in range(PAIRS):
                    for h in range(2):
                        yield q, slice(h * 64, h * 64 + 64)

            def col(k, d):
                return gs4[:, d, k, :].unsqueeze(2).broadcast_to([P, PAIRS, CH])

            def const3(c):
                return K[:, c:c + CH].unsqueeze(1).broadcast_to([P, PAIRS, CH])

            def walk(e, stage):
                def half(d, s, tail, pre):
                    for name, m in HALF:
                        if m:
                            stage(name, m, d, s, None)
                        elif name in TAIL and tail is not None:
                            stage(name, 0, 1 - d, *tail)
                        elif name in PRE and pre is not None:
                            stage(name, 0, 1 - d, *pre)

                def step(s, before, now):
                    half(1, s - 1, (s - 1, before), (s, now))
                    half(0, s, (s - 1, s * -1 + N_CHUNK), (s, s * -1 + (N_CHUNK - 1)))

                for name in PRE:
                    stage(name, 0, 0, 0, LAT_CHUNKS)
                half(0, 0, None, (0, N_CHUNK - 1))
                with e.Fori(0, CTX_CHUNKS - 1) as i:
                    count(e, i)
                    step(i + 1, i + LAT_CHUNKS, i + (LAT_CHUNKS + 1))
                count(e, None, CTX_CHUNKS - 1)
                step(CTX_CHUNKS, N_CHUNK - 1, 0)
                with e.Fori(0, LAT_CHUNKS - 1) as i:
                    count(e, i)
                    step(i + (CTX_CHUNKS + 1), i, i + 1)
                count(e, None, LAT_CHUNKS - 1)
                half(1, NS - 1, (NS - 1, LAT_CHUNKS - 1), None)
                for name in TAIL:
                    stage(name, 0, 1, NS - 1, 0)

            def count(e, i, times=None):
                if e is dve_engine[0] and i is not None:
                    chain["dve"].loop(i, 12)
                elif e is dve_engine[0]:
                    chain["dve"].end(times)

            PRE = ("kq", "rows", "kv", "a", "x0")
            TAIL = ("uw", "ws", "ds", "out")
            HALF = (("t", 1), ("uw", 0), ("x", 1), ("ws", 0), ("t", 2), ("ds", 0), ("x", 2), ("out", 0),
                    ("kq", 0), ("rows", 0), ("t", 3), ("kv", 0), ("x", 3), ("t", 4), ("a", 0), ("x", 4),
                    ("t", 5), ("x0", 0), ("x", 5))
            dve_engine = [None]

            def at(r, d, s):
                return r.at(s * 2 + (d + 1))

            def at_level(r, d, s, m):
                return r.at(s * (2 * (LEVELS - 1)) + (d * (LEVELS - 1) + m))

            def pool(e):
                e.memset(O_OUT, 0.0).then_inc(zeroed.sem, 1)
                e.memset(SS, 0.0).then_inc(zeroed.sem, 1)
                qf = region(C, GQ, 9 * T).rearrange("p (n t) -> p n t", n=9)

                def stage(name, m, d, s, c):
                    if name == "kq":
                        if not (isinstance(s, int) and s == 0):
                            e.wait_ge(tms.sem, at(tms, d, s - 1))
                            e.wait_ge(xt0.sem, at(xt0, d, s - 1))
                            e.wait_ge(am.sem, at_level(am, d, s - 1, LEVELS - 1))
                        e.tensor_copy(st4[:, d], qf[:, :, bass.ds(c * CH, CH)])
                        e.tensor_copy(gs4[:, d].rearrange("p k q -> p (k q)"), GT[:, bass.ds(c * 36 + d * 18, 18)])\
                            .then_inc(staged.sem, 1)
                    elif name == "a":
                        e.wait_ge(staged.sem, at(staged, d, s))
                        e.wait_ge(eg.sem, at(eg, d, s))
                        e.tensor_tensor(QD[:, d], st4[:, d, 0:3], EG[:, d], ALU.mult).then_inc(qd.sem, 1)
                        e.wait_ge(att.sem, at(att, d, s))
                        for m_ in range(1, LEVELS):
                            e.tensor_tensor(AM[:, m_ - 1, d], AT[:, d], const3(K_LEVEL + (m_ * 2 + d) * CH), ALU.mult)\
                                .then_inc(am.sem, 1)
                walk(e, stage)

            def await_(e, *waits):
                if all(isinstance(v, int) for _, v in waits):
                    for r, v in waits:
                        e.wait_ge(r.sem, v)
                    return
                counts = [e.to_reg(v) for _, v in waits]
                e.wait_ge(zeroed.sem, zeroed.at(2))
                for (r, _), v in zip(waits, counts):
                    e.wait_ge(r.sem, v)

            def pe(e):
                e.wait_ge(zeroed.sem, zeroed.at(2))

                def stage(name, m, d, s, c):
                    if name == "kq":
                        if isinstance(s, int) and s == 0:
                            await_(e, (staged, at(staged, d, s)))
                        else:
                            await_(e, (staged, at(staged, d, s)), (snew, at(snew, d, s - 1)), (oadd, at(oadd, d, s - 1)))
                        for q, r in each():
                            ins = e.matmul(bank(d, 0, 2 * CH, q * 2 * CH)[r], st4[r, d, 3 + q, :],
                                           st4[r, d, q:q + 4:3, :], start=True, stop=True)
                        ins.then_inc(prods.sem, 1)
                    elif name == "rows":
                        for q, r in each():
                            e.matmul(bank(d, 1, CH, q * CH)[r], gs4[r, d, 0, q:q + 1].broadcast_to([64, CH]),
                                     K[r, K_CUM + d * CH:K_CUM + d * CH + CH], start=True, stop=True)
                            ins = e.matmul(bank(d, 1, CH, U3 + q * CH)[r], gs4[r, d, 2, q:q + 1].broadcast_to([64, CH]),
                                           K[r, K_ID64:K_ID64 + CH], start=True, stop=True)
                        ins.then_inc(rbs.sem, 1)
                    elif name == "kv":
                        for q, r in each():
                            for w in range(2):
                                ins = e.matmul(bank(d, 2, CH, w * U3 + q * CH)[r], st4[r, d, 3 + 3 * w + q, :],
                                               K[r, K_ID64:K_ID64 + CH], start=True, stop=True)
                        ins.then_inc(tms.sem, 1)
                    elif name == "x0":
                        await_(e, (xt0, at(xt0, d, s)))
                        for q, r in each():
                            ins = e.matmul(bank(d, 3, CH, q * CH)[r], XT[r, d, q, :], K[r, K_ID64:K_ID64 + CH],
                                           start=True, stop=True)
                        ins.then_inc(x0.sem, 1)
                    elif name == "t":
                        if m == 1:
                            await_(e, (am, at_level(am, d, s, 1)), (x0k, at(x0k, d, s)), (kqd, at(kqd, d, s)))
                        else:
                            await_(e, (am, at_level(am, d, s, m)), (xup, at_level(xup, d, s, m - 1)))
                        for q, r in each():
                            ins = e.matmul(bank(d, 0, CH, q * CH)[r], AM[r, m - 1, d, q, :], XX[r, d, q, :],
                                           start=True, stop=True)
                        ins.then_inc(t1.sem, 1)
                    elif name == "x":
                        await_(e, (t1k, at_level(t1k, d, s, m)))
                        for q, r in each():
                            if m < LEVELS - 1:
                                e.matmul(bank(d, 1, CH, q * CH)[r], XT[r, d, q, :], T1S[r, d, q, :],
                                         start=True, stop=True)
                            ins = e.matmul(bank(d, 1, CH, U3 + q * CH)[r], T1S[r, d, q, :], XT[r, d, q, :],
                                           start=True, stop=True)
                        ins.then_inc(dx.sem, 1)
                    elif name == "uw":
                        await_(e, (xup, at_level(xup, d, s, LEVELS - 1)), (rvw, at(rvw, d, s)))
                        for q, r in each():
                            e.matmul(bank(d, 3, CH, q * CH)[r], XT[r, d, q, :], RV[r, d, q, :], start=True, stop=True)
                            ins = e.matmul(bank(d, 3, CH, U3 + q * CH)[r], RW[r, d, q, :], XT[r, d, q, :],
                                           start=True, stop=True)
                        ins.then_inc(uw.sem, 1)
                    elif name == "ws":
                        await_(e, (uwk, at(uwk, d, s)))
                        for q, r in each():
                            ins = e.matmul(bank(d, 0, CH, q * CH)[r], UWb[r, d, 1, q, :], SS[r, d, q, :],
                                           start=True, stop=True)
                        ins.then_inc(ws.sem, 1)
                    elif name == "ds":
                        await_(e, (dl, at(dl, d, s)))
                        for q, r in each():
                            ins = e.matmul(bank(d, 3, CH, q * CH)[r], KD[r, d, q, :], DL[r, d, q, :],
                                           start=True, stop=True)
                        ins.then_inc(ds_.sem, 1)
                        await_(e, (qd, at(qd, d, s)))
                        for q, r in each():
                            e.matmul(bank(d, 1, CH, q * CH)[r], SS[r, d, q, :], QD[r, d, q, :], start=True, stop=False)
                            ins = e.matmul(bank(d, 1, CH, q * CH)[r], DL[r, d, q, :], KQD[r, d, q, :],
                                           start=False, stop=True)
                        ins.then_inc(om.sem, 1)
                walk(e, stage)

            def act(e):
                def stage(name, m, d, s, c):
                    if name == "rows":
                        e.wait_ge(rbs.sem, at(rbs, d, s))
                        e.activation(EG[:, d], bank3(d, 1), ACT.Exp).then_inc(eg.sem, 1)
                    elif name == "kv":
                        e.wait_ge(decin.sem, at(decin, d, s))
                        e.activation(DEC[:, d], DEC[:, d], ACT.Exp).then_inc(dec.sem, 1)
                    elif name == "x0":
                        e.wait_ge(x0.sem, at(x0, d, s))
                        e.activation(XX[:, d], bank3(d, 3), ACT.Copy).then_inc(x0k.sem, 1)
                    elif name == "t":
                        e.wait_ge(t1.sem, at_level(t1, d, s, m))
                        e.activation(T1S[:, d], bank3(d, 0), ACT.Copy).then_inc(t1k.sem, 1)
                    elif name == "uw":
                        e.wait_ge(uw.sem, at(uw, d, s))
                        e.activation(UWb[:, d].rearrange("p w q i -> p (w q i)"), bank(d, 3, 2 * U3), ACT.Copy)\
                            .then_inc(uwk.sem, 1)
                walk(e, stage)

            def dve(e):
                link = chain["dve"].link
                dve_engine[0] = e

                def stage(name, m, d, s, c):
                    later = not (isinstance(s, int) and s == 0)
                    if name == "rows":
                        e.wait_ge(eg.sem, at(eg, d, s))
                        link(e, e.tensor_tensor(DEC[:, d], bank3(d, 1), const3(K_NEG + d * CH), ALU.add))
                        e.tensor_tensor(DEC[:, d], DEC[:, d], col(1, d), ALU.subtract).then_inc(decin.sem, 1)
                    elif name == "kv":
                        e.wait_ge(tms.sem, at(tms, d, s))
                        if later:
                            e.wait_ge(snew.sem, at(snew, d, s - 1))
                        link(e, e.tensor_tensor(RV[:, d], bank3(d, 2, U3), col(2, d), ALU.mult))
                        link(e, e.tensor_tensor(KD[:, d], bank3(d, 2), col(4, d), ALU.mult))
                        e.tensor_tensor(RW[:, d], bank3(d, 2), col(3, d), ALU.mult).then_inc(rvw.sem, 1)
                        link(e, e.tensor_tensor(SC[:, d], SS[:, d], col(5, d), ALU.mult))
                    elif name == "a":
                        kq = bank(d, 0, 2 * U3).rearrange("p (q w i) -> p w q i", q=PAIRS, w=2)
                        e.wait_ge(dec.sem, at(dec, d, s))
                        link(e, e.tensor_tensor(AT[:, d], kq[:, 1], DEC[:, d], ALU.mult))
                        e.tensor_tensor(KQD[:, d], kq[:, 0], DEC[:, d], ALU.mult).then_inc(kqd.sem, 1)
                        e.tensor_tensor(AT[:, d], bank3(d, 1, U3), AT[:, d], ALU.mult).then_inc(att.sem, 1)
                        e.wait_ge(att.sem, at(att, d, s))
                        link(e, e.tensor_tensor(T0[:, d], AT[:, d], const3(K_LEVEL + d * CH), ALU.mult))
                        e.tensor_tensor(XT[:, d], const3(K_ID64), T0[:, d], ALU.subtract).then_inc(xt0.sem, 1)
                    elif name == "x":
                        e.wait_ge(dx.sem, at_level(dx, d, s, m))
                        if m == 1:
                            e.wait_ge(xt0.sem, at(xt0, d, s))
                        if m < LEVELS - 1:
                            e.tensor_tensor(XX[:, d], XX[:, d], bank3(d, 1), ALU.subtract)
                        e.tensor_tensor(XT[:, d], XT[:, d], bank3(d, 1, U3), ALU.subtract).then_inc(xup.sem, 1)
                        e.wait_ge(xup.sem, at_level(xup, d, s, m))
                    elif name == "ws":
                        e.wait_ge(ws.sem, at(ws, d, s))
                        e.tensor_tensor(DL[:, d], UWb[:, d, 0], bank3(d, 0), ALU.subtract).then_inc(dl.sem, 1)
                    elif name == "ds":
                        e.wait_ge(om.sem, at(om, d, s))
                        e.tensor_tensor(SS[:, d], SC[:, d], bank3(d, 3), ALU.add).then_inc(snew.sem, 1)
                        if later or d:
                            e.wait_ge(oadd.sem, oadd.at(s * 2 + d))
                        oo = o3[:, :, bass.ds(c * CH, CH)]
                        e.tensor_tensor(oo, oo, bank3(d, 1), ALU.add).then_inc(oadd.sem, 1)
                walk(e, stage)
            ph.parts = dict(pe=pe, act=act, dve=dve, pool=pool)

        def residual(e, i, u, m, g, which, last, dst=None):
            for t0, tn, v in [(0, SEQ, 0)] + ([] if last else [(SEQ, CTX, 1)]):
                x_ = X[:, bass.ds(m * T + t0, tn)] if not isinstance(m, int) else x3[:, m, t0:t0 + tn]
                gate = S[:, bass.ds((N_VEC + 2 * which + v) + m * 2, 1)]
                ins = e.scalar_tensor_tensor(x_ if dst is None else dst, ps[:, g * GROUP + t0:g * GROUP + t0 + tn],
                                             gate, x_, ALU.mult, ALU.add)
            return ins

        def phase_out(l, last):
            ph = Phase()
            n0 = tiles[0]
            tiles[0] += 8
            ph.ends.append((tile_done.sem, tiles[0]))
            back = ph.sig("x_back", 1, 16)
            added = ph.sig("x_added", 8)
            split = ph.sig("tile_split", 8)
            high = ph.sig("mix_high_made", 8)
            low = ph.sig("mix_low_made", 8)
            src = a["w_out"][l].rearrange("(k p) n -> p k n", p=P)
            mix = [o3[:, j] for j in range(3)] + [mla3[:, j] for j in range(3)] + [hy3[:, j] for j in range(2)]
            width = SEQ if last else T
            parts = [halves(C, FREE + j * T, T) for j in range(8)]
            ring = split_ring(C, FREE + 8 * T)

            def rhs(kk, t0, tn, half):
                return parts[kk][half][:, t0:t0 + tn]

            def pool(e):
                e.dma_start(X[:, :], x_dram).then_inc(back.sem, 16)
                with e.Fori(0, 4) as i:
                    chain["pool"].loop(i, 2)
                    for u in range(2):
                        split_tile(e, tile(n0, i, u), i * 2 + u, DK, P, ring, split)
                chain["pool"].end(4)

            def sp(e):
                for u in range(2):
                    load_tile(e, tile(n0, 0, u), src, u * P, DK, P, split, u)
                with e.Fori(1, 4) as i:
                    for u in range(2):
                        load_tile(e, tile(n0, i, u), src, i * 256 + u * P, DK, P, split, i * 2 + u)

            def act(e):
                for j in range(8):
                    e.activation(parts[j][0][:, 0:width], mix[j][:, 0:width], ACT.Copy).then_inc(high.sem, 1)

            def pe(e):
                e.wait_ge(low.sem, low.at(8))
                for u in range(2):
                    product(e, tile(n0, 0, u), u, DK, P, rhs, last, ring, split)
                with e.Fori(1, 4) as i:
                    for u in range(2):
                        product(e, tile(n0, i, u), i * 2 + u, DK, P, rhs, last, ring, split, (added, i * 2 + (u - 1)))

            def split_mix(e):
                for j in range(8):
                    e.wait_ge(high.sem, high.at(j + 1))
                    e.tensor_tensor(parts[j][1][:, 0:width], mix[j][:, 0:width], parts[j][0][:, 0:width], ALU.subtract)\
                        .then_inc(low.sem, 1)

            def dve(e):
                split_mix(e)
                e.wait_ge(back.sem, back.at(1))
                with e.Fori(0, 4) as i:
                    for u in range(2):
                        g, n, _ = tile(n0, i, u)
                        e.wait_ge(tile_done.sem, n + 1)
                        residual(e, i, u, i * 2 + u, g, 16, last).then_inc(added.sem, 1)
            ph.parts = dict(sp=sp, pe=pe, act=act, dve=dve, pool=pool)

        def phase_ffn_up(l, last):
            ph = Phase()
            n0 = tiles[0]
            assert n0 % 2 == 0 or True
            tiles[0] += 2 * FT
            ph.ends.append((tile_done.sem, tiles[0]))
            width = SEQ if last else T
            zeroed = ph.sig("pads_zeroed", 8)
            raw_ready = ph.sig("raw_ready", FT)
            conv_done = ph.sig("conv_done", FT)
            silu = ph.sig("silu_made", FT)
            act_made = ph.sig("hidden_made", FT)
            high = ph.sig("hidden_high_made", FT)
            low = ph.sig("hidden_low_made", FT)
            split = ph.sig("tile_split", 2 * FT)
            src = a["ffn_w_up"][l].rearrange("(k p) n -> p k n", p=P)
            cv = [region(X, 2 * RAW + s * T, T) for s in range(2)]
            sl = [region(X, 2 * RAW + (2 + s) * T, T) for s in range(2)]

            def pool(e):
                zero_pads(e, zeroed)
                with e.Fori(0, FT) as i:
                    chain["pool"].loop(i, 2)
                    for u in range(2):
                        split_tile(e, tile(n0, i, u), i * 2 + u, DK, P, x_ring, split)
                chain["pool"].end(FT)

            def sp(e):
                with e.Fori(0, FT) as i:
                    load_tile(e, tile(n0, i, 0), src, i * P, DK, P, split, i * 2)
                    load_tile(e, tile(n0, i, 1), src, i * P + D_FF, DK, P, split, i * 2 + 1)

            def pe(e):
                for u in range(2):
                    product(e, tile(n0, 0, u), u, DK, P, h_rhs, last, x_ring, split)
                with e.Fori(1, FT) as i:
                    product(e, tile(n0, i, 0), i * 2, DK, P, h_rhs, last, x_ring, split, (raw_ready, i))
                    product(e, tile(n0, i, 1), i * 2 + 1, DK, P, h_rhs, last, x_ring, split, (act_made, i))

            def act(e):
                e.wait_ge(zeroed.sem, zeroed.at(8))
                with e.Fori(0, FT // 2) as i:
                    for u in range(2):
                        j = i * 2 + u
                        g, n, _ = tile(n0, i, 2 * u, 4)
                        e.wait_ge(tile_done.sem, n + 1)
                        keep_raw(e, g, raws()[u], width, raw_ready)
                        e.wait_ge(conv_done.sem, conv_done.at(j + 1))
                        e.activation(sl[u][:, 0:width], cv[u][:, 0:width], ACT.Silu).then_inc(silu.sem, 1)
                        e.wait_ge(act_made.sem, act_made.at(j + 1))
                        e.activation(cb[:, bass.ds(j * (2 * T), width)], sl[u][:, 0:width], ACT.Copy).then_inc(high.sem, 1)

            def dve(e):
                e.wait_ge(zeroed.sem, zeroed.at(8))
                with e.Fori(0, FT // 2) as i:
                    chain["dve"].loop(i, 4)
                    for u in range(2):
                        j = i * 2 + u
                        e.wait_ge(raw_ready.sem, raw_ready.at(j + 1))
                        w = [S[:, bass.ds(j + (VCOL["ffn_conv_w"] + s * FT), 1)] for s in range(3)]
                        conv(e, raws()[u], w, S[:, bass.ds(j + VCOL["ffn_conv_b"], 1)], cv[u], width, conv_done)
                        e.wait_ge(silu.sem, silu.at(j + 1))
                        g, n, _ = tile(n0, i, 2 * u + 1, 4)
                        e.wait_ge(tile_done.sem, n + 1)
                        e.tensor_tensor(sl[u][:, 0:width], sl[u][:, 0:width], group(g, width), ALU.mult)\
                            .then_inc(act_made.sem, 1)
                        e.wait_ge(act_made.sem, act_made.at(j + 1))
                        e.wait_ge(high.sem, high.at(j + 1))
                        e.tensor_tensor(cb[:, bass.ds(j * (2 * T) + T, width)], sl[u][:, 0:width],
                                        cb[:, bass.ds(j * (2 * T), width)], ALU.subtract).then_inc(low.sem, 1)
                chain["dve"].end(FT // 2)
            ph.parts = dict(sp=sp, pe=pe, act=act, dve=dve, pool=pool)

        def phase_ffn_down(l, last):
            ph = Phase()
            pieces = [(0, 8), (8, 8), (16, FT - 16)]
            loaded = [ph.sig("down_loaded_0", 12, 16), ph.sig("down_loaded_1", 12, 16)]
            split = ph.sig("down_split", 24)
            done = ph.sig("down_done", 8)
            back = ph.sig("x_back", 1, 16)
            added = ph.sig("x_added", 8)
            ring = [[x.rearrange("p (k n) -> p k n", k=FT) for x in halves(H, s * FT * P, FT * P)] for s in range(2)]
            src = a["ffn_w_down"][l].rearrange("(k p) n -> p k n", p=P)
            if last:
                turned = ph.sig("out_turned", 16)
                kept = ph.sig("out_kept", 16)
                stored = [ph.sig("out_stored_0", 4, 16), ph.sig("out_stored_1", 4, 16)]
            xo = [region(H, 2 * FT * P + s * SEQ, SEQ) for s in range(2)]
            xr = [region(H, 2 * FT * P + (2 + s) * SEQ, SEQ).rearrange("p (t f) -> p t f", f=P) for s in range(2)]

            def piece(i, u, c):
                b = 3 * u + c
                return b % 2, i * 6 + b, i * 3 + b // 2

            def pool(e):
                e.dma_start(X[:, :], x_dram).then_inc(back.sem, 16)

                def pair(i, again):
                    for u in range(2):
                        for c, (k0, kn) in enumerate(pieces):
                            g, n, loads = piece(i, u, c)
                            if again and c == 0:
                                copy_waits(e, (loaded[g].sem, loaded[g].at(loads + 1)),
                                           (done.sem, done.at(i * 2 + (u - 1))))
                            else:
                                copy_waits(e, (loaded[g].sem, loaded[g].at(loads + 1)))
                            hi, lo = (x[:, k0:k0 + kn, :] for x in ring[u])
                            chain["pool"].link(e, e.tensor_copy(hi, w3[:, g, 0:kn, :]))
                            e.tensor_tensor(lo, w3[:, g, 0:kn, :], hi, ALU.subtract).then_inc(split.sem, 1)

                pair(0, False)
                with e.Fori(1, 4) as i:
                    chain["pool"].loop_from(i, 6, 1)
                    pair(i, True)
                chain["pool"].end(3)

            def sp(e):
                def pair(i, again):
                    for u in range(2):
                        at = i * 256 + u * P
                        at = at if isinstance(at, int) else e.snap(at)
                        for c, (k0, kn) in enumerate(pieces):
                            g, n, _ = piece(i, u, c)
                            if again or 3 * u + c >= 2:
                                e.wait_ge(split.sem, split.at(n - 1))
                            e.dma_start(w3[:, g, 0:kn, :], src[:, k0:k0 + kn, bass.ds(at, P)]).then_inc(loaded[g].sem, 16)

                pair(0, False)
                with e.Fori(1, 4) as i:
                    pair(i, True)

            def one(e, i, u, free):
                e.wait_ge(split.sem, split.at(i * 6 + (3 * u + 3)))
                if free:
                    e.wait_ge(added.sem, added.at(i * 2 + (u - 1)))
                for b, (t0, tn) in enumerate(tok(last)):
                    for k in range(FT):
                        for q, (w_, r_) in enumerate(HALVES):
                            c = (2 * k + r_) * T + t0
                            ins = e.matmul(ps[:, u * GROUP + b * BANK:u * GROUP + b * BANK + tn], ring[u][w_][:, k, :],
                                           cb[:, c:c + tn], start=(k == 0 and q == 0), stop=(k == FT - 1 and q == 2))
                ins.then_inc(done.sem, 1)

            def turn(e, j, u):
                e.wait_ge(added.sem, added.at(j + 1))
                for half in range(2):
                    if not (isinstance(j, int) and j == 0):
                        e.wait_ge(kept.sem, kept.at(j * 2 + (half - 1)))
                    for q in range(4):
                        b = 4 * half + q
                        ins = e.transpose(ps[:, (6 + half) * BANK + q * P:(6 + half) * BANK + q * P + P],
                                          xo[u][:, b * P:b * P + P], ident)
                    ins.then_inc(turned.sem, 1)

            def pe(e):
                one(e, 0, 0, False)
                one(e, 0, 1, False)
                if last:
                    turn(e, 0, 0)
                with e.Fori(1, 4) as i:
                    one(e, i, 0, True)
                    if last:
                        turn(e, i * 2 - 1, 1)
                    one(e, i, 1, True)
                    if last:
                        turn(e, i * 2, 0)
                if last:
                    turn(e, 7, 1)

            def dve(e):
                e.wait_ge(back.sem, back.at(1))
                with e.Fori(0, 4) as i:
                    for u in range(2):
                        j = i * 2 + u
                        e.wait_ge(done.sem, done.at(j + 1))
                        if last:
                            e.wait_ge(turned.sem, turned_before(j))
                        residual(e, i, u, j, u, 40, last, xo[u] if last else None).then_inc(added.sem, 1)

            def turned_before(j):
                return turned.at(j * 2 - 2)

            def dve_last(e):
                e.wait_ge(back.sem, back.at(1))
                for u in range(2):
                    e.wait_ge(done.sem, done.at(u + 1))
                    residual(e, 0, u, u, u, 40, True, xo[u]).then_inc(added.sem, 1)
                with e.Fori(1, 4) as i:
                    for u in range(2):
                        j = i * 2 + u
                        e.wait_ge(done.sem, done.at(j + 1))
                        e.wait_ge(turned.sem, turned.at(j * 2 - 2))
                        residual(e, i, u, j, u, 40, True, xo[u]).then_inc(added.sem, 1)

            def act(e):
                o_ = out[0].rearrange("(t p) f -> p t f", p=P)

                def one_out(i, u, again):
                    j = i * 2 + u
                    if again:
                        e.wait_ge(stored[u].sem, stored[u].at(i))
                    for half in range(2):
                        e.wait_ge(turned.sem, turned.at(j * 2 + half + 1))
                        e.activation(xr[u][:, 4 * half:4 * half + 4, :],
                                     ps[:, (6 + half) * BANK:(7 + half) * BANK].rearrange("p (t f) -> p t f", f=P),
                                     ACT.Copy).then_inc(kept.sem, 1)
                    e.wait_ge(kept.sem, kept.at(j * 2 + 2))
                    dst = o_[:, :, bass.ds(j * P, P)] if not isinstance(j, int) else o_[:, :, j * P:j * P + P]
                    e.dma_start(dst, xr[u]).then_inc(stored[u].sem, 16)

                one_out(0, 0, False)
                one_out(0, 1, False)
                with e.Fori(1, 4) as i:
                    one_out(i, 0, True)
                    one_out(i, 1, True)
                for u in range(2):
                    e.wait_ge(stored[u].sem, stored[u].at(4))
            ph.parts = dict(sp=sp, pe=pe, dve=dve_last if last else dve, pool=pool)
            if last:
                ph.parts["act"] = act

        phase_input()
        for l in range(DEPTH):
            last = l == DEPTH - 1
            phase_modulation(l)
            phase_norm_mix(l)
            phase_hyena_in(l)
            phase_hyena_filter(l, SEQ, 0)
            phase_hyena_conv(l, SEQ, 0)
            if not last:
                phase_hyena_filter(l, CTX, SEQ)
                phase_hyena_conv(l, CTX, SEQ)
            phase_mla_in(l)
            phase_mla_norm(l)
            phase_mla_heads(l, last)
            phase_gdn_in(l)
            phase_head_norm(l, "qk")
            phase_gates(l)
            phase_scan(l)
            phase_head_norm(l, "out")
            phase_out(l, last)
            phase_norm_ffn(l, last)
            phase_ffn_up(l, last)
            phase_ffn_down(l, last)
        block = ctx.enter_context(nc.Block())

        def run(eng, name):
            for k, ph in enumerate(every):
                if name in ph.parts:
                    settle(eng, k)
                    ph.parts[name](eng)

        @block.sync
        def _(e):
            run(e, "sp")

        @block.tensor
        def _(e):
            run(e, "pe")

        @block.scalar
        def _(e):
            run(e, "act")

        @block.vector
        def _(e):
            run(e, "dve")

        @block.gpsimd
        def _(e):
            run(e, "pool")


_INS = ["x", "c", "ctx", "c_ctx", "ada_w", "ada_b", "mix_norm_g", "w_in", "gdn_conv_w", "gdn_a_log",
        "gdn_dt_bias", "gdn_norm_g", "mla_q_norm_g", "mla_w_uq", "mla_kv_norm_g", "mla_w_ukv",
        "mla_q_head_g", "mla_k_head_g", "hy_conv_w", "hy_conv_b", "hy_w1", "hy_b1", "hy_w2", "hy_b2",
        "hy_w3", "hy_b3", "hy_d", "w_out", "ffn_norm_g", "ffn_w_up", "ffn_conv_w", "ffn_conv_b",
        "ffn_w_down"]


def kernel(**inputs):
    import concourse.bacc as _bacc
    from concourse.bass_utils import run_bass_kernel_spmd as _run

    nc = _bacc.Bacc("TRN2", target_bir_lowering=False, num_devices=1)
    arrays = {n: np.ascontiguousarray(inputs[n]) for n in _INS}
    arrays.update(tables())
    aps = {n: nc.dram_tensor("in_" + n, v.shape, mybir.dt.from_np(v.dtype), kind="ExternalInput").ap()
           for n, v in arrays.items()}
    out = nc.dram_tensor("out_0", (1, SEQ, D), F32, kind="ExternalOutput").ap()
    build(nc, aps, out)
    r = _run(nc, [{"in_" + n: v for n, v in arrays.items()}], core_ids=[0])
    return r.results[0]["out_0"]
```

```python
from contextlib import ExitStack

import numpy as np

import concourse.bass as bass
from concourse import mybir

F32 = mybir.dt.float32
BF16 = mybir.dt.bfloat16
ACT = mybir.ActivationFunctionType
ALU = mybir.AluOpType
AX = mybir.AxisListType

P = 128
D = 1024
DK = D // P
SEQ, CTX = 1024, 256
T = SEQ + CTX
DEPTH = 2
EPS = 1e-6
GRID_W = 64

HEADS = 6
PAIRS = 3
CH = 64
GDN_QKV = 1152
GDN_W = 384
N_CHUNK = T // CH
LAT_CHUNKS, CTX_CHUNKS = SEQ // CH, CTX // CH

QR, KVR, NOPE, ROPE, VD = 256, 128, 64, 32, 64
QK = NOPE + ROPE
HY = 256
HY_EMB, HY_HID = 33, 64
D_FF = 2816
FT = D_FF // P
GDN_IN = GDN_QKV + GDN_W + 4 * HEADS
MLA_COL = GDN_IN
HY_COL = GDN_IN + QR + KVR + ROPE
P_IN = HY_COL + 3 * HY

HALVES = ((0, 0), (0, 1), (1, 0))

LEVELS = 6
NEG = -1e30
TWO_PI = 2 * np.pi
RAW = T + 4
RAW_AT = ((0, SEQ, 0), (SEQ, CTX, SEQ + 2))
GROUP = 1536
FIRST_MOD = 16
MOD_AT = PAIRS * P
BANK = 512
SEL = P

K_ID = 0
K_BLOCK = K_ID + P
K_ONES = K_BLOCK + P
K_CUM = K_ONES + P
K_LEVEL = K_CUM + 2 * CH
K_NEG = K_LEVEL + LEVELS * 2 * CH
K_ROT = K_NEG + 2 * CH
K_ID64 = K_ROT + QK
K_T0 = K_ID64 + CH
K_TN = K_T0 + 1
K_DELTA = K_TN + SEQ // P + CTX // P
K_EPS = K_DELTA + HY
K_N = K_EPS + 1

VEC_A = (("ada_b", 48), ("mix_norm_g", 8), ("ffn_norm_g", 8), ("gdn_conv_w", 27), ("hy_conv_w", 18),
         ("hy_conv_b", 6), ("hy_d", 2), ("mla_q_norm_g", 2), ("mla_kv_norm_g", 1))
VEC_B = (("ffn_conv_w", 66), ("ffn_conv_b", 22), ("c", 8), ("c_ctx", 8))
VCOL, _at = {}, 0
for _n, _k in VEC_A + VEC_B:
    VCOL[_n] = _at
    _at += _k
N_VEC = _at
N_ROWS = len(VEC_A) + len(VEC_B) + 6 + 4
N_VEC_A = sum(k for _, k in VEC_A)
N_VEC_B = sum(k for _, k in VEC_B)
SMALL = N_VEC + 96 + 2 * 2 * 8 + 12 + 8 + 16 + 96


def tables():
    k = np.zeros((P, K_N), np.float32)
    k[:, K_ID:K_ID + P] = np.eye(P)
    for h in range(2):
        k[h * 64:h * 64 + 64, K_BLOCK + h * 64:K_BLOCK + h * 64 + 64] = 1
    k[:, K_ONES:K_ONES + P] = 1
    j, i = np.meshgrid(np.arange(CH), np.arange(CH), indexing="ij")
    for d in range(2):
        before = (i >= j) if d == 0 else (i <= j)
        k[:, K_CUM + d * CH:K_CUM + d * CH + CH] = np.tile(before, (2, 1))
        k[:, K_NEG + d * CH:K_NEG + d * CH + CH] = np.tile(np.where(before, 0, NEG), (2, 1))
        for l in range(LEVELS):
            b = 1 << l
            same = (i // (2 * b)) == (j // (2 * b))
            first, second = (j, i) if d == 0 else (i, j)
            m = same & ((first // b) % 2 == 0) & ((second // b) % 2 == 1)
            c = K_LEVEL + (l * 2 + d) * CH
            k[:, c:c + CH] = np.tile(m, (2, 1))
    half = ROPE // 2
    for r in range(half):
        k[NOPE + half + r, K_ROT + NOPE + r] = -1
        k[NOPE + r, K_ROT + NOPE + half + r] = 1
    k[:, K_ID64:K_ID64 + CH] = np.tile(np.eye(CH), (2, 1))
    k[:, K_T0] = 1
    k[0, K_T0] = 0
    lo, hi = np.log(1e-2) / 1.5, np.log(1e-2) / 0.3
    k[:, K_DELTA:K_DELTA + HY] = np.abs(np.linspace(lo, hi, HY, dtype=np.float32))
    k[:, K_EPS] = EPS
    select = np.zeros((P, 6 * SEL), np.float32)
    for j in range(6):
        for h in range(2):
            select[h * 64:h * 64 + 64, j * SEL + 2 * j + h] = 1
    spread = np.concatenate([select[:, j * SEL:j * SEL + SEL].T for j in range(6)], axis=1)
    out = {"k_table": k, "k_select": select, "k_spread": np.ascontiguousarray(spread)}
    at = 0
    for name, length in (("lat", SEQ), ("ctx", CTX)):
        t = np.arange(length, dtype=np.float32)
        tn = t / np.float32(max(length - 1, 1))
        k[:, K_TN + at:K_TN + at + length // P] = -tn.reshape(-1, P).T
        at += length // P
        bands = np.linspace(1e-4, 15, 16, dtype=np.float32)
        ang = (np.float32(2.0 * np.pi) * t[:, None] * bands[None, :] / np.float32(length)).astype(np.float32)
        z = np.concatenate([tn[:, None], np.cos(ang), np.sin(ang)], axis=-1)
        out["k_z_" + name] = np.ascontiguousarray(z.T.astype(np.float32))
        th = np.pi * np.outer(np.arange(length), 2 * np.arange(length) + 1) / (2 * length)
        cs = np.stack([np.cos(th), np.sin(th)])
        out["k_dft_" + name] = cs.astype(np.float32)
        out["k_idft_" + name] = np.ascontiguousarray((cs / length).transpose(0, 2, 1).astype(np.float32))
    rows = SEQ // GRID_W
    row = np.repeat(np.arange(rows, dtype=np.float32), GRID_W)
    col = np.tile(np.arange(GRID_W, dtype=np.float32), rows)
    inv = (np.float32(10000.0) ** (-np.arange(0, 16, 2, dtype=np.float32) / 16)).astype(np.float32)
    ang = np.concatenate([row[:, None] * inv, col[:, None] * inv], axis=-1).T
    rope = np.zeros((2, QK, SEQ), np.float32)
    rope[0, :NOPE] = 1
    rope[0, NOPE:] = np.tile(np.cos(ang), (2, 1))
    rope[1, NOPE:] = np.tile(np.sin(ang), (2, 1))
    out["k_rope"] = rope
    return out


class Signal:

    def __init__(self, sem):
        self.sem, self.total = sem, 0


class Ref:

    def __init__(self, signal, n, unit):
        self.sem, self.base, self.unit = signal.sem, signal.total, unit
        signal.total += n * unit
        self.end = signal.total

    def at(self, k):
        return k * self.unit + self.base


def build(nc, a, out):
    with ExitStack() as ctx:
        def sb(name, n):
            return ctx.enter_context(nc.sbuf_tensor(name, [P, n], F32))

        X = sb("X", DK * T)
        H = sb("H", DK * T)
        C = sb("C", FT * T)
        W = sb("W", 2 * DK * P)
        K = sb("K", K_N)
        S = sb("S", SMALL)
        ps = ctx.enter_context(nc.psum_tensor("ps", [P, 8 * BANK], F32))
        x_dram = nc.dram_tensor("x_stream", [P, DK * T], F32, kind="Internal").ap()

        signals = {}
        every = []

        def signal(name):
            if name not in signals:
                signals[name] = Signal(ctx.enter_context(nc.semaphore(name)))
            return signals[name]

        class Phase:

            def __init__(self):
                self.ends = []
                self.parts = {}
                self.uses_w = False
                every.append(self)

            def sig(self, name, n, unit=1):
                r = Ref(signal(name), n, unit)
                self.ends.append((r.sem, r.end))
                return r

        tile_done = signal("tile_done")
        w_loaded = [signal("w_loaded_0"), signal("w_loaded_1")]
        tiles = [0]

        x3 = X[:, :].rearrange("p (k t) -> p k t", k=DK)
        h3 = H[:, :].rearrange("p (k t) -> p k t", k=DK)
        w3 = W[:, :].rearrange("p (s k n) -> p s k n", s=2, k=DK)
        ident = K[:, K_ID:K_ID + P]
        eps = K[:, K_EPS:K_EPS + 1]
        mod = S[:, N_VEC:N_VEC + 96].rearrange("p (m v) -> p m v", v=2)
        gain = S[:, N_VEC + 96:N_VEC + 128].rearrange("p (w k v) -> p w k v", w=2, v=2)
        AL = S[:, N_VEC + 128:N_VEC + 134]
        DT = S[:, N_VEC + 134:N_VEC + 140]
        gdn_g = S[:, N_VEC + 140:N_VEC + 141]
        q_g = S[0:QK, N_VEC + 141:N_VEC + 142]
        k_g = S[0:QK, N_VEC + 142:N_VEC + 143]
        b1 = S[0:HY_HID, N_VEC + 143:N_VEC + 144]
        b2 = S[0:HY_HID, N_VEC + 144:N_VEC + 145]
        inv_norm = S[:, N_VEC + 145:N_VEC + 147]
        c_silu = S[:, N_VEC + 148:N_VEC + 164].rearrange("p (k v) -> p k v", v=2)
        next_mod = S[:, N_VEC + 164:N_VEC + 260].rearrange("p (m v) -> p m v", v=2)

        def vec(name, j=0):
            c = VCOL[name] + j
            return S[:, c:c + 1]

        def region(t, at, n):
            return t[:, at:at + n]

        class Chain:

            def __init__(self, name):
                self.s = signal(name)
                self.base, self.c, self.i, self.per, self.first = 0, 0, None, 0, 0

            def link(self, eng, ins):
                self.c += 1
                ins.then_inc(self.s.sem, 1)
                v = self.base + self.c if self.i is None else self.i * self.per + (self.base + self.c)
                eng.wait_ge(self.s.sem, v)

            def loop(self, i, per):
                self.base, self.c = self.base + self.c, 0
                self.i, self.per = i, per

            def loop_from(self, i, per, first):
                self.base, self.c = self.base + self.c - first * per, 0
                self.i, self.per, self.first = i, per, first

            def end(self, times):
                assert self.c == self.per, (self.c, self.per)
                self.base, self.c, self.i = self.base + self.per * (times + self.first), 0, None
                self.first = 0

        hb, cb = H[:, :].bitcast(BF16), C[:, :].bitcast(BF16)

        def halves(t, at, n):
            b = t[:, at:at + n].bitcast(BF16)
            return b[:, 0:n], b[:, n:2 * n]

        def split_ring(t, at):
            return [[x.rearrange("p (k n) -> p k n", k=DK) for x in halves(t, at + s * D, D)] for s in range(2)]

        chain = {e: Chain(e + "_own") for e in ("dve", "act", "pool")}

        def tok(last):
            return [(0, BANK), (BANK, BANK)] + ([] if last else [(SEQ, CTX)])

        def group(g, n, lo=0, hi=P):
            return ps[lo:hi, g * GROUP:g * GROUP + n]

        def tile(base, i=0, u=0, per=2):
            b = base + u
            return b % 2, i * per + b, i * (per // 2) + b // 2

        def load_tile(sp, num, src, col, k, width, split=None, j=0):
            slot, n, _ = num
            c = col if isinstance(col, int) else sp.snap(col)
            if split is not None and not (isinstance(j, int) and j < 2):
                sp.wait_ge(split.sem, split.at(j - 1))
            elif split is None and not (isinstance(n, int) and n < 2):
                sp.wait_ge(tile_done.sem, n - 1)
            sp.dma_start(w3[:, slot, 0:k, 0:width], src[:, :, bass.ds(c, width)]).then_inc(w_loaded[slot].sem, 16)

        def copy_waits(pool, *waits):
            counts = [v if isinstance(v, int) else pool.to_reg(v) for _, v in waits]
            pool.wait_ge(signal("table_loaded").sem, 16)
            for (sem, _), v in zip(waits, counts):
                pool.wait_ge(sem, v)

        def split_tile(pool, num, j, k, width, ring, split):
            g, n, loads = num
            if isinstance(j, int) and j < 2:
                copy_waits(pool, (w_loaded[g].sem, loads * 16 + 16))
            else:
                copy_waits(pool, (w_loaded[g].sem, loads * 16 + 16), (tile_done.sem, n - 1))
            hi, lo = (x[:, 0:k, 0:width] for x in ring[g])
            chain["pool"].link(pool, pool.tensor_copy(hi, w3[:, g, 0:k, 0:width]))
            pool.tensor_tensor(lo, w3[:, g, 0:k, 0:width], hi, ALU.subtract).then_inc(split.sem, 1)

        def whole_product(pe, num, k, width, rhs, last, free=None, lo=0):
            g, n, loads = num
            pe.wait_ge(w_loaded[g].sem, loads * 16 + 16)
            if free is not None:
                pe.wait_ge(free[0].sem, free[0].at(free[1]))
            for b, (t0, tn) in enumerate(tok(last)):
                for kk in range(k):
                    ins = pe.matmul(ps[lo:lo + width, g * GROUP + b * BANK:g * GROUP + b * BANK + tn],
                                    w3[:, g, kk, 0:width], rhs(kk, t0, tn), start=(kk == 0), stop=(kk == k - 1))
            ins.then_inc(tile_done.sem, 1)

        def whole_h(kk, t0, tn):
            return h3[:, kk, t0:t0 + tn]

        def product(pe, num, j, k, width, rhs, last, ring, split, free=None, lo=0):
            g, n, _ = num
            pe.wait_ge(split.sem, split.at(j + 1))
            if free is not None:
                pe.wait_ge(free[0].sem, free[0].at(free[1]))
            for b, (t0, tn) in enumerate(tok(last)):
                for kk in range(k):
                    for q, (w_, r_) in enumerate(HALVES):
                        ins = pe.matmul(ps[lo:lo + width, g * GROUP + b * BANK:g * GROUP + b * BANK + tn],
                                        ring[g][w_][:, kk, 0:width], rhs(kk, t0, tn, r_),
                                        start=(kk == 0 and q == 0), stop=(kk == k - 1 and q == 2))
            ins.then_inc(tile_done.sem, 1)

        def h_rhs(kk, t0, tn, half):
            c = (2 * kk + half) * T + t0
            return hb[:, c:c + tn]

        x_ring = split_ring(X, 8 * D)

        def keep_raw(act, g, raw, width, ready):
            for t0, tn, r0 in RAW_AT:
                if t0 < width:
                    ins = act.activation(raw[:, r0 + 1:r0 + 1 + tn], ps[:, g * GROUP + t0:g * GROUP + t0 + tn], ACT.Copy)
            ins.then_inc(ready.sem, 1)

        def conv(dve, raw, w, bias, dst, width, done):
            for step in range(3):
                for t0, tn, r0 in RAW_AT:
                    if t0 >= width:
                        continue
                    src = raw[:, r0 + step:r0 + step + tn]
                    o = dst[:, t0:t0 + tn]
                    if step == 0 and bias is None:
                        ins = dve.tensor_scalar(o, src, w[0], None, ALU.mult)
                    elif step == 0:
                        ins = dve.tensor_scalar(o, src, w[0], bias, ALU.mult, ALU.add)
                    else:
                        ins = dve.scalar_tensor_tensor(o, src, w[step], o, ALU.mult, ALU.add)
                if step < 2:
                    chain["dve"].link(dve, ins)
            ins.then_inc(done.sem, 1)

        def settle(eng, k):
            if k:
                for sem, end in every[k - 1].ends:
                    eng.wait_ge(sem, end)

        def phase_input():
            ph = Phase()
            table = ph.sig("table_loaded", 1, 16)
            rows = ph.sig("rows_loaded", 10, 16)
            turned = ph.sig("rows_turned", 20)
            kept = ph.sig("rows_kept", 20)
            ring = [region(C, s * D, D) for s in range(10)]

            def sp(e):
                e.dma_start(K[:, :], a["k_table"]).then_inc(table.sem, 16)
                for n in range(10):
                    src = a["x"][0, n * P:n * P + P, :] if n < 8 else a["ctx"][0, (n - 8) * P:(n - 7) * P, :]
                    if n:
                        e.wait_ge(rows.sem, rows.at(n))
                    e.dma_start(ring[n], src).then_inc(rows.sem, 16)

            def pe(e):
                e.wait_ge(table.sem, table.at(1))
                for n in range(10):
                    e.wait_ge(rows.sem, rows.at(n + 1))
                    for half in range(2):
                        c = 2 * n + half
                        if c >= 4:
                            e.wait_ge(kept.sem, kept.at(c - 3))
                        for q in range(4):
                            k = half * 4 + q
                            ins = e.transpose(ps[:, (c % 4) * BANK + q * P:(c % 4) * BANK + q * P + P],
                                              ring[n][:, k * P:k * P + P], ident)
                        ins.then_inc(turned.sem, 1)

            def act(e):
                for n in range(10):
                    for half in range(2):
                        c = 2 * n + half
                        e.wait_ge(turned.sem, turned.at(c + 1))
                        e.activation(x3[:, half * 4:half * 4 + 4, n * P:n * P + P],
                                     ps[:, (c % 4) * BANK:(c % 4 + 1) * BANK].rearrange("p (k t) -> p k t", k=4),
                                     ACT.Copy).then_inc(kept.sem, 1)
            ph.parts = dict(sp=sp, pe=pe, act=act)

        def phase_modulation(l):
            ph = Phase()
            NC = FIRST_MOD // 4 if l == 0 else 0
            rows = ph.sig("vectors_loaded", N_ROWS, 16)
            turned = ph.sig("vectors_turned", 1)
            kept = ph.sig("vectors_kept", 2)
            moved = ph.sig("mod_made", 2 if l == 0 else 3)
            if l == 0:
                silu = ph.sig("c_silu", 1)
                loaded = [ph.sig("ada_loaded_0", NC // 2, 16), ph.sig("ada_loaded_1", NC // 2, 16)]
                used = ph.sig("ada_used", NC)
            rows_a = region(C, 0, P)
            rows_b = region(C, P, P)
            cT = S[:, VCOL["c"]:VCOL["c"] + 16].rearrange("p (v k) -> p k v", v=2)
            cS = c_silu
            ring = [region(C, 1024 + s * 4096, 4096).rearrange("p (k n) -> p k n", k=DK) for s in range(2)]

            def pool(e):
                at = 0
                for dst, names in ((rows_a, VEC_A), (rows_b, VEC_B)):
                    at = 0
                    for name, k in names:
                        src = a[name] if name == "c_ctx" else a[name][0 if name == "c" else l]
                        src = src.rearrange("w (k p) -> (w k) p", p=P) if len(src.shape) == 2 \
                            else src.rearrange("(k p) -> k p", p=P)
                        e.dma_start(dst[at:at + k, :], src).then_inc(rows.sem, 16)
                        at += k
                for h in range(2):
                    r = slice(h * 64, h * 64 + 64)
                    for dst, name in ((AL, "gdn_a_log"), (DT, "gdn_dt_bias")):
                        src = a[name][l].rearrange("d (p h) -> h d p", h=2)[h:h + 1]
                        e.dma_start(dst[r, :].rearrange("q (d p) -> q d p", d=2),
                                    src.broadcast_to([64, 2, PAIRS]), allow_slow_non_contiguous=True)\
                            .then_inc(rows.sem, 16)
                    e.dma_start(gdn_g[r, :], a["gdn_norm_g"][l].rearrange("(p o) -> p o", o=1)).then_inc(rows.sem, 16)
                for dst, name in ((q_g, "mla_q_head_g"), (k_g, "mla_k_head_g")):
                    e.dma_start(dst, a[name][l].rearrange("(p o) -> p o", o=1)).then_inc(rows.sem, 16)
                for dst, name in ((b1, "hy_b1"), (b2, "hy_b2")):
                    e.dma_start(dst, a[name][l].rearrange("(p o) -> p o", o=1)).then_inc(rows.sem, 16)

            def sp(e):
                w = a["ada_w"][l].rearrange("(k p) n -> p k n", p=P)
                for n in range(NC):
                    if n >= 2:
                        e.wait_ge(used.sem, used.at(n - 1))
                    e.dma_start(ring[n % 2], w[:, :, n * 512:n * 512 + 512]).then_inc(loaded[n % 2].sem, 16)

            def pe(e):
                e.wait_ge(rows.sem, rows.at(N_ROWS))
                e.transpose(ps[:, 0:N_VEC_A], rows_a[0:N_VEC_A, :], ident[0:N_VEC_A, 0:N_VEC_A])
                e.transpose(ps[:, P:P + N_VEC_B], rows_b[0:N_VEC_B, :], ident[0:N_VEC_B, 0:N_VEC_B])\
                    .then_inc(turned.sem, 1)
                if l:
                    return
                e.wait_ge(silu.sem, silu.at(1))
                for n in range(NC):
                    e.wait_ge(loaded[n % 2].sem, loaded[n % 2].at(n // 2 + 1))
                    for q in range(4):
                        c = 4 * n + q
                        for k in range(DK):
                            ins = e.matmul(ps[:, BANK + 2 * c:BANK + 2 * c + 2], ring[n % 2][:, k, q * P:q * P + P],
                                           cS[:, k, :], start=(k == 0), stop=(k == DK - 1))
                    ins.then_inc(used.sem, 1)

            def act(e):
                e.wait_ge(kept.sem, kept.at(2))
                e.activation(cS, cT, ACT.Silu).then_inc(silu.sem, 1)

            def dve(e):
                e.wait_ge(turned.sem, turned.at(1))
                e.tensor_copy(S[:, 0:N_VEC_A], ps[:, 0:N_VEC_A]).then_inc(kept.sem, 1)
                e.tensor_copy(S[:, N_VEC_A:N_VEC], ps[:, P:P + N_VEC_B]).then_inc(kept.sem, 1)
                e.wait_ge(kept.sem, kept.at(2))
                n = FIRST_MOD if l == 0 else 48
                if l == 0:
                    e.wait_ge(used.sem, used.at(NC))
                made = ps[:, BANK:BANK + 2 * n].rearrange("p (m v) -> p m v", v=2) if l == 0 else next_mod
                e.tensor_tensor(mod[:, 0:n, :], made, S[:, 0:n].unsqueeze(2).broadcast_to([P, n, 2]), ALU.add)\
                    .then_inc(moved.sem, 1)
                e.wait_ge(moved.sem, moved.at(1))
                for w in range(1 if l == 0 else 2):
                    make_gain(e, w).then_inc(moved.sem, 1)
            ph.parts = dict(pe=pe, dve=dve, pool=pool)
            if l == 0:
                ph.parts.update(sp=sp, act=act)

        def make_gain(e, w):
            name, sc = (("mix_norm_g", 8), ("ffn_norm_g", 32))[w]
            g = S[:, VCOL[name]:VCOL[name] + 8]
            return e.scalar_tensor_tensor(gain[:, w], mod[:, sc:sc + 8, :], 1.0,
                                          g.unsqueeze(2).broadcast_to([P, 8, 2]), ALU.add, ALU.mult)

        def phase_modulation_rest():
            ph = Phase()
            kept = ph.sig("mod_rest_kept", 3)

            def dve(e):
                n = 48 - FIRST_MOD
                rest = ps[:, 3 * BANK + MOD_AT:3 * BANK + MOD_AT + 2 * n].rearrange("p (m v) -> p m v", v=2)
                e.tensor_tensor(mod[:, FIRST_MOD:48, :], rest,
                                S[:, FIRST_MOD:48].unsqueeze(2).broadcast_to([P, n, 2]), ALU.add).then_inc(kept.sem, 1)
                e.wait_ge(kept.sem, kept.at(1))
                make_gain(e, 1).then_inc(kept.sem, 1)
                e.tensor_copy(next_mod, ps[:, 7 * BANK + MOD_AT:7 * BANK + MOD_AT + 96].rearrange("p (m v) -> p m v", v=2))\
                    .then_inc(kept.sem, 1)
            ph.parts = dict(dve=dve)


        def phase_norm_mix(l):
            ph = Phase()
            which, last = 0, False
            width = SEQ if last else T
            squared = ph.sig("squared", DK)
            summed = ph.sig("squares_summed", DK)
            root = ph.sig("root_made", 1)
            inv = ph.sig("rstd_made", 1)
            scaled = ph.sig("h_scaled", DK)
            made = ph.sig("h_made", DK * (1 if last else 2))
            saved = ph.sig("x_saved", 1, 16)
            sq = [region(C, 0, T), region(C, T, T)]
            rt, rs = region(C, 2 * T, T), region(C, 3 * T, T)
            segs = [(0, SEQ, 0)] + ([] if last else [(SEQ, CTX, 1)])
            shift = 0 if which == 0 else 24

            def pool(e):
                e.dma_start(x_dram, X[:, :]).then_inc(saved.sem, 16)

            def act(e):
                for k in range(DK):
                    if k >= 2:
                        e.wait_ge(summed.sem, summed.at(k - 1))
                    e.activation(sq[k % 2][:, 0:width], x3[:, k, 0:width], ACT.Square).then_inc(squared.sem, 1)
                e.wait_ge(summed.sem, summed.at(DK))
                e.activation(rt[:, 0:width], group(0, width), ACT.Sqrt, bias=eps, scale=1.0 / D).then_inc(root.sem, 1)
                for k in range(DK):
                    e.wait_ge(scaled.sem, scaled.at(k + 1))
                    for t0, tn, v in segs:
                        e.activation(h3[:, k, t0:t0 + tn], h3[:, k, t0:t0 + tn], ACT.Identity,
                                     bias=mod[:, shift + k, v:v + 1]).then_inc(made.sem, 1)

            def pe(e):
                for k in range(DK):
                    e.wait_ge(squared.sem, squared.at(k + 1))
                    for b, (t0, tn) in enumerate(tok(last)):
                        ins = e.matmul(ps[:, b * BANK:b * BANK + tn], K[:, K_ONES:K_ONES + P], sq[k % 2][:, t0:t0 + tn],
                                       start=(k == 0), stop=(k == DK - 1))
                    ins.then_inc(summed.sem, 1)

            def dve(e):
                e.wait_ge(root.sem, root.at(1))
                e.reciprocal(rs[:, 0:width], rt[:, 0:width]).then_inc(inv.sem, 1)
                e.wait_ge(inv.sem, inv.at(1))
                for k in range(DK):
                    for t0, tn, v in segs:
                        ins = e.scalar_tensor_tensor(h3[:, k, t0:t0 + tn], x3[:, k, t0:t0 + tn],
                                                     gain[:, which, k, v:v + 1], rs[:, t0:t0 + tn], ALU.mult, ALU.mult)
                    ins.then_inc(scaled.sem, 1)
            ph.parts = dict(pe=pe, act=act, dve=dve, pool=pool)

        def phase_norm_ffn(l, last):
            ph = Phase()
            which = 1
            width = SEQ if last else T
            squared = ph.sig("squared", DK)
            summed = ph.sig("squares_summed", DK)
            root = ph.sig("root_made", 1)
            inv = ph.sig("rstd_made", 1)
            scaled = ph.sig("h_scaled", DK)
            made = ph.sig("h_high_made", DK)
            lows = ph.sig("h_low_made", DK)
            saved = ph.sig("x_saved", 1, 16)
            sq = [region(C, 0, T), region(C, T, T)]
            rt, rs = region(C, 2 * T, T), region(C, 3 * T, T)
            tmp = [region(C, (4 + s) * T, T) for s in range(3)]
            segs = [(0, SEQ, 0)] + ([] if last else [(SEQ, CTX, 1)])
            shift = 0 if which == 0 else 24

            def pool(e):
                e.dma_start(x_dram, X[:, :]).then_inc(saved.sem, 16)

            def act(e):
                for k in range(DK):
                    if k >= 2:
                        e.wait_ge(summed.sem, summed.at(k - 1))
                    e.activation(sq[k % 2][:, 0:width], x3[:, k, 0:width], ACT.Square).then_inc(squared.sem, 1)
                e.wait_ge(summed.sem, summed.at(DK))
                e.activation(rt[:, 0:width], group(0, width), ACT.Sqrt, bias=eps, scale=1.0 / D).then_inc(root.sem, 1)
                for k in range(DK):
                    e.wait_ge(scaled.sem, scaled.at(k + 1))
                    for t0, tn, v in segs:
                        ins = e.activation(h_rhs(k, t0, tn, 0), tmp[k % 3][:, t0:t0 + tn], ACT.Identity,
                                           bias=mod[:, shift + k, v:v + 1])
                    ins.then_inc(made.sem, 1)

            def pe(e):
                for k in range(DK):
                    e.wait_ge(squared.sem, squared.at(k + 1))
                    for b, (t0, tn) in enumerate(tok(last)):
                        ins = e.matmul(ps[:, b * BANK:b * BANK + tn], K[:, K_ONES:K_ONES + P], sq[k % 2][:, t0:t0 + tn],
                                       start=(k == 0), stop=(k == DK - 1))
                    ins.then_inc(summed.sem, 1)

            def dve(e):
                e.wait_ge(root.sem, root.at(1))
                e.reciprocal(rs[:, 0:width], rt[:, 0:width]).then_inc(inv.sem, 1)
                e.wait_ge(inv.sem, inv.at(1))
                for k in range(DK + 1):
                    if k < DK:
                        if k >= 3:
                            e.wait_ge(lows.sem, lows.at(k - 2))
                        for t0, tn, v in segs:
                            ins = e.scalar_tensor_tensor(tmp[k % 3][:, t0:t0 + tn], x3[:, k, t0:t0 + tn],
                                                         gain[:, which, k, v:v + 1], rs[:, t0:t0 + tn], ALU.mult, ALU.mult)
                        ins.then_inc(scaled.sem, 1)
                    if k:
                        e.wait_ge(scaled.sem, scaled.at(k))
                        e.wait_ge(made.sem, made.at(k))
                        for t0, tn, v in segs:
                            ins = e.scalar_tensor_tensor(h_rhs(k - 1, t0, tn, 1), tmp[(k - 1) % 3][:, t0:t0 + tn],
                                                         mod[:, shift + k - 1, v:v + 1], h_rhs(k - 1, t0, tn, 0),
                                                         ALU.add, ALU.subtract)
                        ins.then_inc(lows.sem, 1)
            ph.parts = dict(pe=pe, act=act, dve=dve, pool=pool)

        HY_OUT = region(C, 0, 2 * T)
        MLA_OUT = region(C, 2 * T, 3 * T)
        FREE = 5 * T
        hy3 = HY_OUT.rearrange("p (c t) -> p c t", c=2)
        mla3 = MLA_OUT.rearrange("p (c t) -> p c t", c=3)

        def raws():
            return [region(X, s * RAW, RAW) for s in range(2)]

        def zero_pads(e, sigref):
            for s in range(2):
                for c in (0, SEQ + 1, SEQ + 2, RAW - 1):
                    e.memset(raws()[s][:, c:c + 1], 0.0).then_inc(sigref.sem, 1)

        zt = region(C, FREE, 2 * T)
        z3 = zt.rearrange("p (c t) -> p c t", c=2)

        def phase_hyena_in(l):
            ph = Phase()
            ph.uses_w = True
            n0 = tiles[0]
            tiles[0] += 6
            ph.ends.append((tile_done.sem, tiles[0]))
            zeroed = ph.sig("pads_zeroed", 8)
            raw_ready = ph.sig("raw_ready", 6)
            conv_done = ph.sig("conv_done", 6)
            z_made = ph.sig("z_made", 2)
            order = [0, 2, 4, 1, 3, 5]
            tmp = region(X, 2 * RAW, T)
            src = a["w_in"][l].rearrange("(k p) n -> p k n", p=P)

            def pool(e):
                zero_pads(e, zeroed)

            def sp(e):
                for j, t in enumerate(order):
                    c = HY_COL + t * P
                    load_tile(e, tile(n0, 0, j), src, c, DK, P)

            def pe(e):
                for j in range(6):
                    whole_product(e, tile(n0, 0, j), DK, P, whole_h, False, (raw_ready, j - 1) if j >= 2 else None)

            def act(e):
                e.wait_ge(zeroed.sem, zeroed.at(8))
                for j in range(6):
                    n = n0 + j
                    e.wait_ge(tile_done.sem, n + 1)
                    if j >= 2:
                        e.wait_ge(conv_done.sem, conv_done.at(j - 1))
                    keep_raw(e, n % 2, raws()[j % 2], T, raw_ready)

            def dve(e):
                e.wait_ge(zeroed.sem, zeroed.at(8))
                for j, t in enumerate(order):
                    e.wait_ge(raw_ready.sem, raw_ready.at(j + 1))
                    kind, c = t // 2, t % 2
                    dst = hy3[:, c] if kind == 0 else (z3[:, c] if kind == 1 else tmp)
                    w = [vec("hy_conv_w", s * 6 + t) for s in range(3)]
                    conv(e, raws()[j % 2], w, vec("hy_conv_b", t), dst, T, conv_done)
                    if kind == 2:
                        e.wait_ge(conv_done.sem, conv_done.at(j + 1))
                        e.tensor_tensor(z3[:, c], z3[:, c], tmp, ALU.mult).then_inc(z_made.sem, 1)
                        e.wait_ge(z_made.sem, z_made.at(c + 1))
            ph.parts = dict(sp=sp, pe=pe, act=act, dve=dve, pool=pool)

        def phase_hyena_filter(l, length, at):
            ph = Phase()
            NT = length // P
            name = "lat" if length == SEQ else "ctx"
            HN = min(BANK, length)
            NH = length // HN
            ld = ph.sig("filter_loaded", 6, 16)
            ones = ph.sig("ones_row", 1)
            l1 = ph.sig("layer1", NH)
            s1 = ph.sig("sin1", NH)
            l2 = ph.sig("layer2", NH)
            s2 = ph.sig("sin2", NH)
            l3 = ph.sig("layer3", NT)
            dec = ph.sig("decay_made", NT)
            hh = ph.sig("filter_made", NT)
            ab = ph.sig("filter_abs", NT)
            nrm = ph.sig("norm_summed", NT)
            zt_ = ph.sig("z_turned", NT)
            zk = ph.sig("z_kept", NT)
            fin = ph.sig("inv_norm_made", 1)
            o = FREE + 2 * T
            zf = region(C, o, SEQ)
            h1 = region(C, o + SEQ, SEQ)
            h2 = region(C, o + 2 * SEQ, SEQ)
            t1 = region(C, o + 3 * SEQ, SEQ)
            t2 = region(C, o + 4 * SEQ, SEQ)
            o += 5 * SEQ
            w1 = region(C, o, HY_HID)
            w2 = region(C, o + 64, HY_HID)
            w3_ = region(C, o + 128, 2 * HY)
            o += 128 + 512
            hf = [region(C, o + s * 512, 512) for s in range(2)]
            ha = [region(C, o + 1024 + s * 512, 512) for s in range(2)]
            dc = [region(C, o + 2048 + s * 256, 256) for s in range(2)]
            nsum = region(C, o + 2560, 4)
            assert o + 2564 <= FT * T
            ezo = region(X, 0, NT * 768).rearrange("p (t w c) -> p t w c", w=3, c=HY)

            def pool(e):
                e.dma_start(zf[0:HY_EMB, 0:length], a["k_z_" + name]).then_inc(ld.sem, 16)
                e.dma_start(w1[0:HY_EMB, :], a["hy_w1"][l]).then_inc(ld.sem, 16)
                e.dma_start(w2[0:HY_HID, :], a["hy_w2"][l]).then_inc(ld.sem, 16)
                e.dma_start(w3_[0:HY_HID, :], a["hy_w3"][l]).then_inc(ld.sem, 16)
                e.dma_start(w3_[HY_HID:HY_HID + 1, :], a["hy_b3"][l:l + 1, :]).then_inc(ld.sem, 16)
                e.dma_start(t2[0:1, 0:1], a["c"][0:1, 0:1]).then_inc(ld.sem, 16)
                e.memset(h2[HY_HID:HY_HID + 1, 0:length], 1.0).then_inc(ones.sem, 1)

            def pe(e):
                e.wait_ge(ld.sem, ld.at(6))
                e.wait_ge(ones.sem, ones.at(1))
                for b in range(NH):
                    e.matmul(ps[0:64, b * BANK:b * BANK + HN], w1[0:HY_EMB, :], zf[0:HY_EMB, b * HN:b * HN + HN],
                             start=True, stop=True).then_inc(l1.sem, 1)
                for b in range(NH):
                    e.wait_ge(s1.sem, s1.at(b + 1))
                    e.matmul(ps[0:64, (2 + b) * BANK:(2 + b) * BANK + HN], w2[0:HY_HID, :],
                             h1[0:HY_HID, b * HN:b * HN + HN], start=True, stop=True).then_inc(l2.sem, 1)
                e.wait_ge(s2.sem, s2.at(NH))
                for t in range(NT):
                    if t >= 2:
                        e.wait_ge(hh.sem, hh.at(t - 1))
                    e.matmul(ps[:, (t % 2) * BANK:(t % 2) * BANK + 512], h2[0:HY_HID + 1, t * P:t * P + P],
                             w3_[0:HY_HID + 1, :], start=True, stop=True).then_inc(l3.sem, 1)
                    if t >= 2:
                        e.wait_ge(zk.sem, zk.at(t - 1))
                    for c in range(2):
                        ins = e.transpose(ps[:, (4 + t % 2) * BANK + c * P:(4 + t % 2) * BANK + c * P + P],
                                          z3[:, c, at + t * P:at + t * P + P], ident)
                    ins.then_inc(zt_.sem, 1)
                    if t >= 1:
                        sum_tile(e, t - 1)
                sum_tile(e, NT - 1)

            def sum_tile(e, t):
                e.wait_ge(ab.sem, ab.at(t + 1))
                for c in range(4):
                    ins = e.matmul(ps[:, 6 * BANK + c * 8 + t:6 * BANK + c * 8 + t + 1],
                                   ha[t % 2][:, c * P:c * P + P], K[:, K_ONES:K_ONES + 1], start=True, stop=True)
                ins.then_inc(nrm.sem, 1)

            def act(e):
                e.wait_ge(ld.sem, ld.at(6))
                for w, (pre, post, bank, hout) in enumerate(((sm1, s1, 0, h1), (sm2, s2, 2, h2))):
                    for b in range(NH):
                        e.wait_ge(pre.sem, pre.at(b + 1))
                        e.activation(hout[0:HY_HID, b * HN:b * HN + HN], t1[0:HY_HID, b * HN:b * HN + HN], ACT.Sin)\
                            .then_inc(post.sem, 1)
                for t in range(NT):
                    if t >= 2:
                        e.wait_ge(hh.sem, hh.at(t - 1))
                    c = K_TN + (0 if length == SEQ else SEQ // P) + t
                    e.activation(dc[t % 2], K[:, K_DELTA:K_DELTA + HY], ACT.Exp, scale=K[:, c:c + 1])\
                        .then_inc(dec.sem, 1)
                    e.wait_ge(zt_.sem, zt_.at(t + 1))
                    e.activation(ezo[:, t, 1, :], ps[:, (4 + t % 2) * BANK:(4 + t % 2) * BANK + HY], ACT.Copy)\
                        .then_inc(zk.sem, 1)
                    e.wait_ge(hh.sem, hh.at(t + 1))
                    if t >= 2:
                        e.wait_ge(nrm.sem, nrm.at(t - 1))
                    e.activation(ha[t % 2], hf[t % 2], ACT.Abs).then_inc(ab.sem, 1)

            sm1 = ph.sig("reduced1", NH)
            sm2 = ph.sig("reduced2", NH)
            ez = ph.sig("ezo_made", NT)

            def dve(e):
                link = chain["dve"].link
                MAGIC = 1.5 * 2.0 ** 23
                A1 = 6.28125
                A2 = float(np.float32(TWO_PI - A1))
                A3 = float(TWO_PI - A1 - A2)
                for w, (pre, post, bank, bias) in enumerate(((l1, sm1, 0, b1), (l2, sm2, 2, b2))):
                    for b in range(NH):
                        sl = slice(b * HN, b * HN + HN)
                        u, r = t1[0:HY_HID, sl], t2[0:HY_HID, sl]
                        e.wait_ge(pre.sem, pre.at(b + 1))
                        if w:
                            e.wait_ge(s1.sem, s1.at(b + 1))
                        link(e, e.tensor_scalar(u, ps[0:64, (bank + b) * BANK:(bank + b) * BANK + HN], bias, None, ALU.add))
                        link(e, e.tensor_scalar(r, u, float(1 / TWO_PI), MAGIC, ALU.mult, ALU.add))
                        link(e, e.tensor_scalar(r, r, -MAGIC, None, ALU.add))
                        link(e, e.scalar_tensor_tensor(u, r, -A1, u, ALU.mult, ALU.add))
                        link(e, e.scalar_tensor_tensor(u, r, -A2, u, ALU.mult, ALU.add))
                        link(e, e.scalar_tensor_tensor(u, r, -A3, u, ALU.mult, ALU.add))
                        e.tensor_scalar(u, u, 3.1415925, -3.1415925, ALU.min, ALU.max).then_inc(post.sem, 1)
                for t in range(NT):
                    e.wait_ge(l3.sem, l3.at(t + 1))
                    e.wait_ge(dec.sem, dec.at(t + 1))
                    if t >= 2:
                        e.wait_ge(ab.sem, ab.at(t - 1))
                    o_, i_ = hf[t % 2].rearrange("p (w c) -> p w c", w=2), \
                        ps[:, (t % 2) * BANK:(t % 2) * BANK + 512].rearrange("p (w c) -> p w c", w=2)
                    ins = e.tensor_tensor(o_, i_, dc[t % 2].unsqueeze(1).broadcast_to([P, 2, HY]), ALU.mult)
                    if t == 0:
                        link(e, ins)
                        ins = e.tensor_scalar(o_[:, 1, :], o_[:, 1, :], K[:, K_T0:K_T0 + 1], None, ALU.mult)
                    ins.then_inc(hh.sem, 1)
                    e.wait_ge(hh.sem, hh.at(t + 1))
                    e.tensor_tensor(ezo[:, t, 0, :], o_[:, 0, :], o_[:, 1, :], ALU.add)
                    e.tensor_tensor(ezo[:, t, 2, :], o_[:, 0, :], o_[:, 1, :], ALU.subtract).then_inc(ez.sem, 1)
                e.wait_ge(nrm.sem, nrm.at(NT))
                link(e, e.tensor_reduce(nsum, ps[:, 6 * BANK:6 * BANK + 32].rearrange("p (c t) -> p c t", t=8)[:, :, 0:NT],
                                        AX.X, ALU.add))
                link(e, e.tensor_tensor(nsum[:, 0:2], nsum[:, 0:2], nsum[:, 2:4], ALU.add))
                e.reciprocal(inv_norm, nsum[:, 0:2]).then_inc(fin.sem, 1)
            ph.parts = dict(pe=pe, act=act, dve=dve, pool=pool)

        def phase_hyena_conv(l, length, at):
            ph = Phase()
            ph.uses_w = True
            NT = length // P
            name = "lat" if length == SEQ else "ctx"
            HN = min(BANK, length)
            NH = length // HN
            n0 = tiles[0]
            tiles[0] += 4 * NT
            ph.ends.append((tile_done.sem, tiles[0]))
            spec = ph.sig("spectrum_kept", NT)
            yy = ph.sig("products_made", NT)
            fin = ph.sig("hyena_out", 2)
            ezo = region(X, 0, NT * 768).rearrange("p (t w c) -> p t w c", w=3, c=HY)
            o = FREE + 2 * T
            y = region(C, o, NT * 512).rearrange("p (f r c) -> p f r c", r=2, c=HY)
            o += 4096
            sp_ = [region(C, o + s * 1024, 1024).rearrange("p (r c) -> p r c", r=4) for s in range(2)]
            ta = region(C, o + 2048, 256)
            tmp = region(C, o + 2304, T)

            def sp(e):
                for f in range(NT):
                    for r in range(2):
                        src = a["k_dft_" + name][r].rearrange("(k p) n -> p k n", p=P)
                        load_tile(e, tile(n0, 0, 2 * f + r), src, f * P, NT, P)
                for f in range(NT):
                    for r in range(2):
                        n = n0 + 2 * NT + 2 * f + r
                        e.wait_ge(tile_done.sem, n - 1)
                        e.dma_start(W[:, (n % 2) * D:(n % 2) * D + length], a["k_idft_" + name][r, f * P:f * P + P, :])\
                            .then_inc(w_loaded[n % 2].sem, 16)

            def pe(e):
                for f in range(NT):
                    if f >= 2:
                        e.wait_ge(spec.sem, spec.at(f - 1))
                    for r in range(2):
                        n = n0 + 2 * f + r
                        e.wait_ge(w_loaded[n % 2].sem, (n // 2 + 1) * 16)
                        b = 2 * (f % 2) + r
                        for t in range(NT):
                            ins = e.matmul(ps[:, b * BANK:b * BANK + 512], w3[:, n % 2, t, :],
                                           ezo[:, t, r:r + 2, :], start=(t == 0), stop=(t == NT - 1))
                        ins.then_inc(tile_done.sem, 1)
                for f in range(NT):
                    for r in range(2):
                        n = n0 + 2 * NT + 2 * f + r
                        e.wait_ge(w_loaded[n % 2].sem, (n // 2 + 1) * 16)
                        e.wait_ge(yy.sem, yy.at(f + 1))
                        for c in range(2):
                            for b in range(NH):
                                ins = e.matmul(ps[:, (4 + 2 * c + b) * BANK:(4 + 2 * c + b) * BANK + HN],
                                               y[:, f, r, c * P:c * P + P],
                                               W[:, (n % 2) * D + b * HN:(n % 2) * D + b * HN + HN],
                                               start=(f == 0 and r == 0), stop=(f == NT - 1 and r == 1))
                        ins.then_inc(tile_done.sem, 1)

            def act(e):
                for f in range(NT):
                    n = n0 + 2 * f + 1
                    e.wait_ge(tile_done.sem, n + 1)
                    if f >= 2:
                        e.wait_ge(yy.sem, yy.at(f - 1))
                    b = 2 * (f % 2)
                    e.activation(sp_[f % 2], ps[:, b * BANK:b * BANK + 1024].rearrange("p (r c) -> p r c", r=4),
                                 ACT.Copy).then_inc(spec.sem, 1)

            def dve(e):
                link = chain["dve"].link
                for f in range(NT):
                    e.wait_ge(spec.sem, spec.at(f + 1))
                    hr, zr, zs, hs = (sp_[f % 2][:, i] for i in range(4))
                    link(e, e.tensor_tensor(ta, zs, hs, ALU.mult))
                    link(e, e.tensor_tensor(y[:, f, 0], zr, hr, ALU.mult))
                    link(e, e.tensor_tensor(y[:, f, 0], y[:, f, 0], ta, ALU.subtract))
                    link(e, e.tensor_tensor(ta, zr, hs, ALU.mult))
                    link(e, e.tensor_tensor(y[:, f, 1], zs, hr, ALU.mult))
                    e.tensor_tensor(y[:, f, 1], y[:, f, 1], ta, ALU.add).then_inc(yy.sem, 1)
                    e.wait_ge(yy.sem, yy.at(f + 1))
                e.wait_ge(tile_done.sem, tiles_end)
                for c in range(2):
                    t_ = tmp[:, 0:length]
                    zz, oo = z3[:, c, at:at + length], hy3[:, c, at:at + length]
                    link(e, e.tensor_scalar(t_, zz, vec("hy_d", c), None, ALU.mult))
                    link(e, e.scalar_tensor_tensor(t_, ps[:, (4 + 2 * c) * BANK:(4 + 2 * c) * BANK + length],
                                                   inv_norm[:, c:c + 1], t_, ALU.mult, ALU.add))
                    e.tensor_tensor(oo, oo, t_, ALU.mult).then_inc(fin.sem, 1)
                    e.wait_ge(fin.sem, fin.at(c + 1))
            tiles_end = tiles[0]
            ph.parts = dict(sp=sp, pe=pe, act=act, dve=dve)

        CQ = region(C, FREE, 2 * T).rearrange("p (k t) -> p k t", k=2)
        CKV = region(C, FREE + 2 * T, T)
        KRAW = region(C, FREE + 3 * T, T)
        ATT = FREE + 4 * T

        def phase_mla_in(l):
            ph = Phase()
            ph.uses_w = True
            n0 = tiles[0]
            tiles[0] += 4
            ph.ends.append((tile_done.sem, tiles[0]))
            kept = ph.sig("latents_kept", 4)
            src = a["w_in"][l].rearrange("(k p) n -> p k n", p=P)

            def sp(e):
                for j in range(4):
                    c = MLA_COL + j * P
                    w = P if j < 3 else ROPE
                    load_tile(e, tile(n0, 0, j), src, c, DK, w)

            def pe(e):
                for j in range(4):
                    whole_product(e, tile(n0, 0, j), DK, P if j < 3 else ROPE, whole_h, False,
                            (kept, j - 1) if j >= 2 else None, lo=0 if j < 3 else NOPE)

            def act(e):
                for j in range(4):
                    n = n0 + j
                    e.wait_ge(tile_done.sem, n + 1)
                    dst = (CQ[:, 0], CQ[:, 1], CKV, KRAW[NOPE:QK, :])[j]
                    src_ = group(n % 2, T) if j < 3 else group(n % 2, T, NOPE, QK)
                    e.activation(dst, src_, ACT.Copy).then_inc(kept.sem, 1)
            ph.parts = dict(sp=sp, pe=pe, act=act)

        def phase_mla_norm(l):
            ph = Phase()
            squared = ph.sig("squared", 3)
            summed = ph.sig("squares_summed", 2)
            root = ph.sig("root_made", 2)
            inv = ph.sig("rstd_made", 2)
            made = ph.sig("latents_normed", 3)
            sq = [region(X, s * T, T) for s in range(3)]
            rt = [region(X, (3 + s) * T, T) for s in range(2)]
            src = (CQ[:, 0], CQ[:, 1], CKV)

            def act(e):
                for j in range(3):
                    e.activation(sq[j], src[j], ACT.Square).then_inc(squared.sem, 1)
                for w, r in enumerate((QR, KVR)):
                    e.wait_ge(summed.sem, summed.at(w + 1))
                    e.activation(rt[w], group(w, T), ACT.Sqrt, bias=eps, scale=1.0 / r).then_inc(root.sem, 1)

            def pe(e):
                for w, js in enumerate(((0, 1), (2,))):
                    e.wait_ge(squared.sem, squared.at(js[-1] + 1))
                    for b, (t0, tn) in enumerate(tok(False)):
                        for j in js:
                            ins = e.matmul(ps[:, w * GROUP + b * BANK:w * GROUP + b * BANK + tn],
                                           K[:, K_ONES:K_ONES + P], sq[j][:, t0:t0 + tn],
                                           start=(j == js[0]), stop=(j == js[-1]))
                    ins.then_inc(summed.sem, 1)

            def dve(e):
                for w, js in enumerate(((0, 1), (2,))):
                    e.wait_ge(root.sem, root.at(w + 1))
                    e.reciprocal(rt[w], rt[w]).then_inc(inv.sem, 1)
                    e.wait_ge(inv.sem, inv.at(w + 1))
                    for j in js:
                        g = vec("mla_q_norm_g", j) if j < 2 else vec("mla_kv_norm_g")
                        e.scalar_tensor_tensor(src[j], src[j], g, rt[w], ALU.mult, ALU.mult).then_inc(made.sem, 1)
            ph.parts = dict(pe=pe, act=act, dve=dve)

        def phase_mla_heads(l, last):
            ph = Phase()
            NQ = 8 if last else 10
            SCALE = float(QK) ** -0.5
            HD = HEADS
            steps = [(b * BANK, BANK, kt, 6 + b, b) for b in range(2) for kt in range(10)]
            if not last:
                steps += [(SEQ, CTX, kt, 6, 2) for kt in (8, 9)]
            NS, NB = len(steps), steps[-1][4] + 1
            PREP_AT = {0: 0, 1: 1, 3: 2, 5: 3, 12: 4, 15: 5}
            rope_ld = ph.sig("rope_loaded", 2, 16)
            wl = ph.sig("pair_w_loaded", PAIRS, 64)
            ready = ph.sig("head_buffers_ready", 3)
            proj = ph.sig("head_projected", 2 * HD)
            kept = ph.sig("head_kept", 2 * HD)
            squared = ph.sig("head_squared", 2 * HD)
            summed = ph.sig("head_summed", 2 * HD)
            rooted = ph.sig("head_root", 2 * HD)
            inv = ph.sig("head_rstd", 2 * HD)
            normed = ph.sig("head_normed", 2 * HD)
            turned = ph.sig("head_turned", 2 * HD)
            sined = ph.sig("head_sined", 2 * HD)
            cosed = ph.sig("head_cosed", 2 * HD)
            roped = ph.sig("head_roped", 2 * HD)
            vproj = ph.sig("values_projected", PAIRS)
            vkept = ph.sig("values_kept", PAIRS)
            scored = ph.sig("scored", NQ * HD)
            maxed = ph.sig("maxed", NQ * HD)
            rowed = ph.sig("maxima_rowed", HD)
            rowkept = ph.sig("maxima_kept", HD)
            keyed = ph.sig("scored_by_key", NS * HD)
            exped = ph.sig("exped", NS * HD + 1)
            onormed = ph.sig("attention_normed", NB * HD + 1)
            mixed = ph.sig("values_mixed", NS * HD)
            oinv = ph.sig("sum_inverted", NB * HD)
            o = ATT
            Q = [region(C, o + j * T, T) for j in range(2)]
            Kh = [region(C, o + (2 + j) * T, T) for j in range(2)]
            SQ0, SQ1, RT0, RT1, QRAW = (region(C, o + (4 + j) * T, T) for j in range(5))
            o += 9 * T
            cos, sin = region(C, o, SEQ), region(C, o + SEQ, SEQ)
            o += 2 * SEQ
            TM = region(C, o, SEQ)
            o += SEQ
            assert o <= FT * T
            V = region(X, 0, 10 * 4 * VD).rearrange("p (t w v) -> p t w v", w=4, v=VD)
            PT = [region(X, 2 * T + s * BANK, BANK) for s in range(4)]
            RB = [region(X, 4 * T + s * BANK, BANK) for s in range(3)]
            wq = [region(X, 6 * T + s * 192, 192).rearrange("p (k n) -> p k n", k=2) for s in range(2)]
            wkv = region(X, 6 * T + 384, 256).rearrange("p (h n) -> p h n", h=2)
            st = region(X, 6 * T + 640, 16)
            raws_, sqs, rts = (QRAW, KRAW), (SQ0, SQ1), (RT0, RT1)

            def blocks(t):
                return (0, T) if t < 8 else (SEQ, CTX)

            def pool(e):
                e.memset(V[:, :, 1:3, :], 1.0).then_inc(ready.sem, 1)
                for u in range(2):
                    e.wait_ge(ready.sem, ready.at(u + 1))
                    e.memset(Kh[u][QK:P, :], 0.0).then_inc(ready.sem, 1)
                e.wait_ge(ready.sem, ready.at(3))
                e.memset(Kh[0][QK:QK + 1, :], 1.0).then_inc(exped.sem, 1)
                e.wait_ge(exped.sem, exped.at(1))
                e.memset(Kh[1][QK:QK + 1, :], 1.0).then_inc(onormed.sem, 1)

            def sp(e):
                for r, t_ in enumerate((cos, sin)):
                    e.dma_start(t_[0:QK, :], a["k_rope"][r]).then_inc(rope_ld.sem, 16)
                uq = a["mla_w_uq"][l].rearrange("(k p) n -> p k n", p=P)
                ukv = a["mla_w_ukv"][l]

                def load(u, cq, ckv):
                    e.dma_start(wq[u], uq[:, :, bass.ds(cq, QK)]).then_inc(wl.sem, 16)
                    e.dma_start(wkv[:, u], ukv[:, bass.ds(ckv, 2 * VD)]).then_inc(wl.sem, 16)

                for u in range(2):
                    load(u, u * QK, u * 2 * VD)
                for i in range(1, PAIRS):
                    e.wait_ge(proj.sem, proj.at(i * 4))
                    for u in range(2):
                        load(u, (2 * i + u) * QK, (2 * i + u) * 2 * VD)

            def every_head(prep, main):
                for stage in range(6):
                    prep(stage, 0, 0, 0)

                def pair(i, final):
                    main(i, 0, i * 2, lambda stage: prep(stage, i * 2 + 1, 1, i))
                    main(i, 1, i * 2 + 1, (lambda stage: None) if final
                         else (lambda stage: prep(stage, i * 2 + 2, 0, i + 1)))
                return pair

            def pe(e):
                e.wait_ge(rope_ld.sem, rope_ld.at(2))
                e.wait_ge(exped.sem, exped.at(1))
                e.wait_ge(onormed.sem, onormed.at(1))

                def prep(stage, h, u, pair):
                    j = stage % 2
                    if stage < 2:
                        if stage == 0:
                            e.wait_ge(wl.sem, wl.at(pair + 1))
                        else:
                            e.wait_ge(kept.sem, kept.at(h * 2 + 1))
                        for b, (t0, tn) in enumerate(tok(False)):
                            c = GROUP + b * BANK
                            if stage == 0:
                                for k in range(2):
                                    ins = e.matmul(ps[0:QK, c:c + tn], wq[u][:, k, :], CQ[:, k, t0:t0 + tn],
                                                   start=(k == 0), stop=(k == 1))
                            else:
                                ins = e.matmul(ps[0:NOPE, c:c + tn], wkv[:, u, 0:NOPE], CKV[:, t0:t0 + tn],
                                               start=True, stop=True)
                        ins.then_inc(proj.sem, 1)
                    elif stage < 4:
                        if j == 0:
                            e.wait_ge(kept.sem, kept.at(h * 2 + 2))
                        else:
                            e.wait_ge(rooted.sem, rooted.at(h * 2 + 1))
                        e.wait_ge(squared.sem, squared.at(h * 2 + j + 1))
                        for b, (t0, tn) in enumerate(tok(False)):
                            ins = e.matmul(ps[0:QK, GROUP + b * BANK:GROUP + b * BANK + tn],
                                           K[0:QK, K_ONES:K_ONES + QK], sqs[j][0:QK, t0:t0 + tn], start=True, stop=True)
                        ins.then_inc(summed.sem, 1)
                    else:
                        if j == 0:
                            e.wait_ge(rooted.sem, rooted.at(h * 2 + 2))
                        else:
                            e.wait_ge(sined.sem, sined.at(h * 2 + 1))
                        e.wait_ge(normed.sem, normed.at(h * 2 + j + 1))
                        for b in range(2):
                            ins = e.matmul(ps[0:QK, GROUP + b * BANK:GROUP + b * BANK + BANK], K[0:QK, K_ROT:K_ROT + QK],
                                           (Q, Kh)[j][u][0:QK, b * BANK:b * BANK + BANK], start=True, stop=True)
                        ins.then_inc(turned.sem, 1)

                def score(t, u):
                    k0, kn = blocks(t)
                    c = (t + 1) % 2 * GROUP
                    for b in range(0, kn, BANK):
                        n = min(BANK, kn - b)
                        ins = e.matmul(ps[:, c + b:c + b + n], Q[u][0:QK, t * P:t * P + P],
                                       Kh[u][0:QK, k0 + b:k0 + b + n], start=True, stop=True)
                    ins.then_inc(scored.sem, 1)

                def row(t, h):
                    e.wait_ge(maxed.sem, maxed.at(h * NQ + t + 1))
                    if t == 0:
                        e.wait_ge(onormed.sem, onormed.at(h * NB + 1))
                    c = 6 * BANK + t * P if t < 8 else 2 * BANK + (t - 8) * P
                    ins = e.matmul(ps[QK:P, c:c + P], st[:, t:t + 1].broadcast_to([P, P - QK]), ident,
                                   start=True, stop=True)
                    if t == NQ - 1:
                        ins.then_inc(rowed.sem, 1)

                def by_key(s, u, h):
                    q0, n, kt, _, _ = steps[s]
                    if s >= 3:
                        e.wait_ge(exped.sem, exped.at(h * NS + s - 1))
                    e.matmul(ps[:, s % 3 * BANK:s % 3 * BANK + n], Kh[u][:, kt * P:kt * P + P], Q[u][:, q0:q0 + n],
                             start=True, stop=True).then_inc(keyed.sem, 1)

                def main(i, u, h, next_):
                    if u == 0:
                        e.wait_ge(exped.sem, exped.at(h * NS + 1))
                        for t in range(10):
                            ins = e.matmul(ps[:, t * P:t * P + P], CKV[:, t * P:t * P + P], wkv[:, :, NOPE:NOPE + VD],
                                           start=True, stop=True)
                        ins.then_inc(vproj.sem, 1)
                    e.wait_ge(roped.sem, roped.at(h * 2 + 2))
                    for t in range(NQ):
                        if t == 1 and u == 0:
                            e.wait_ge(vkept.sem, vkept.at(i + 1))
                        elif t == 1:
                            e.wait_ge(exped.sem, exped.at(h * NS + 1))
                        elif t >= 2:
                            e.wait_ge(maxed.sem, maxed.at(h * NQ + t - 1))
                        score(t, u)
                        if t >= 2:
                            row(t - 2, h)
                    row(NQ - 2, h)
                    row(NQ - 1, h)
                    next_(0)
                    e.wait_ge(rowkept.sem, rowkept.at(h + 1))
                    for s in range(3):
                        by_key(s, u, h)
                    for s, (_, n, kt, bank, b) in enumerate(steps):
                        e.wait_ge(exped.sem, exped.at(h * NS + s + 2))
                        if b == 2 and kt == 8:
                            e.wait_ge(onormed.sem, onormed.at(h * NB + 2))
                        first = s == 0 or steps[s - 1][4] != b
                        final = s == NS - 1 or steps[s + 1][4] != b
                        e.matmul(ps[:, bank * BANK:bank * BANK + n],
                                 V[:, kt, 2 * u:2 * u + 2, :].rearrange("p w v -> p (w v)"), PT[s % 4][:, 0:n],
                                 start=first, stop=final).then_inc(mixed.sem, 1)
                        if s + 3 < NS:
                            by_key(s + 3, u, h)
                        if PREP_AT.get(s):
                            next_(PREP_AT[s])

                pair = every_head(prep, main)
                with e.Fori(0, PAIRS - 1) as i:
                    pair(i, False)
                pair(PAIRS - 1, True)

            def act(e):
                def prep(stage, h, u, pair):
                    j = stage % 2
                    if stage < 2:
                        e.wait_ge(proj.sem, proj.at(h * 2 + j + 1))
                        n = (QK, NOPE)[j]
                        e.activation(raws_[j][0:n, :], group(1, T, 0, n), ACT.Copy).then_inc(kept.sem, 1)
                        e.wait_ge(kept.sem, kept.at(h * 2 + j + 1))
                        e.activation(sqs[j][0:QK, :], raws_[j][0:QK, :], ACT.Square).then_inc(squared.sem, 1)
                    elif stage < 4:
                        e.wait_ge(summed.sem, summed.at(h * 2 + j + 1))
                        e.activation(rts[j][0:QK, :], group(1, T, 0, QK), ACT.Sqrt, bias=eps[0:QK, :], scale=1.0 / QK)\
                            .then_inc(rooted.sem, 1)

                def main(i, u, h, next_):
                    if u == 0:
                        e.wait_ge(vproj.sem, vproj.at(i + 1))
                        e.activation(V[:, :, 0:4:3, :], group(0, T).rearrange("p (t w v) -> p t w v", w=2, v=VD), ACT.Copy)\
                            .then_inc(vkept.sem, 1)
                    e.wait_ge(rowed.sem, rowed.at(h + 1))
                    ins = e.activation(Q[u][QK:P, 0:SEQ], ps[QK:P, 6 * BANK:8 * BANK], ACT.Copy, scale=-1.0)
                    if not last:
                        ins = e.activation(Q[u][QK:P, SEQ:T], ps[QK:P, 2 * BANK:2 * BANK + CTX], ACT.Copy, scale=-1.0)
                    ins.then_inc(rowkept.sem, 1)

                    for s, (_, n, _, _, b) in enumerate(steps):
                        e.wait_ge(keyed.sem, keyed.at(h * NS + s + 1))
                        if s >= 4:
                            e.wait_ge(mixed.sem, mixed.at(h * NS + s - 3))
                        e.activation(PT[s % 4][:, 0:n], ps[:, s % 3 * BANK:s % 3 * BANK + n], ACT.Exp, scale=SCALE)\
                            .then_inc(exped.sem, 1)
                        if s - 2 in PREP_AT:
                            next_(PREP_AT[s - 2])

                pair = every_head(prep, main)
                with e.Fori(0, PAIRS - 1) as i:
                    pair(i, False)
                pair(PAIRS - 1, True)

            def dve(e):
                def prep(stage, h, u, pair):
                    j = stage % 2
                    at = h * 2 + j + 1
                    if 2 <= stage < 4:
                        e.wait_ge(rooted.sem, rooted.at(at))
                        e.reciprocal(rts[j][0:QK, :], rts[j][0:QK, :]).then_inc(inv.sem, 1)
                        e.wait_ge(inv.sem, inv.at(at))
                        e.scalar_tensor_tensor((Q, Kh)[j][u][0:QK, :], raws_[j][0:QK, :], (q_g, k_g)[j],
                                               rts[j][0:QK, :], ALU.mult, ALU.mult).then_inc(normed.sem, 1)
                    elif stage >= 4:
                        lat = (Q, Kh)[j][u][0:QK, 0:SEQ]
                        e.wait_ge(turned.sem, turned.at(at))
                        if j:
                            e.wait_ge(roped.sem, roped.at(h * 2 + 1))
                        e.tensor_tensor(TM[0:QK, :], group(1, SEQ, 0, QK), sin[0:QK, :], ALU.mult).then_inc(sined.sem, 1)
                        e.tensor_tensor(lat, lat, cos[0:QK, :], ALU.mult).then_inc(cosed.sem, 1)
                        e.wait_ge(sined.sem, sined.at(at))
                        e.wait_ge(cosed.sem, cosed.at(at))
                        e.tensor_tensor(lat, lat, TM[0:QK, :], ALU.add).then_inc(roped.sem, 1)

                def main(i, u, h, next_):
                    for t in range(NQ):
                        e.wait_ge(scored.sem, scored.at(h * NQ + t + 1))
                        c = (t + 1) % 2 * GROUP
                        e.tensor_reduce(st[:, t:t + 1], ps[:, c:c + blocks(t)[1]], AX.X, ALU.max).then_inc(maxed.sem, 1)

                    def norm(b):
                        mine = slice(u * 64, u * 64 + 64)
                        other = slice(64 - u * 64, 128 - u * 64)
                        n, bank = (BANK if b < 2 else CTX), 6 + b % 2
                        s_end = max(s for s in range(NS) if steps[s][4] == b)
                        e.wait_ge(mixed.sem, mixed.at(h * NS + s_end + 1))
                        e.reciprocal(RB[b][mine, 0:n], ps[other, bank * BANK:bank * BANK + n]).then_inc(oinv.sem, 1)
                        e.wait_ge(oinv.sem, oinv.at(h * NB + b + 1))
                        e.tensor_tensor(MLA_OUT[mine, bass.ds(i * T + b * BANK, n)], ps[mine, bank * BANK:bank * BANK + n],
                                        RB[b][mine, 0:n], ALU.mult).then_inc(onormed.sem, 1)

                    next_(2)
                    next_(3)
                    norm(0)
                    next_(4)
                    next_(5)
                    for b in range(1, NB):
                        norm(b)

                pair = every_head(prep, main)
                with e.Fori(0, PAIRS - 1) as i:
                    pair(i, False)
                pair(PAIRS - 1, True)
            ph.parts = dict(sp=sp, pe=pe, act=act, dve=dve, pool=pool)

        GQ = FREE
        qkv = region(C, GQ, 9 * T).rearrange("p (n t) -> p n t", n=9)
        zz3 = region(C, GQ + 9 * T, 3 * T).rearrange("p (n t) -> p n t", n=3)
        O_OUT = region(C, GQ + 12 * T, 3 * T)
        o3 = O_OUT.rearrange("p (n t) -> p n t", n=3)
        abT = region(C, GQ + 15 * T, T)
        GT = region(C, GQ + 16 * T, N_CHUNK * 36)
        assert GQ + 16 * T + N_CHUNK * 36 <= FT * T
        gt5 = GT.rearrange("p (n d k q) -> p n d k q", n=N_CHUNK, d=2, k=6)

        def phase_gdn_in(l):
            ph = Phase()
            ph.uses_w = True
            n0 = tiles[0]
            tiles[0] += 13
            ph.ends.append((tile_done.sem, tiles[0]))
            zeroed = ph.sig("pads_zeroed", 8)
            raw_ready = ph.sig("raw_ready", 9)
            conv_done = ph.sig("conv_done", 9)
            silu = ph.sig("silu_made", 9)
            zk = ph.sig("z_gate_kept", 4)
            src = a["w_in"][l].rearrange("(k p) n -> p k n", p=P)
            cv = [region(X, 2 * RAW + s * T, T) for s in range(2)]

            def pool(e):
                zero_pads(e, zeroed)

            def sp(e):
                with e.Fori(0, 4) as i:
                    for u in range(2):
                        load_tile(e, tile(n0, i, u), src, i * 256 + u * P, DK, P)
                for j in range(8, 13):
                    w = P if j < 12 else 4 * HEADS
                    load_tile(e, tile(n0, 0, j), src, j * P, DK, w)

            def pe(e):
                whole_product(e, tile(n0, 0, 0), DK, P, whole_h, False)
                whole_product(e, tile(n0, 0, 1), DK, P, whole_h, False)
                with e.Fori(1, 4) as i:
                    for u in range(2):
                        whole_product(e, tile(n0, i, u), DK, P, whole_h, False, (raw_ready, i * 2 + (u - 1)))
                for j in range(8, 13):
                    free = (raw_ready, j - 1) if j < 11 else (zk, j - 10)
                    whole_product(e, tile(n0, 0, j), DK, P if j < 12 else 4 * HEADS, whole_h, False, free)

            def conv_act(e, i, u, j):
                g, n, _ = tile(n0, i, u)
                e.wait_ge(tile_done.sem, n + 1)
                keep_raw(e, g, raws()[u], T, raw_ready)
                e.wait_ge(conv_done.sem, conv_done.at(j + 1))
                dst = region(C, GQ, 9 * T)[:, bass.ds(j * T, T)] if not isinstance(j, int) else qkv[:, j]
                e.activation(dst, cv[u], ACT.Silu).then_inc(silu.sem, 1)

            def act(e):
                e.wait_ge(zeroed.sem, zeroed.at(8))
                with e.Fori(0, 4) as i:
                    for u in range(2):
                        conv_act(e, i, u, i * 2 + u)
                conv_act(e, 4, 0, 8)
                for j in range(9, 13):
                    n = n0 + j
                    e.wait_ge(tile_done.sem, n + 1)
                    if j < 12:
                        e.activation(zz3[:, j - 9], group(n % 2, T), ACT.Silu).then_inc(zk.sem, 1)
                    else:
                        e.activation(abT[0:24, :], group(n % 2, T, 0, 24), ACT.Copy).then_inc(zk.sem, 1)

            def one_conv(e, u, j):
                e.wait_ge(raw_ready.sem, raw_ready.at(j + 1))
                w = [S[:, bass.ds(VCOL["gdn_conv_w"] + s * 9 + j, 1)] if not isinstance(j, int)
                     else vec("gdn_conv_w", s * 9 + j) for s in range(3)]
                conv(e, raws()[u], w, None, cv[u], T, conv_done)
                e.wait_ge(silu.sem, silu.at(j + 1))

            def dve(e):
                e.wait_ge(zeroed.sem, zeroed.at(8))
                with e.Fori(0, 4) as i:
                    chain["dve"].loop(i, 4)
                    for u in range(2):
                        one_conv(e, u, i * 2 + u)
                chain["dve"].end(4)
                one_conv(e, 0, 8)
            ph.parts = dict(sp=sp, pe=pe, act=act, dve=dve, pool=pool)

        def phase_head_norm(l, kind):
            ph = Phase()
            n = 6 if kind == "qk" else 3
            loaded = ph.sig("selectors_loaded", 2, 16)
            squared = ph.sig("squared", n)
            summed = ph.sig("squares_summed", n)
            root = ph.sig("root_made", 1)
            inv = ph.sig("rstd_made", 1)
            spread = ph.sig("rstd_spread", n)
            made = ph.sig("heads_normed", n)
            sq = [region(X, s * T, T) for s in range(2)]
            rt = region(X, 2 * T, T)[0:SEL, :]
            select = region(X, 3 * T, 6 * SEL)
            back = region(X, 3 * T + 6 * SEL, 6 * P)[0:SEL, :]

            def part(j):
                return qkv[:, j] if kind == "qk" else o3[:, j]

            def sp(e):
                e.dma_start(select, a["k_select"]).then_inc(loaded.sem, 16)
                e.dma_start(back, a["k_spread"]).then_inc(loaded.sem, 16)

            def act(e):
                for j in range(n):
                    if j >= 2:
                        e.wait_ge(summed.sem, summed.at(j - 1))
                    e.activation(sq[j % 2], part(j), ACT.Square).then_inc(squared.sem, 1)
                e.wait_ge(summed.sem, summed.at(n))
                e.activation(rt, group(0, T, 0, SEL), ACT.Sqrt, bias=eps[0:SEL, :],
                             scale=1.0 if kind == "qk" else 1.0 / CH).then_inc(root.sem, 1)

            def pe(e):
                e.wait_ge(loaded.sem, loaded.at(2))
                for j in range(n):
                    e.wait_ge(squared.sem, squared.at(j + 1))
                    for b, (t0, tn) in enumerate(tok(False)):
                        ins = e.matmul(ps[0:SEL, b * BANK:b * BANK + tn], select[:, j * SEL:j * SEL + SEL],
                                       sq[j % 2][:, t0:t0 + tn], start=(j == 0), stop=(j == n - 1))
                    ins.then_inc(summed.sem, 1)
                e.wait_ge(inv.sem, inv.at(1))
                for j in range(n):
                    g = (j + 1) % 2
                    if j >= 2:
                        e.wait_ge(made.sem, made.at(j - 1))
                    for b, (t0, tn) in enumerate(tok(False)):
                        ins = e.matmul(ps[:, g * GROUP + b * BANK:g * GROUP + b * BANK + tn], back[:, j * P:j * P + P],
                                       rt[:, t0:t0 + tn], start=True, stop=True)
                    ins.then_inc(spread.sem, 1)

            def dve(e):
                e.wait_ge(root.sem, root.at(1))
                e.reciprocal(rt, rt).then_inc(inv.sem, 1)
                for j in range(n):
                    r = group((j + 1) % 2, T)
                    e.wait_ge(spread.sem, spread.at(j + 1))
                    if kind == "qk":
                        e.scalar_tensor_tensor(part(j), part(j), CH ** -0.5 if j < 3 else 1.0, r, ALU.mult, ALU.mult)\
                            .then_inc(made.sem, 1)
                    else:
                        chain["dve"].link(e, e.scalar_tensor_tensor(part(j), part(j), gdn_g, r, ALU.mult, ALU.mult))
                        e.tensor_tensor(part(j), part(j), zz3[:, j], ALU.mult).then_inc(made.sem, 1)
            ph.parts = dict(sp=sp, pe=pe, act=act, dve=dve)

        def phase_gates(l):
            ph = Phase()
            abm = ph.sig("gates_turned", 1)
            cut = ph.sig("gates_cut", 2)
            biased = ph.sig("gate_biased", 1)
            absd = ph.sig("gate_abs", 1)
            e1 = ph.sig("gate_exp", 2)
            ln = ph.sig("gate_log", 1)
            sig_ = ph.sig("beta_made", 1)
            sp_ = ph.sig("softplus_made", 1)
            gm = ph.sig("g_made", 1)
            summed = ph.sig("g_summed", 1)
            gk = ph.sig("gc_kept", 2)
            ex = ph.sig("gate_exps", 3)
            be = ph.sig("beta_decay_made", 1)
            NU = N_CHUNK * 2 * PAIRS
            AB = region(X, 0, N_CHUNK * 12)
            ab4 = AB.rearrange("p (n x q) -> p n x q", n=N_CHUNK, x=4)
            t1, t2, t3, t4 = (region(X, 240 + j * NU, NU).rearrange("p (n x q) -> p n x q", n=N_CHUNK, x=2)
                              for j in range(4))
            ea = region(X, 240 + 4 * NU, 6)

            def pe(e):
                for n in range(N_CHUNK):
                    for h in range(2):
                        ins = e.matmul(ps[h * 64:h * 64 + 64, n * 24:n * 24 + 24], abT[0:24, n * CH:n * CH + CH],
                                       ident[0:24, 0:24], start=True, stop=True)
                ins.then_inc(abm.sem, 1)
                e.wait_ge(gm.sem, gm.at(1))
                for h in range(2):
                    r = slice(h * 64, h * 64 + 64)
                    for d in range(2):
                        g = gt5[r, :, d, 0, :]
                        e.matmul(ps[r, BANK + d * 60:BANK + d * 60 + 60], K[r, K_CUM + d * CH:K_CUM + d * CH + CH], g,
                                 start=True, stop=True)
                        ins = e.matmul(ps[r, 2 * BANK + d * 60:2 * BANK + d * 60 + 60], K[r, K_ONES:K_ONES + CH], g,
                                       start=True, stop=True)
                ins.then_inc(summed.sem, 1)

            def act(e):
                e.activation(ea, AL, ACT.Exp).then_inc(e1.sem, 1)
                e.wait_ge(absd.sem, absd.at(1))
                e.activation(t3, t2, ACT.Exp, scale=-1.0).then_inc(e1.sem, 1)
                e.wait_ge(e1.sem, e1.at(2))
                e.activation(t4, t3, ACT.Ln, bias=1.0).then_inc(ln.sem, 1)
                e.activation(gt5[:, :, :, 2, :], ab4[:, :, 2:4, :], ACT.Sigmoid).then_inc(sig_.sem, 1)
                e.wait_ge(gk.sem, gk.at(2))
                e.activation(gt5[:, :, :, 4, :], t1, ACT.Exp).then_inc(ex.sem, 1)
                e.activation(gt5[:, :, :, 5, :], t3, ACT.Exp).then_inc(ex.sem, 1)
                e.activation(gt5[:, :, :, 3, :], gt5[:, :, :, 1, :], ACT.Exp).then_inc(ex.sem, 1)

            def dve(e):
                e.wait_ge(abm.sem, abm.at(1))
                for h in range(2):
                    r = slice(h * 64, h * 64 + 64)
                    v = ps[r, 0:N_CHUNK * 24].rearrange("p (n x q h) -> p n x q h", n=N_CHUNK, x=4, h=2)[:, :, :, :, h]
                    e.tensor_copy(ab4[r], v).then_inc(cut.sem, 1)
                e.wait_ge(cut.sem, cut.at(2))
                dt_ = DT.rearrange("p (x q) -> p x q", x=2).unsqueeze(1).broadcast_to([P, N_CHUNK, 2, PAIRS])
                e.tensor_tensor(t1, ab4[:, :, 0:2, :], dt_, ALU.add).then_inc(biased.sem, 1)
                e.wait_ge(biased.sem, biased.at(1))
                e.scalar_tensor_tensor(t2, t1, -1.0, t1, ALU.mult, ALU.max).then_inc(absd.sem, 1)
                e.wait_ge(ln.sem, ln.at(1))
                e.scalar_tensor_tensor(t1, t1, 0.0, t4, ALU.max, ALU.add).then_inc(sp_.sem, 1)
                e.wait_ge(sp_.sem, sp_.at(1))
                ea_ = ea.rearrange("p (x q) -> p x q", x=2).unsqueeze(1).broadcast_to([P, N_CHUNK, 2, PAIRS])
                chain["dve"].link(e, e.tensor_tensor(t1, t1, ea_, ALU.mult))
                e.tensor_scalar(gt5[:, :, :, 0, :], t1, -1.0, None, ALU.mult).then_inc(gm.sem, 1)
                e.wait_ge(summed.sem, summed.at(1))
                sums = [ps[:, b * BANK:b * BANK + 120].rearrange("p (x n q) -> p n x q", x=2, q=PAIRS) for b in (1, 2)]
                chain["dve"].link(e, e.tensor_copy(gt5[:, :, :, 1, :], sums[0]))
                e.tensor_copy(t3, sums[1]).then_inc(gk.sem, 1)
                e.wait_ge(gk.sem, gk.at(1))
                e.tensor_tensor(t1, t3, gt5[:, :, :, 1, :], ALU.subtract).then_inc(gk.sem, 1)
                e.wait_ge(ex.sem, ex.at(3))
                e.tensor_tensor(gt5[:, :, :, 3, :], gt5[:, :, :, 3, :], gt5[:, :, :, 2, :], ALU.mult).then_inc(be.sem, 1)
            ph.parts = dict(pe=pe, act=act, dve=dve)

        def phase_scan(l):
            ph = Phase()
            ph.uses_w = True
            NS = N_CHUNK
            U3 = PAIRS * CH
            U6 = PAIRS * P
            NL = LEVELS - 1
            zeroed = ph.sig("scan_zeroed", 2)
            cleared = ph.sig("scan_cleared", 1)
            staged = ph.sig("qk_staged", 2 * NS)
            paired = ph.sig("kv_paired", 2 * NS)
            rhs_made = ph.sig("row_sources_made", 2 * NS)
            prods = ph.sig("kk_kq_made", 2 * NS)
            rows = ph.sig("rows_spread", 2 * NS)
            turned = ph.sig("kv_turned", 2 * NS)
            eg = ph.sig("decay_row_made", 2 * NS)
            decin = ph.sig("decay_arg_made", 2 * NS)
            dec = ph.sig("decay_mat_made", 2 * NS)
            kd = ph.sig("k_decayed", 2 * NS)
            att = ph.sig("a_made", 2 * NS)
            qd = ph.sig("qk_row_decayed", 2 * NS)
            xt0 = ph.sig("xt0_made", 2 * NS)
            am = ph.sig("a_levels", 2 * NL * NS)
            x0 = ph.sig("x0_turned", 2 * NS)
            x0k = ph.sig("x0_kept", 2 * NS)
            ax = ph.sig("ax_made", 2 * NL * NS)
            axk = ph.sig("ax_kept", 2 * NL * NS)
            xax = ph.sig("xax_made", 2 * (NL - 1) * NS)
            xup = ph.sig("x_updated", 2 * (NL - 1) * NS)
            xaxt = ph.sig("xaxt_made", 2 * NL * NS)
            xtup = ph.sig("xt_updated", 2 * NL * NS)
            ks = ph.sig("ks_made", 2 * NS)
            resid = ph.sig("residual_made", 2 * NS)
            delta = ph.sig("delta_made", 2 * NS)
            dk = ph.sig("delta_kept", 2 * NS)
            MOD = (((48 - FIRST_MOD) // LAT_CHUNKS, (3, 0)), (48 // LAT_CHUNKS, (0, 1, 2)))
            PER_SLOT = (2, 1, 1, 1)
            if l == 0:
                ada_in = [ph.sig("ada_slot_%d" % k, PER_SLOT[k] * LAT_CHUNKS, 16) for k in range(4)]
                ada_used = ph.sig("ada_column_used", 5 * LAT_CHUNKS)
            om = ph.sig("o_made", 2 * NS)
            snew = ph.sig("state_made", 2 * NS)
            oadd = ph.sig("o_added", 2 * NS)
            place = {"X": 0, "H": 0}

            def buf(n, t="X"):
                r = region(X if t == "X" else H, place[t], n)
                place[t] += n
                return r

            def stacked():
                return buf(2 * U3).rearrange("p (d q i) -> p d q i", d=2, q=PAIRS)

            def pairs(t="X"):
                return buf(2 * U6, t).rearrange("p (d q i) -> p d q i", d=2, q=PAIRS)

            KV = buf(4 * U6, "H").rearrange("p (d n i) -> p d n i", d=2, n=2 * PAIRS)
            QKD = buf(4 * U6, "H").rearrange("p (d w q i) -> p d w q i", d=2, w=2, q=PAIRS)
            AM = buf(NL * 2 * U6, "H").rearrange("p (m d q i) -> p m d q i", m=NL, d=2, q=PAIRS)
            XT, KQD, SS = (pairs("H") for _ in range(3))
            ST = buf(4 * U3).rearrange("p (d n i) -> p d n i", d=2, n=2 * PAIRS)
            gs4 = buf(36).rearrange("p (d k q) -> p d k q", d=2, k=6)
            RS = buf(4 * U3).rearrange("p (d w q i) -> p d w q i", d=2, w=2, q=PAIRS)
            DEC, EG, AT, T0 = (stacked() for _ in range(4))
            XX, AX_, DL, KD, SC, ZR, RV = (pairs() for _ in range(7))
            ada = [x.rearrange("p (k n) -> p k n", k=DK)
                   for x in (W[:, 0:D], W[:, D:2 * D], buf(D), buf(D, "H"))]
            assert place["X"] <= DK * T and place["H"] <= DK * T
            CLEAR = place["H"] - D
            SPLIT = 9 * T // 3

            def bank(d, b, q=None):
                c = (4 * d + b) * BANK
                return ps[:, c:c + U6] if q is None else ps[:, c + q * P:c + q * P + P]

            def bank3(d, b):
                return bank(d, b).rearrange("p (q i) -> p q i", q=PAIRS)

            def halves_of(x):
                return [x[h * CH:h * CH + CH, :, h * CH:h * CH + CH] for h in range(2)]

            HEAD = [slice(h * CH, h * CH + CH) for h in range(2)]

            def col(k, d, w=CH, r=slice(0, P)):
                return gs4[r, d, k, :].unsqueeze(2).broadcast_to([r.stop - r.start, PAIRS, w])

            def const3(c, r=slice(0, P)):
                return K[r, c:c + CH].unsqueeze(1).broadcast_to([r.stop - r.start, PAIRS, CH])

            PRE = ("load", "kq", "rows", "kv", "a", "x0")
            TAIL = ("ks", "delta", "out")
            HALF = (("ax", 1), ("load", 0), ("ks", 0), ("xax", 1), ("delta", 0), ("ax", 2), ("out", 0), ("xax", 2),
                    ("kq", 0), ("rows", 0), ("ax", 3), ("kv", 0), ("xax", 3), ("ax", 4), ("a", 0),
                    ("xax", 4), ("ax", 5), ("x0", 0), ("xax", 5))
            LINKS = 10
            latents = [False]
            MOD_STAGE, MOD_LEVELS = ("xax",), (2, 3, 4)

            def walk(e, stage, own=None):
                def half(d, s, tail, pre):
                    for name, m in HALF:
                        if m:
                            stage(name, m, d, s, None)
                        elif name in TAIL and tail is not None:
                            stage(name, 0, 1 - d, *tail)
                        elif name in PRE and pre is not None:
                            stage(name, 0, 1 - d, *pre)

                def step(s, before, now):
                    half(1, s - 1, (s - 1, before), (s, now))
                    half(0, s, (s - 1, s * -1 + N_CHUNK), (s, s * -1 + (N_CHUNK - 1)))

                for name in PRE:
                    stage(name, 0, 0, 0, LAT_CHUNKS)
                half(0, 0, None, (0, N_CHUNK - 1))
                with e.Fori(0, CTX_CHUNKS - 1) as i:
                    if own:
                        own.loop(i, LINKS)
                    step(i + 1, i + LAT_CHUNKS, i + (LAT_CHUNKS + 1))
                if own:
                    own.end(CTX_CHUNKS - 1)
                step(CTX_CHUNKS, N_CHUNK - 1, 0)
                with e.Fori(0, LAT_CHUNKS - 1) as i:
                    if own:
                        own.loop(i, LINKS)
                    latents[0] = True
                    step(i + (CTX_CHUNKS + 1), i, i + 1)
                    latents[0] = False
                if own:
                    own.end(LAT_CHUNKS - 1)
                half(1, NS - 1, (NS - 1, LAT_CHUNKS - 1), None)
                for name in TAIL:
                    stage(name, 0, 1, NS - 1, 0)

            def at(r, d, s):
                return r.at(s * 2 + (d + 1))

            def at_level(r, d, s, m):
                return r.at(s * (2 * NL) + (d * NL + m))

            def at_mid(r, d, s, m):
                return r.at(s * (2 * (NL - 1)) + (d * (NL - 1) + m))

            def later(s):
                return not (isinstance(s, int) and s == 0)

            qf = region(C, GQ, 9 * T).rearrange("p (n t) -> p n t", n=9)

            def pool(e):
                e.memset(O_OUT, 0.0).then_inc(zeroed.sem, 1)
                e.wait_ge(zeroed.sem, zeroed.at(1))
                e.memset(H[:, 0:SPLIT], 0.0).then_inc(zeroed.sem, 1)
                e.wait_ge(zeroed.sem, zeroed.at(2))
                e.wait_ge(cleared.sem, cleared.at(1))

                def stage(name, m, d, s, c):
                    if name == "load":
                        if later(s):
                            e.wait_ge(resid.sem, at(resid, d, s - 1))
                        if later(s) or d:
                            e.wait_ge(am.sem, at_level(am, 1 - d, s - 1 + d, NL))
                        e.tensor_copy(ST[:, d], qf[:, 0:2 * PAIRS, bass.ds(c * CH, CH)])
                        e.tensor_copy(gs4[:, d].rearrange("p k q -> p (k q)"), GT[:, bass.ds(c * 36 + d * 18, 18)])\
                            .then_inc(staged.sem, 1)
                        e.wait_ge(staged.sem, at(staged, d, s))
                        e.tensor_tensor(RS[:, d, 0], const3(K_CUM + d * CH), col(0, d), ALU.mult)
                        e.tensor_tensor(RS[:, d, 1], const3(K_ID64), col(2, d), ALU.mult).then_inc(rhs_made.sem, 1)
                    elif name == "a":
                        e.wait_ge(rhs_made.sem, at(rhs_made, d, s))
                        e.wait_ge(eg.sem, at(eg, d, s))
                        for h in range(2):
                            ins = e.tensor_tensor(QKD[HEAD[h], d, :, :, h * CH:h * CH + CH],
                                                  ST[HEAD[h], d].rearrange("p (w q) i -> p w q i", w=2),
                                                  EG[HEAD[h], d].unsqueeze(1).broadcast_to([CH, 2, PAIRS, CH]), ALU.mult)
                        ins.then_inc(qd.sem, 1)
                        e.wait_ge(att.sem, at(att, d, s))
                        for m_ in range(1, LEVELS):
                            for h in range(2):
                                ins = e.tensor_tensor(halves_of(AM[:, m_ - 1, d])[h], AT[HEAD[h], d],
                                                      const3(K_LEVEL + (m_ * 2 + d) * CH, HEAD[h]), ALU.mult)
                            ins.then_inc(am.sem, 1)
                walk(e, stage)

            def sp(e):
                w = [a["ada_w"][j].rearrange("(k p) n -> p k n", p=P) for j in range(2)]

                def load(i, again):
                    for x, (layer, slot, before) in enumerate(((1, 0, 0), (1, 1, -3), (1, 2, -2), (0, 3, -1), (0, 0, 1))):
                        u = x if layer else x - 3
                        n = i * (MOD[layer][0] * P) + (u * P if layer else (FIRST_MOD + u) * P)
                        n = n if isinstance(n, int) else e.snap(n)
                        if again or x == 4:
                            e.wait_ge(ada_used.sem, ada_used.at(i * 5 + before))
                        e.dma_start(ada[slot], w[layer][:, :, bass.ds(n, P)]).then_inc(ada_in[slot].sem, 16)
                load(0, False)
                with e.Fori(1, LAT_CHUNKS) as i:
                    load(i, True)

            def modulate(e, d, s, u):
                i = s - (CTX_CHUNKS - d)
                if u < MOD[d][0]:
                    slot = MOD[d][1][u]
                    e.wait_ge(ada_in[slot].sem, ada_in[slot].at(i * PER_SLOT[slot] + (2 if d == 0 and u == 1 else 1)))
                    at_ = i * (2 * MOD[d][0]) + ((4 * d + 3) * BANK + MOD_AT + 2 * u)
                    for k in range(DK):
                        ins = e.matmul(ps[:, bass.ds(at_, 2)], ada[slot][:, k, :], c_silu[:, k, :],
                                       start=(k == 0), stop=(k == DK - 1))
                    ins.then_inc(ada_used.sem, 1)

            def pe(e):
                e.wait_ge(zeroed.sem, zeroed.at(2))
                e.wait_ge(cleared.sem, cleared.at(1))

                def stage(name, m, d, s, c):
                    if name in MOD_STAGE and l == 0 and (s == CTX_CHUNKS - d if isinstance(s, int) else latents[0]):
                        if m in MOD_LEVELS:
                            modulate(e, d, s, MOD_LEVELS.index(m))
                    if name == "kq":
                        e.wait_ge(staged.sem, at(staged, d, s))
                        e.wait_ge(paired.sem, at(paired, d, s))
                        if later(s):
                            e.wait_ge(snew.sem, at(snew, d, s - 1))
                            e.wait_ge(oadd.sem, at(oadd, d, s - 1))
                        for q in range(PAIRS):
                            ins = e.matmul(bank(d, 0, q), KV[:, d, q, :], ST[:, d, q:q + 4:3, :], start=True, stop=True)
                        ins.then_inc(prods.sem, 1)
                    elif name == "rows":
                        e.wait_ge(rhs_made.sem, at(rhs_made, d, s))
                        e.matmul(bank(d, 1), K[:, K_BLOCK:K_BLOCK + P], RS[:, d].rearrange("p w q i -> p (w q i)"),
                                 start=True, stop=True).then_inc(rows.sem, 1)
                    elif name == "kv":
                        for w in range(2):
                            for q in range(PAIRS):
                                ins = e.matmul(bank(d, 2 + w, q), KV[:, d, w * PAIRS + q, :], ident, start=True, stop=True)
                        ins.then_inc(turned.sem, 1)
                    elif name == "x0":
                        e.wait_ge(xt0.sem, at(xt0, d, s))
                        for q in range(PAIRS):
                            ins = e.matmul(bank(d, 0, q), XT[:, d, q, :], ident, start=True, stop=True)
                        ins.then_inc(x0.sem, 1)
                    elif name == "ax":
                        e.wait_ge(am.sem, at_level(am, d, s, m))
                        if m == 1:
                            e.wait_ge(x0k.sem, at(x0k, d, s))
                        else:
                            e.wait_ge(xup.sem, at_mid(xup, d, s, m - 1))
                        for q in range(PAIRS):
                            ins = e.matmul(bank(d, 0, q), AM[:, m - 1, d, q, :], XX[:, d, q, :], start=True, stop=True)
                        ins.then_inc(ax.sem, 1)
                    elif name == "xax":
                        e.wait_ge(axk.sem, at_level(axk, d, s, m))
                        if m > 1:
                            e.wait_ge(xtup.sem, at_level(xtup, d, s, m - 1))
                        if m < NL:
                            for q in range(PAIRS):
                                ins = e.matmul(bank(d, 1, q), XT[:, d, q, :], AX_[:, d, q, :], start=True, stop=True)
                            ins.then_inc(xax.sem, 1)
                        for q in range(PAIRS):
                            ins = e.matmul(bank(d, 2, q), AX_[:, d, q, :], XT[:, d, q, :], start=True, stop=True)
                        ins.then_inc(xaxt.sem, 1)
                    elif name == "ks":
                        e.wait_ge(qd.sem, at(qd, d, s))
                        e.wait_ge(xtup.sem, at_level(xtup, d, s, NL))
                        for q in range(PAIRS):
                            ins = e.matmul(bank(d, 0, q), QKD[:, d, 1, q, :], SS[:, d, q, :], start=True, stop=True)
                        ins.then_inc(ks.sem, 1)
                    elif name == "delta":
                        e.wait_ge(resid.sem, at(resid, d, s))
                        for q in range(PAIRS):
                            ins = e.matmul(bank(d, 2, q), XT[:, d, q, :], ZR[:, d, q, :], start=True, stop=True)
                        ins.then_inc(delta.sem, 1)
                    elif name == "out":
                        e.wait_ge(kd.sem, at(kd, d, s))
                        e.wait_ge(dk.sem, at(dk, d, s))
                        for q in range(PAIRS):
                            e.matmul(bank(d, 3, q), KD[:, d, q, :], DL[:, d, q, :], start=True, stop=True)
                        for q in range(PAIRS):
                            e.matmul(bank(d, 1, q), SS[:, d, q, :], QKD[:, d, 0, q, :], start=True, stop=False)
                            ins = e.matmul(bank(d, 1, q), DL[:, d, q, :], KQD[:, d, q, :], start=False, stop=True)
                        ins.then_inc(om.sem, 1)
                walk(e, stage)

            def act(e):
                e.wait_ge(zeroed.sem, zeroed.at(2))
                e.wait_ge(cleared.sem, cleared.at(1))

                def stage(name, m, d, s, c):
                    if name == "load":
                        if later(s):
                            e.wait_ge(turned.sem, at(turned, d, s - 1))
                        for h in range(2):
                            ins = e.activation(halves_of(KV[:, d])[h], qf[HEAD[h], PAIRS:3 * PAIRS, bass.ds(c * CH, CH)],
                                               ACT.Copy)
                        ins.then_inc(paired.sem, 1)
                    elif name == "rows":
                        e.wait_ge(rows.sem, at(rows, d, s))
                        e.activation(EG[:, d].rearrange("p q i -> p (q i)"), bank(d, 1)[:, 0:U3], ACT.Exp)\
                            .then_inc(eg.sem, 1)
                    elif name == "kv":
                        e.wait_ge(decin.sem, at(decin, d, s))
                        e.activation(DEC[:, d], DEC[:, d], ACT.Exp).then_inc(dec.sem, 1)
                    elif name == "x0":
                        e.wait_ge(x0.sem, at(x0, d, s))
                        e.activation(XX[:, d], bank3(d, 0), ACT.Copy).then_inc(x0k.sem, 1)
                    elif name == "ax":
                        e.wait_ge(ax.sem, at_level(ax, d, s, m))
                        e.activation(AX_[:, d], bank3(d, 0), ACT.Copy).then_inc(axk.sem, 1)
                    elif name == "delta":
                        e.wait_ge(delta.sem, at(delta, d, s))
                        e.activation(DL[:, d], bank3(d, 2), ACT.Copy).then_inc(dk.sem, 1)
                walk(e, stage)

            def dve(e):
                link = chain["dve"].link
                e.memset(H[:, SPLIT:CLEAR], 0.0).then_inc(cleared.sem, 1)
                e.wait_ge(zeroed.sem, zeroed.at(2))
                e.wait_ge(cleared.sem, cleared.at(1))

                def stage(name, m, d, s, c):
                    if name == "rows":
                        e.wait_ge(eg.sem, at(eg, d, s))
                        gsum = bank(d, 1)[:, 0:U3].rearrange("p (q i) -> p q i", q=PAIRS)
                        link(e, e.tensor_tensor(DEC[:, d], gsum, const3(K_NEG + d * CH), ALU.add))
                        e.tensor_tensor(DEC[:, d], DEC[:, d], col(1, d), ALU.subtract).then_inc(decin.sem, 1)
                    elif name == "kv":
                        e.wait_ge(turned.sem, at(turned, d, s))
                        e.tensor_tensor(RV[:, d], bank3(d, 3), col(2, d, P), ALU.mult)
                        e.tensor_tensor(KD[:, d], bank3(d, 2), col(4, d, P), ALU.mult).then_inc(kd.sem, 1)
                        if later(s):
                            e.wait_ge(snew.sem, at(snew, d, s - 1))
                        link(e, e.tensor_tensor(SC[:, d], SS[:, d], col(5, d, P), ALU.mult))
                    elif name == "a":
                        kq = bank(d, 0).rearrange("p (q w i) -> p w q i", q=PAIRS, w=2)
                        beta = bank(d, 1)[:, U3:U6].rearrange("p (q i) -> p q i", q=PAIRS)
                        e.wait_ge(dec.sem, at(dec, d, s))
                        link(e, e.tensor_tensor(AT[:, d], kq[:, 1], DEC[:, d], ALU.mult))
                        e.tensor_tensor(AT[:, d], beta, AT[:, d], ALU.mult).then_inc(att.sem, 1)
                        for h in range(2):
                            e.tensor_tensor(halves_of(KQD[:, d])[h], kq[HEAD[h], 0], DEC[HEAD[h], d], ALU.mult)
                        e.wait_ge(att.sem, at(att, d, s))
                        link(e, e.tensor_tensor(T0[:, d], AT[:, d], const3(K_LEVEL + d * CH), ALU.mult))
                        for h in range(2):
                            ins = e.tensor_tensor(halves_of(XT[:, d])[h], const3(K_ID64, HEAD[h]), T0[HEAD[h], d],
                                                  ALU.subtract)
                        ins.then_inc(xt0.sem, 1)
                    elif name == "xax":
                        if m < NL:
                            e.wait_ge(xax.sem, at_mid(xax, d, s, m))
                            if m > 1:
                                e.wait_ge(xup.sem, at_mid(xup, d, s, m - 1))
                            e.tensor_tensor(XX[:, d], XX[:, d], bank3(d, 1), ALU.subtract).then_inc(xup.sem, 1)
                        e.wait_ge(xaxt.sem, at_level(xaxt, d, s, m))
                        if m == 1:
                            e.wait_ge(xt0.sem, at(xt0, d, s))
                        else:
                            e.wait_ge(xtup.sem, at_level(xtup, d, s, m - 1))
                        e.tensor_tensor(XT[:, d], XT[:, d], bank3(d, 2), ALU.subtract).then_inc(xtup.sem, 1)
                    elif name == "ks":
                        e.wait_ge(ks.sem, at(ks, d, s))
                        link(e, e.tensor_tensor(ZR[:, d], bank3(d, 0), col(2, d, P), ALU.mult))
                        e.tensor_tensor(ZR[:, d], RV[:, d], ZR[:, d], ALU.subtract).then_inc(resid.sem, 1)
                    elif name == "out":
                        e.wait_ge(om.sem, at(om, d, s))
                        e.tensor_tensor(SS[:, d], SC[:, d], bank3(d, 3), ALU.add).then_inc(snew.sem, 1)
                        if later(s) or d:
                            e.wait_ge(oadd.sem, oadd.at(s * 2 + d))
                        for h in range(2):
                            oo = o3[HEAD[h], :, bass.ds(c * CH, CH)]
                            ins = e.tensor_tensor(oo, oo, halves_of(bank3(d, 1))[h], ALU.add)
                        ins.then_inc(oadd.sem, 1)
                walk(e, stage, chain["dve"])
            ph.parts = dict(pe=pe, act=act, dve=dve, pool=pool)
            if l == 0:
                ph.parts["sp"] = sp

        def residual(e, i, u, m, g, which, last, dst=None):
            for t0, tn, v in [(0, SEQ, 0)] + ([] if last else [(SEQ, CTX, 1)]):
                x_ = X[:, bass.ds(m * T + t0, tn)] if not isinstance(m, int) else x3[:, m, t0:t0 + tn]
                gate = S[:, bass.ds((N_VEC + 2 * which + v) + m * 2, 1)]
                ins = e.scalar_tensor_tensor(x_ if dst is None else dst, ps[:, g * GROUP + t0:g * GROUP + t0 + tn],
                                             gate, x_, ALU.mult, ALU.add)
            return ins

        def phase_out(l, last):
            ph = Phase()
            ph.uses_w = True
            n0 = tiles[0]
            tiles[0] += 8
            ph.ends.append((tile_done.sem, tiles[0]))
            back = ph.sig("x_back", 1, 16)
            added = ph.sig("x_added", 8)
            split = ph.sig("tile_split", 8)
            high = ph.sig("mix_high_made", 8)
            low = ph.sig("mix_low_made", 8)
            src = a["w_out"][l].rearrange("(k p) n -> p k n", p=P)
            mix = [o3[:, j] for j in range(3)] + [mla3[:, j] for j in range(3)] + [hy3[:, j] for j in range(2)]
            width = SEQ if last else T
            parts = [halves(C, FREE + j * T, T) for j in range(8)]
            ring = split_ring(C, FREE + 8 * T)

            def rhs(kk, t0, tn, half):
                return parts[kk][half][:, t0:t0 + tn]

            def pool(e):
                e.dma_start(X[:, :], x_dram).then_inc(back.sem, 16)
                with e.Fori(0, 4) as i:
                    chain["pool"].loop(i, 2)
                    for u in range(2):
                        split_tile(e, tile(n0, i, u), i * 2 + u, DK, P, ring, split)
                chain["pool"].end(4)

            def sp(e):
                for u in range(2):
                    load_tile(e, tile(n0, 0, u), src, u * P, DK, P, split, u)
                with e.Fori(1, 4) as i:
                    for u in range(2):
                        load_tile(e, tile(n0, i, u), src, i * 256 + u * P, DK, P, split, i * 2 + u)

            def act(e):
                for j in range(8):
                    e.activation(parts[j][0][:, 0:width], mix[j][:, 0:width], ACT.Copy).then_inc(high.sem, 1)

            def pe(e):
                e.wait_ge(low.sem, low.at(8))
                for u in range(2):
                    product(e, tile(n0, 0, u), u, DK, P, rhs, last, ring, split)
                with e.Fori(1, 4) as i:
                    for u in range(2):
                        product(e, tile(n0, i, u), i * 2 + u, DK, P, rhs, last, ring, split, (added, i * 2 + (u - 1)))

            def split_mix(e):
                for j in range(8):
                    e.wait_ge(high.sem, high.at(j + 1))
                    e.tensor_tensor(parts[j][1][:, 0:width], mix[j][:, 0:width], parts[j][0][:, 0:width], ALU.subtract)\
                        .then_inc(low.sem, 1)

            def dve(e):
                split_mix(e)
                e.wait_ge(back.sem, back.at(1))
                with e.Fori(0, 4) as i:
                    for u in range(2):
                        g, n, _ = tile(n0, i, u)
                        e.wait_ge(tile_done.sem, n + 1)
                        residual(e, i, u, i * 2 + u, g, 16, last).then_inc(added.sem, 1)
            ph.parts = dict(sp=sp, pe=pe, act=act, dve=dve, pool=pool)

        def phase_ffn_up(l, last):
            ph = Phase()
            ph.uses_w = True
            n0 = tiles[0]
            tiles[0] += 2 * FT
            ph.ends.append((tile_done.sem, tiles[0]))
            width = SEQ if last else T
            zeroed = ph.sig("pads_zeroed", 8)
            raw_ready = ph.sig("raw_ready", FT)
            conv_done = ph.sig("conv_done", FT)
            silu = ph.sig("silu_made", FT)
            act_made = ph.sig("hidden_made", FT)
            high = ph.sig("hidden_high_made", FT)
            low = ph.sig("hidden_low_made", FT)
            split = ph.sig("tile_split", 2 * FT)
            src = a["ffn_w_up"][l].rearrange("(k p) n -> p k n", p=P)
            cv = [region(X, 2 * RAW + s * T, T) for s in range(2)]
            sl = [region(X, 2 * RAW + (2 + s) * T, T) for s in range(2)]

            def pool(e):
                zero_pads(e, zeroed)
                with e.Fori(0, FT) as i:
                    chain["pool"].loop(i, 2)
                    for u in range(2):
                        split_tile(e, tile(n0, i, u), i * 2 + u, DK, P, x_ring, split)
                chain["pool"].end(FT)

            def sp(e):
                with e.Fori(0, FT) as i:
                    load_tile(e, tile(n0, i, 0), src, i * P, DK, P, split, i * 2)
                    load_tile(e, tile(n0, i, 1), src, i * P + D_FF, DK, P, split, i * 2 + 1)

            def pe(e):
                for u in range(2):
                    product(e, tile(n0, 0, u), u, DK, P, h_rhs, last, x_ring, split)
                with e.Fori(1, FT) as i:
                    product(e, tile(n0, i, 0), i * 2, DK, P, h_rhs, last, x_ring, split, (raw_ready, i))
                    product(e, tile(n0, i, 1), i * 2 + 1, DK, P, h_rhs, last, x_ring, split, (act_made, i))

            def act(e):
                e.wait_ge(zeroed.sem, zeroed.at(8))
                with e.Fori(0, FT // 2) as i:
                    for u in range(2):
                        j = i * 2 + u
                        g, n, _ = tile(n0, i, 2 * u, 4)
                        e.wait_ge(tile_done.sem, n + 1)
                        keep_raw(e, g, raws()[u], width, raw_ready)
                        e.wait_ge(conv_done.sem, conv_done.at(j + 1))
                        e.activation(sl[u][:, 0:width], cv[u][:, 0:width], ACT.Silu).then_inc(silu.sem, 1)
                        e.wait_ge(act_made.sem, act_made.at(j + 1))
                        e.activation(cb[:, bass.ds(j * (2 * T), width)], sl[u][:, 0:width], ACT.Copy).then_inc(high.sem, 1)

            def dve(e):
                e.wait_ge(zeroed.sem, zeroed.at(8))
                with e.Fori(0, FT // 2) as i:
                    chain["dve"].loop(i, 4)
                    for u in range(2):
                        j = i * 2 + u
                        e.wait_ge(raw_ready.sem, raw_ready.at(j + 1))
                        w = [S[:, bass.ds(j + (VCOL["ffn_conv_w"] + s * FT), 1)] for s in range(3)]
                        conv(e, raws()[u], w, S[:, bass.ds(j + VCOL["ffn_conv_b"], 1)], cv[u], width, conv_done)
                        e.wait_ge(silu.sem, silu.at(j + 1))
                        g, n, _ = tile(n0, i, 2 * u + 1, 4)
                        e.wait_ge(tile_done.sem, n + 1)
                        e.tensor_tensor(sl[u][:, 0:width], sl[u][:, 0:width], group(g, width), ALU.mult)\
                            .then_inc(act_made.sem, 1)
                        e.wait_ge(act_made.sem, act_made.at(j + 1))
                        e.wait_ge(high.sem, high.at(j + 1))
                        e.tensor_tensor(cb[:, bass.ds(j * (2 * T) + T, width)], sl[u][:, 0:width],
                                        cb[:, bass.ds(j * (2 * T), width)], ALU.subtract).then_inc(low.sem, 1)
                chain["dve"].end(FT // 2)
            ph.parts = dict(sp=sp, pe=pe, act=act, dve=dve, pool=pool)

        def phase_ffn_down(l, last):
            ph = Phase()
            ph.uses_w = True
            pieces = [(0, 8), (8, 8), (16, FT - 16)]
            loaded = [ph.sig("down_loaded_0", 12, 16), ph.sig("down_loaded_1", 12, 16)]
            split = ph.sig("down_split", 24)
            done = ph.sig("down_done", 8)
            back = ph.sig("x_back", 1, 16)
            added = ph.sig("x_added", 8)
            ring = [[x.rearrange("p (k n) -> p k n", k=FT) for x in halves(H, s * FT * P, FT * P)] for s in range(2)]
            src = a["ffn_w_down"][l].rearrange("(k p) n -> p k n", p=P)
            if last:
                turned = ph.sig("out_turned", 16)
                kept = ph.sig("out_kept", 16)
                stored = [ph.sig("out_stored_0", 4, 16), ph.sig("out_stored_1", 4, 16)]
            xo = [region(H, 2 * FT * P + s * SEQ, SEQ) for s in range(2)]
            xr = [region(H, 2 * FT * P + (2 + s) * SEQ, SEQ).rearrange("p (t f) -> p t f", f=P) for s in range(2)]

            def piece(i, u, c):
                b = 3 * u + c
                return b % 2, i * 6 + b, i * 3 + b // 2

            def pool(e):
                e.dma_start(X[:, :], x_dram).then_inc(back.sem, 16)

                def pair(i, again):
                    for u in range(2):
                        for c, (k0, kn) in enumerate(pieces):
                            g, n, loads = piece(i, u, c)
                            if again and c == 0:
                                copy_waits(e, (loaded[g].sem, loaded[g].at(loads + 1)),
                                           (done.sem, done.at(i * 2 + (u - 1))))
                            else:
                                copy_waits(e, (loaded[g].sem, loaded[g].at(loads + 1)))
                            hi, lo = (x[:, k0:k0 + kn, :] for x in ring[u])
                            chain["pool"].link(e, e.tensor_copy(hi, w3[:, g, 0:kn, :]))
                            e.tensor_tensor(lo, w3[:, g, 0:kn, :], hi, ALU.subtract).then_inc(split.sem, 1)

                pair(0, False)
                with e.Fori(1, 4) as i:
                    chain["pool"].loop_from(i, 6, 1)
                    pair(i, True)
                chain["pool"].end(3)

            def sp(e):
                def pair(i, again):
                    for u in range(2):
                        at = i * 256 + u * P
                        at = at if isinstance(at, int) else e.snap(at)
                        for c, (k0, kn) in enumerate(pieces):
                            g, n, _ = piece(i, u, c)
                            if again or 3 * u + c >= 2:
                                e.wait_ge(split.sem, split.at(n - 1))
                            e.dma_start(w3[:, g, 0:kn, :], src[:, k0:k0 + kn, bass.ds(at, P)]).then_inc(loaded[g].sem, 16)

                pair(0, False)
                with e.Fori(1, 4) as i:
                    pair(i, True)

            def one(e, i, u, free):
                e.wait_ge(split.sem, split.at(i * 6 + (3 * u + 3)))
                if free:
                    e.wait_ge(added.sem, added.at(i * 2 + (u - 1)))
                for b, (t0, tn) in enumerate(tok(last)):
                    for k in range(FT):
                        for q, (w_, r_) in enumerate(HALVES):
                            c = (2 * k + r_) * T + t0
                            ins = e.matmul(ps[:, u * GROUP + b * BANK:u * GROUP + b * BANK + tn], ring[u][w_][:, k, :],
                                           cb[:, c:c + tn], start=(k == 0 and q == 0), stop=(k == FT - 1 and q == 2))
                ins.then_inc(done.sem, 1)

            def turn(e, j, u):
                e.wait_ge(added.sem, added.at(j + 1))
                for half in range(2):
                    if not (isinstance(j, int) and j == 0):
                        e.wait_ge(kept.sem, kept.at(j * 2 + (half - 1)))
                    for q in range(4):
                        b = 4 * half + q
                        ins = e.transpose(ps[:, (6 + half) * BANK + q * P:(6 + half) * BANK + q * P + P],
                                          xo[u][:, b * P:b * P + P], ident)
                    ins.then_inc(turned.sem, 1)

            def pe(e):
                one(e, 0, 0, False)
                one(e, 0, 1, False)
                if last:
                    turn(e, 0, 0)
                with e.Fori(1, 4) as i:
                    one(e, i, 0, True)
                    if last:
                        turn(e, i * 2 - 1, 1)
                    one(e, i, 1, True)
                    if last:
                        turn(e, i * 2, 0)
                if last:
                    turn(e, 7, 1)

            def dve(e):
                e.wait_ge(back.sem, back.at(1))
                with e.Fori(0, 4) as i:
                    for u in range(2):
                        j = i * 2 + u
                        e.wait_ge(done.sem, done.at(j + 1))
                        residual(e, i, u, j, u, 40, last).then_inc(added.sem, 1)

            def dve_last(e):
                e.wait_ge(back.sem, back.at(1))
                for u in range(2):
                    e.wait_ge(done.sem, done.at(u + 1))
                    residual(e, 0, u, u, u, 40, True, xo[u]).then_inc(added.sem, 1)
                with e.Fori(1, 4) as i:
                    for u in range(2):
                        j = i * 2 + u
                        e.wait_ge(done.sem, done.at(j + 1))
                        e.wait_ge(turned.sem, turned.at(j * 2 - 2))
                        residual(e, i, u, j, u, 40, True, xo[u]).then_inc(added.sem, 1)

            def act(e):
                o_ = out[0].rearrange("(t p) f -> p t f", p=P)

                def one_out(i, u, again):
                    j = i * 2 + u
                    if again:
                        e.wait_ge(stored[u].sem, stored[u].at(i))
                    for half in range(2):
                        e.wait_ge(turned.sem, turned.at(j * 2 + half + 1))
                        e.activation(xr[u][:, 4 * half:4 * half + 4, :],
                                     ps[:, (6 + half) * BANK:(7 + half) * BANK].rearrange("p (t f) -> p t f", f=P),
                                     ACT.Copy).then_inc(kept.sem, 1)
                    e.wait_ge(kept.sem, kept.at(j * 2 + 2))
                    dst = o_[:, :, bass.ds(j * P, P)] if not isinstance(j, int) else o_[:, :, j * P:j * P + P]
                    e.dma_start(dst, xr[u]).then_inc(stored[u].sem, 16)

                one_out(0, 0, False)
                one_out(0, 1, False)
                with e.Fori(1, 4) as i:
                    one_out(i, 0, True)
                    one_out(i, 1, True)
                for u in range(2):
                    e.wait_ge(stored[u].sem, stored[u].at(4))
            ph.parts = dict(sp=sp, pe=pe, dve=dve_last if last else dve, pool=pool)
            if last:
                ph.parts["act"] = act

        phase_input()
        for l in range(DEPTH):
            last = l == DEPTH - 1
            phase_modulation(l)
            phase_norm_mix(l)
            phase_hyena_in(l)
            phase_hyena_filter(l, SEQ, 0)
            phase_hyena_conv(l, SEQ, 0)
            if not last:
                phase_hyena_filter(l, CTX, SEQ)
                phase_hyena_conv(l, CTX, SEQ)
            phase_mla_in(l)
            phase_mla_norm(l)
            phase_mla_heads(l, last)
            phase_gdn_in(l)
            phase_head_norm(l, "qk")
            phase_gates(l)
            phase_scan(l)
            if l == 0:
                phase_modulation_rest()
            phase_head_norm(l, "out")
            phase_out(l, last)
            phase_norm_ffn(l, last)
            phase_ffn_up(l, last)
            phase_ffn_down(l, last)
        block = ctx.enter_context(nc.Block())

        def run(eng, name):
            for k, ph in enumerate(every):
                if name in ph.parts:
                    ahead = name == "sp" and ph.uses_w and k and not every[k - 1].uses_w
                    settle(eng, k - 1 if ahead else k)
                    ph.parts[name](eng)

        @block.sync
        def _(e):
            run(e, "sp")

        @block.tensor
        def _(e):
            run(e, "pe")

        @block.scalar
        def _(e):
            run(e, "act")

        @block.vector
        def _(e):
            run(e, "dve")

        @block.gpsimd
        def _(e):
            run(e, "pool")


_INS = ["x", "c", "ctx", "c_ctx", "ada_w", "ada_b", "mix_norm_g", "w_in", "gdn_conv_w", "gdn_a_log",
        "gdn_dt_bias", "gdn_norm_g", "mla_q_norm_g", "mla_w_uq", "mla_kv_norm_g", "mla_w_ukv",
        "mla_q_head_g", "mla_k_head_g", "hy_conv_w", "hy_conv_b", "hy_w1", "hy_b1", "hy_w2", "hy_b2",
        "hy_w3", "hy_b3", "hy_d", "w_out", "ffn_norm_g", "ffn_w_up", "ffn_conv_w", "ffn_conv_b",
        "ffn_w_down"]


def kernel(**inputs):
    import concourse.bacc as _bacc
    from concourse.bass_utils import run_bass_kernel_spmd as _run

    nc = _bacc.Bacc("TRN2", target_bir_lowering=False, num_devices=1)
    arrays = {n: np.ascontiguousarray(inputs[n]) for n in _INS}
    arrays.update(tables())
    aps = {n: nc.dram_tensor("in_" + n, v.shape, mybir.dt.from_np(v.dtype), kind="ExternalInput").ap()
           for n, v in arrays.items()}
    out = nc.dram_tensor("out_0", (1, SEQ, D), F32, kind="ExternalOutput").ap()
    build(nc, aps, out)
    r = _run(nc, [{"in_" + n: v for n, v in arrays.items()}], core_ids=[0])
    return r.results[0]["out_0"]
```
